# Optimizing a Trainium2 kernel written in Bass

```python
import math
import jax
import jax.numpy as jnp
from jax import lax
import numpy as np

D_MODEL = 1024
BATCH = 1
SEQ = 512
DEPTH = 2

HEAD_DIM = 64
Q_BLOCK = 128
NORM_EPS = 1e-6
NEG_INF = -1e30
FORCE_SCORE = 1e4

DIFF_HEADS = D_MODEL // (2 * HEAD_DIM)
DIFF_QK_DIM = HEAD_DIM // 2
DIFF_V_DIM = HEAD_DIM

NSA_HEADS = D_MODEL // (2 * HEAD_DIM)
NSA_KV_GROUPS = 2
NSA_HEADS_PER_GROUP = NSA_HEADS // NSA_KV_GROUPS
NSA_CMP_BLOCK = 32
NSA_CMP_STRIDE = 16
NSA_SEL_BLOCK = 64
NSA_TOP_N = 16
NSA_WINDOW = 512
NSA_BRANCHES = 3

DIFF_QK_COLS = DIFF_HEADS * 2 * DIFF_QK_DIM
DIFF_V_COLS = DIFF_HEADS * DIFF_V_DIM
NSA_Q_COLS = NSA_HEADS * HEAD_DIM
NSA_KV_COLS = NSA_BRANCHES * 2 * NSA_KV_GROUPS * HEAD_DIM
NSA_GATE_COLS = NSA_BRANCHES * NSA_HEADS
IN_COLS = 2 * DIFF_QK_COLS + DIFF_V_COLS + NSA_Q_COLS + NSA_KV_COLS + NSA_GATE_COLS
ATTN_OUT = DIFF_V_COLS + NSA_Q_COLS

RWKV_HEAD = 64
RWKV_HEADS = D_MODEL // RWKV_HEAD
RWKV_DECAY_LORA = 64
RWKV_ICLR_LORA = 64
RWKV_GATE_LORA = 160
RWKV_LNX_EPS = 64e-5

N_GROUPS = 4
EXPERTS_PER_GROUP = 8
N_EXPERTS = N_GROUPS * EXPERTS_PER_GROUP
TOP_K_IN_GROUP = 2
D_EXPERT = 256
MOE_BLOCK = 128

kernel_name = 'hybrid_diff_nsa_rwkv7_hmoe'

def rms_norm(x, gain, eps=NORM_EPS):
    xf = x.astype(jnp.float32)
    y = xf * lax.rsqrt(jnp.mean(xf * xf, axis=-1, keepdims=True) + eps)
    return (y * gain.astype(jnp.float32)).astype(x.dtype)

def masked_softmax(scores, mask):
    return jax.nn.softmax(jnp.where(mask, scores.astype(jnp.float32), NEG_INF), axis=-1)

def diff_attention(q, k, v, q_gain, k_gain, lam_p, subln_gain, lambda_init):
    B, S, H, _, dq = q.shape
    q = rms_norm(q, q_gain)
    k = rms_norm(k, k_gain)
    lp = lam_p.astype(jnp.float32)
    lam = jnp.exp(jnp.sum(lp[0] * lp[1])) - jnp.exp(jnp.sum(lp[2] * lp[3])) + lambda_init
    scale = dq ** -0.5
    outs = []
    for blk in range(S // Q_BLOCK):
        q0, q1 = blk * Q_BLOCK, (blk + 1) * Q_BLOCK
        s = jnp.einsum('bqhmd,bkhmd->bhmqk', q[:, q0:q1], k[:, :q1]) * scale
        causal = jnp.arange(q0, q1)[:, None] >= jnp.arange(q1)[None, :]
        p = masked_softmax(s, causal)
        p_diff = p[:, :, 0] - lam * p[:, :, 1]
        outs.append(jnp.einsum('bhqk,bkhd->bqhd', p_diff.astype(v.dtype), v[:, :q1]))
    o = jnp.concatenate(outs, axis=1)
    o = rms_norm(o, subln_gain) * (1.0 - lambda_init)
    return o.reshape(B, S, H * v.shape[-1])

def nsa_attention(q, kv, gates, q_gain, k_gain, cmp_pe, cmp_w1, cmp_w2):
    B, S, H, dh = q.shape
    G, HPG = NSA_KV_GROUPS, NSA_HEADS_PER_GROUP
    scale = dh ** -0.5
    pos = jnp.arange(S)
    n_qb = S // Q_BLOCK
    q = rms_norm(q, q_gain).reshape(B, S, G, HPG, dh)

    n_cmp = (S - NSA_CMP_BLOCK) // NSA_CMP_STRIDE + 1
    c_start = jnp.arange(n_cmp) * NSA_CMP_STRIDE
    c_idx = c_start[:, None] + jnp.arange(NSA_CMP_BLOCK)[None, :]

    def compress(t, pe, w1, w2):
        blocks = t[:, c_idx] + pe[:, None, :]
        flat = jnp.swapaxes(blocks, 2, 3).reshape(B, n_cmp, G, NSA_CMP_BLOCK * dh)
        return jax.nn.gelu(flat @ w1) @ w2

    k_cmp = rms_norm(compress(kv[:, :, 0, 0], cmp_pe[0], cmp_w1[0], cmp_w2[0]), k_gain[0])
    v_cmp = compress(kv[:, :, 0, 1], cmp_pe[1], cmp_w1[1], cmp_w2[1])
    cmp_ok = ((c_start + NSA_CMP_BLOCK - 1)[None, :] <= pos[:, None])[None, :, None, None, :]
    s_cmp = jnp.einsum('bsghd,bcgd->bsghc', q, k_cmp) * scale
    p_cmp = masked_softmax(s_cmp, cmp_ok) * cmp_ok
    o_cmp = jnp.einsum('bsghc,bcgd->bsghd', p_cmp.astype(v_cmp.dtype), v_cmp)

    n_sel = S // NSA_SEL_BLOCK
    top_n = min(NSA_TOP_N, n_sel)
    s_start = jnp.arange(n_sel) * NSA_SEL_BLOCK
    cover = ((c_start[:, None] < s_start[None, :] + NSA_SEL_BLOCK)
             & (c_start[:, None] + NSA_CMP_BLOCK > s_start[None, :])).astype(jnp.float32)
    importance = jnp.einsum('bsghc,cj->bsgj', p_cmp, cover)
    blk = jnp.arange(n_sel)[None, :]
    cur = (pos // NSA_SEL_BLOCK)[:, None]
    forced = ((blk == cur) | (blk == 0))[None, :, None, :]
    future = (blk > cur)[None, :, None, :]
    importance = jnp.where(forced, FORCE_SCORE, jnp.where(future, NEG_INF, importance))
    _, sel_idx = lax.top_k(importance, top_n)

    def to_blocks(t):
        return t.reshape(B, n_sel, NSA_SEL_BLOCK, G, dh).transpose(0, 3, 1, 2, 4)

    k_blk = to_blocks(rms_norm(kv[:, :, 1, 0], k_gain[1]))
    v_blk = to_blocks(kv[:, :, 1, 1])
    b_ix = jnp.arange(B)[:, None, None, None]
    g_ix = jnp.arange(G)[None, None, :, None]
    in_blk = jnp.arange(NSA_SEL_BLOCK)

    def select_block(args):
        q_c, idx_c, pos_c = args
        k_g = k_blk[b_ix, g_ix, idx_c]
        v_g = v_blk[b_ix, g_ix, idx_c]
        s = jnp.einsum('bqghd,bqgnkd->bqghnk', q_c, k_g) * scale
        ok = (idx_c[..., None] * NSA_SEL_BLOCK + in_blk) <= pos_c[None, :, None, None, None]
        s = s.reshape(B, Q_BLOCK, G, HPG, top_n * NSA_SEL_BLOCK)
        ok = ok.reshape(B, Q_BLOCK, G, 1, top_n * NSA_SEL_BLOCK)
        p = masked_softmax(s, ok).reshape(B, Q_BLOCK, G, HPG, top_n, NSA_SEL_BLOCK)
        return jnp.einsum('bqghnk,bqgnkd->bqghd', p.astype(v_g.dtype), v_g)

    def chunk(t):
        return jnp.swapaxes(t.reshape(B, n_qb, Q_BLOCK, *t.shape[2:]), 0, 1)

    o_sel = lax.map(select_block, (chunk(q), chunk(sel_idx), pos.reshape(n_qb, Q_BLOCK)))
    o_sel = jnp.swapaxes(o_sel, 0, 1).reshape(B, S, G, HPG, dh)

    pad = ((0, 0), (NSA_WINDOW, 0), (0, 0), (0, 0))
    span = Q_BLOCK + NSA_WINDOW
    band = (jnp.arange(n_qb) * Q_BLOCK)[:, None] + jnp.arange(span)[None, :]
    k_band = jnp.pad(rms_norm(kv[:, :, 2, 0], k_gain[2]), pad)[:, band]
    v_band = jnp.pad(kv[:, :, 2, 1], pad)[:, band]
    q_b = q.reshape(B, n_qb, Q_BLOCK, G, HPG, dh)
    s_win = jnp.einsum('bnqghd,bnkgd->bnghqk', q_b, k_band) * scale
    k_pos = (band - NSA_WINDOW)[:, None, :]
    q_pos = pos.reshape(n_qb, Q_BLOCK)[:, :, None]
    win_ok = (k_pos >= 0) & (k_pos <= q_pos) & (k_pos > q_pos - NSA_WINDOW)
    p_win = masked_softmax(s_win, win_ok[None, :, None, None])
    o_win = jnp.einsum('bnghqk,bnkgd->bnqghd', p_win.astype(v_band.dtype), v_band)
    o_win = o_win.reshape(B, S, G, HPG, dh)

    g = gates.reshape(B, S, G, HPG, NSA_BRANCHES, 1)
    o = g[..., 0, :] * o_cmp + g[..., 1, :] * o_sel + g[..., 2, :] * o_win
    return o.reshape(B, S, H * dh)

def hybrid_attention_mixer(xn, layer, w_in, gate_bias, diff_q_gain, diff_k_gain, diff_lam,
                           diff_subln, nsa_q_gain, nsa_k_gain, cmp_pe, cmp_w1, cmp_w2, w_out):
    B, S, _ = xn.shape
    h = xn @ w_in
    offs = np.cumsum([0, DIFF_QK_COLS, DIFF_QK_COLS, DIFF_V_COLS, NSA_Q_COLS, NSA_KV_COLS, NSA_GATE_COLS])
    d_q, d_k, d_v, n_q, n_kv, n_g = (h[..., int(offs[j]):int(offs[j + 1])] for j in range(6))
    lambda_init = 0.8 - 0.6 * math.exp(-0.3 * layer)
    diff_out = diff_attention(
        d_q.reshape(B, S, DIFF_HEADS, 2, DIFF_QK_DIM),
        d_k.reshape(B, S, DIFF_HEADS, 2, DIFF_QK_DIM),
        d_v.reshape(B, S, DIFF_HEADS, DIFF_V_DIM),
        diff_q_gain, diff_k_gain, diff_lam, diff_subln, lambda_init)
    gates = jax.nn.sigmoid(n_g + gate_bias).reshape(B, S, NSA_HEADS, NSA_BRANCHES)
    nsa_out = nsa_attention(
        n_q.reshape(B, S, NSA_HEADS, HEAD_DIM),
        n_kv.reshape(B, S, NSA_BRANCHES, 2, NSA_KV_GROUPS, HEAD_DIM),
        gates, nsa_q_gain, nsa_k_gain, cmp_pe, cmp_w1, cmp_w2)
    return jnp.concatenate([diff_out, nsa_out], axis=-1) @ w_out

def rwkv7_time_mix(xn, mix, w_r, w_k, w_v, w0, w1, w2, a0, a1, a2, g1, g2, k_k, k_a, r_k,
                   ln_w, ln_b, w_o):
    B, S, D = xn.shape
    H, N = RWKV_HEADS, RWKV_HEAD
    f32 = jnp.float32
    dx = jnp.pad(xn, ((0, 0), (1, 0), (0, 0)))[:, :-1] - xn
    xr, xw, xk, xv, xa, xg = (xn + dx * mix[j] for j in range(6))
    r = xr @ w_r
    k = xk @ w_k
    v = xv @ w_v
    w = -jax.nn.softplus(-(w0 + jnp.tanh(xw @ w1) @ w2).astype(f32)) - 0.5
    a = jax.nn.sigmoid((a0 + (xa @ a1) @ a2).astype(f32))
    g = jax.nn.sigmoid(xg @ g1) @ g2

    def heads(t):
        return t.astype(f32).reshape(B, S, H, N)

    kk = heads(k * k_k)
    kk = kk / jnp.maximum(jnp.linalg.norm(kk, axis=-1, keepdims=True), 1e-12)
    k = k.astype(f32) * (1.0 + (a - 1.0) * k_a.astype(f32))
    r_h, k_h, v_h, a_h = heads(r), heads(k), heads(v), heads(a)
    decay = jnp.exp(-jnp.exp(heads(w)))

    def step(state, inp):
        r_t, d_t, k_t, v_t, kk_t, a_t = inp
        s_kk = jnp.einsum('bhvk,bhk->bhv', state, -kk_t)
        state = (state * d_t[:, :, None, :]
                 + s_kk[..., None] * (kk_t * a_t)[:, :, None, :]
                 + v_t[..., None] * k_t[:, :, None, :])
        return state, jnp.einsum('bhvk,bhk->bhv', state, r_t)

    def tm(t):
        return jnp.moveaxis(t, 1, 0)

    _, y = lax.scan(step, jnp.zeros((B, H, N, N), f32),
                    (tm(r_h), tm(decay), tm(k_h), tm(v_h), tm(kk), tm(a_h)))
    y = jnp.moveaxis(y, 0, 1)
    mu = jnp.mean(y, axis=-1, keepdims=True)
    var = jnp.mean(jnp.square(y - mu), axis=-1, keepdims=True)
    y = ((y - mu) * lax.rsqrt(var + RWKV_LNX_EPS)).reshape(B, S, D) * ln_w + ln_b
    bonus = jnp.sum(r_h * k_h * r_k.astype(f32).reshape(H, N), axis=-1, keepdims=True) * v_h
    y = y + bonus.reshape(B, S, D)
    return (y * g.astype(f32)).astype(xn.dtype) @ w_o

def hier_moe(xn, wg, bg, we, be, e_gate, e_up, e_down):
    B, S, D = xn.shape
    f32 = jnp.float32
    xf = xn.reshape(-1, D)
    n_tok = xf.shape[0]
    grp_prob = jax.nn.softmax((xf @ wg + bg).astype(f32), axis=-1)
    grp_p, grp_idx = lax.top_k(grp_prob, 1)
    exp_logits = (xf @ we + be).astype(f32).reshape(n_tok, N_GROUPS, EXPERTS_PER_GROUP)
    in_grp = jnp.take_along_axis(exp_logits, grp_idx[:, :, None], axis=1)[:, 0]
    top_val, top_idx = lax.top_k(in_grp, TOP_K_IN_GROUP)
    gate = grp_p * jax.nn.softmax(top_val, axis=-1)
    expert = grp_idx * EXPERTS_PER_GROUP + top_idx

    n_pairs = n_tok * TOP_K_IN_GROUP
    flat_e = expert.reshape(-1)
    order = jnp.argsort(flat_e)
    e_sorted = flat_e[order]
    tok_sorted = order // TOP_K_IN_GROUP
    gate_sorted = gate.reshape(-1)[order]
    counts = jnp.bincount(flat_e, length=N_EXPERTS)
    padded = (counts + MOE_BLOCK - 1) // MOE_BLOCK * MOE_BLOCK
    pad_end = jnp.cumsum(padded)
    pad_start = pad_end - padded
    start = jnp.cumsum(counts) - counts
    dest = pad_start[e_sorted] + jnp.arange(n_pairs) - start[e_sorted]
    n_blocks = -(-n_pairs // MOE_BLOCK) + N_EXPERTS
    slot_tok = jnp.full((n_blocks * MOE_BLOCK,), n_tok, jnp.int32).at[dest].set(tok_sorted)
    block_e = jnp.minimum(jnp.searchsorted(pad_end, jnp.arange(n_blocks) * MOE_BLOCK, side='right'),
                          N_EXPERTS - 1)
    x_pad = jnp.concatenate([xf, jnp.zeros((1, D), xf.dtype)], axis=0)
    xb = x_pad[slot_tok].reshape(n_blocks, MOE_BLOCK, D)

    def run_block(args):
        x_blk, e = args
        hid = jax.nn.silu(x_blk @ e_gate[e]) * (x_blk @ e_up[e])
        return hid @ e_down[e]

    y_slots = lax.map(run_block, (xb, block_e)).reshape(n_blocks * MOE_BLOCK, D)
    y = jnp.zeros_like(xf).at[tok_sorted].add(y_slots[dest] * gate_sorted[:, None].astype(xf.dtype))
    return y.reshape(B, S, D)

def setup_inputs(seed: int = 0) -> dict:
    key = jax.random.key(seed)
    keys = jax.random.split(key, 48)
    ks = iter([keys[j] for j in range(48)])
    n_a = (DEPTH + 1) // 2
    n_r = DEPTH // 2
    D = D_MODEL
    L = NSA_CMP_BLOCK

    def nrm(shape, scale):
        return jax.random.normal(next(ks), shape, jnp.float32) * scale

    def gain(shape):
        return 1.0 + nrm(shape, 0.05)

    def unif(shape, lo, hi):
        return jax.random.uniform(next(ks), shape, jnp.float32, lo, hi)

    return {
        'x': nrm((BATCH, SEQ, D), 1.0),
        'mix_norm': gain((DEPTH, D)),
        'attn_w_in': nrm((n_a, D, IN_COLS), D ** -0.5),
        'attn_gate_bias': nrm((n_a, NSA_GATE_COLS), 0.1),
        'diff_q_norm': gain((n_a, DIFF_QK_DIM)),
        'diff_k_norm': gain((n_a, DIFF_QK_DIM)),
        'diff_lambda': nrm((n_a, 4, DIFF_QK_DIM), 0.1),
        'diff_subln': gain((n_a, DIFF_V_DIM)),
        'nsa_q_norm': gain((n_a, HEAD_DIM)),
        'nsa_k_norm': gain((n_a, NSA_BRANCHES, HEAD_DIM)),
        'nsa_cmp_pe': nrm((n_a, 2, L, HEAD_DIM), 0.1),
        'nsa_cmp_w1': nrm((n_a, 2, L * HEAD_DIM, HEAD_DIM), (L * HEAD_DIM) ** -0.5),
        'nsa_cmp_w2': nrm((n_a, 2, HEAD_DIM, HEAD_DIM), HEAD_DIM ** -0.5),
        'attn_w_out': nrm((n_a, ATTN_OUT, D), ATTN_OUT ** -0.5),
        'rwkv_mix': unif((n_r, 6, D), 0.0, 1.0),
        'rwkv_w_r': nrm((n_r, D, D), D ** -0.5),
        'rwkv_w_k': nrm((n_r, D, D), D ** -0.5),
        'rwkv_w_v': nrm((n_r, D, D), D ** -0.5),
        'rwkv_decay_w0': unif((n_r, D), -5.0, 0.0),
        'rwkv_decay_w1': nrm((n_r, D, RWKV_DECAY_LORA), D ** -0.5),
        'rwkv_decay_w2': nrm((n_r, RWKV_DECAY_LORA, D), 0.1 * RWKV_DECAY_LORA ** -0.5),
        'rwkv_iclr_a0': nrm((n_r, D), 0.1),
        'rwkv_iclr_a1': nrm((n_r, D, RWKV_ICLR_LORA), D ** -0.5),
        'rwkv_iclr_a2': nrm((n_r, RWKV_ICLR_LORA, D), 0.1 * RWKV_ICLR_LORA ** -0.5),
        'rwkv_gate_g1': nrm((n_r, D, RWKV_GATE_LORA), D ** -0.5),
        'rwkv_gate_g2': nrm((n_r, RWKV_GATE_LORA, D), RWKV_GATE_LORA ** -0.5),
        'rwkv_k_k': 0.85 + nrm((n_r, D), 0.05),
        'rwkv_k_a': gain((n_r, D)),
        'rwkv_r_k': nrm((n_r, D), 0.1),
        'rwkv_ln_w': gain((n_r, D)),
        'rwkv_ln_b': nrm((n_r, D), 0.01),
        'rwkv_w_o': nrm((n_r, D, D), D ** -0.5),
        'ffn_norm': gain((DEPTH, D)),
        'router_group_w': nrm((DEPTH, D, N_GROUPS), D ** -0.5),
        'router_group_b': nrm((DEPTH, N_GROUPS), 0.01),
        'router_expert_w': nrm((DEPTH, D, N_EXPERTS), D ** -0.5),
        'router_expert_b': nrm((DEPTH, N_EXPERTS), 0.01),
        'expert_w_gate': nrm((DEPTH, N_EXPERTS, D, D_EXPERT), D ** -0.5),
        'expert_w_up': nrm((DEPTH, N_EXPERTS, D, D_EXPERT), D ** -0.5),
        'expert_w_down': nrm((DEPTH, N_EXPERTS, D_EXPERT, D), D_EXPERT ** -0.5),
    }

def reference(x, mix_norm, attn_w_in, attn_gate_bias, diff_q_norm, diff_k_norm, diff_lambda,
              diff_subln, nsa_q_norm, nsa_k_norm, nsa_cmp_pe, nsa_cmp_w1, nsa_cmp_w2, attn_w_out,
              rwkv_mix, rwkv_w_r, rwkv_w_k, rwkv_w_v, rwkv_decay_w0, rwkv_decay_w1, rwkv_decay_w2,
              rwkv_iclr_a0, rwkv_iclr_a1, rwkv_iclr_a2, rwkv_gate_g1, rwkv_gate_g2, rwkv_k_k,
              rwkv_k_a, rwkv_r_k, rwkv_ln_w, rwkv_ln_b, rwkv_w_o, ffn_norm, router_group_w,
              router_group_b, router_expert_w, router_expert_b, expert_w_gate, expert_w_up,
              expert_w_down):
    for layer in range(DEPTH):
        i = layer // 2
        xn = rms_norm(x, mix_norm[layer])
        if layer % 2 == 0:
            x = x + hybrid_attention_mixer(
                xn, layer, attn_w_in[i], attn_gate_bias[i], diff_q_norm[i], diff_k_norm[i],
                diff_lambda[i], diff_subln[i], nsa_q_norm[i], nsa_k_norm[i], nsa_cmp_pe[i],
                nsa_cmp_w1[i], nsa_cmp_w2[i], attn_w_out[i])
        else:
            x = x + rwkv7_time_mix(
                xn, rwkv_mix[i], rwkv_w_r[i], rwkv_w_k[i], rwkv_w_v[i], rwkv_decay_w0[i],
                rwkv_decay_w1[i], rwkv_decay_w2[i], rwkv_iclr_a0[i], rwkv_iclr_a1[i],
                rwkv_iclr_a2[i], rwkv_gate_g1[i], rwkv_gate_g2[i], rwkv_k_k[i], rwkv_k_a[i],
                rwkv_r_k[i], rwkv_ln_w[i], rwkv_ln_b[i], rwkv_w_o[i])
        x = x + hier_moe(
            rms_norm(x, ffn_norm[layer]), router_group_w[layer], router_group_b[layer],
            router_expert_w[layer], router_expert_b[layer], expert_w_gate[layer],
            expert_w_up[layer], expert_w_down[layer])
    return x


_drawn_inputs = setup_inputs


def setup_inputs(seed=0):
    import zlib

    import numpy as np

    out = dict(_drawn_inputs(seed))
    spreads = {}
    factors = {'nsa_q_norm': 3.265,
     'nsa_k_norm': 2.851,
     'rwkv_decay_w1': 5.645,
     'rwkv_decay_w2': 6.04,
     'rwkv_ln_b': 5.105,
     'router_group_b': 2.786,
     'router_expert_b': 3.486}
    for name, (base, spread) in spreads.items():
        noise = np.random.default_rng([zlib.crc32(name.encode()), seed]).standard_normal(out[name].shape)
        drawn = base * np.exp(spread * noise) if base else spread * noise
        out[name] = jnp.asarray(drawn.astype(out[name].dtype))
    for name, factor in factors.items():
        out[name] = (out[name] * factor).astype(out[name].dtype)
    return out
```

```python
import numpy as np
from contextlib import ExitStack, contextmanager

import concourse.bass as bass
from concourse import mybir

FP32 = mybir.dt.float32
BF16 = mybir.dt.bfloat16
I32 = mybir.dt.int32
U32 = mybir.dt.uint32
ALU = mybir.AluOpType
ACT = mybir.ActivationFunctionType
AX = mybir.AxisListType

P = 128
S = 512
D = 1024
TT = S // P
KT = D // P
EPS = 1e-6
BIG = 1e30

DQ0, DK0, DV0, NQ0, KV0, GT0, IN_COLS = 0, 512, 1024, 1536, 2048, 2816, 2840
IN_CHUNK = IN_COLS // 8
NCMP = 31
LAMBDA_INIT = 0.8 - 0.6

NE, NG, EPG, DE = 32, 4, 8, 256
CAP = 96
ROUNDS = -(-S // CAP)
LORA_G = 160
HEADS = 16
CH = 64
DECAY = float(np.exp(-0.5))

V_MIX0, V_MIX1, V_MU, V_W0, V_A0, V_KK, V_KA, V_RK, V_LNW, V_LNB = 0, 8, 16, 64, 72, 80, 88, 96, 104, 112
V_DQ, V_DK, V_NQ, V_NK0, V_NK1, V_NK2, V_SUB, V_ROWS = 120, 121, 122, 123, 124, 125, 126, 127


class Link:

    def __init__(self, eng, sem, base=0):
        self.eng, self.sem, self.base, self.n = eng, sem, base, 0

    def __call__(self, ins):
        self.n += 1
        ins.then_inc(self.sem, 1)
        self.eng.wait_ge(self.sem, self.base + self.n)


class Held:

    def __init__(self, eng, sem):
        self.eng, self.sem = eng, sem

    def __call__(self):
        self.eng.sem_inc(self.sem, 1)


class Shared:
    pass


def const_table():
    p, t = np.arange(P)[:, None], np.arange(P)[None, :]
    parts = {"ident": (p == t), "neg": np.where(t > p, -BIG, 0.0)}
    c = np.arange(NCMP)[None, None, :]
    pos = (np.arange(TT)[None, :, None] * P + np.arange(P)[:, None, None])
    ok = (16 * c + 31 <= pos)
    parts["cneg"] = np.where(ok, 0.0, -BIG).reshape(P, -1)
    parts["cok"] = ok.reshape(P, -1)
    parts["upper"] = (p < t)
    parts["ones"] = np.ones((P, P))
    parts["iota4"] = np.broadcast_to(np.arange(NG), (P, NG))
    parts["iota32"] = np.broadcast_to(np.arange(NE), (P, NE))
    parts["pair"] = (np.arange(2)[None, :, None] * S + np.arange(TT)[None, None, :] * P
                     + np.arange(P)[:, None, None]).reshape(P, -1)
    parts["scan"] = np.broadcast_to((np.arange(S) % CH != 0), (P, S))
    s, u = (np.arange(P) % CH)[:, None], np.arange(CH)[None, :]
    for n in (1, 2, 4, 8, 16, 32):
        parts[f"lev{n}"] = (s // (2 * n) == u // (2 * n)) & (u % (2 * n) >= n) & (s % (2 * n) < n)
    parts["lev1t"] = (s // 2 == u // 2) & (s % 2 == 1) & (u % 2 == 0)
    parts["eye64"] = (s == u)
    parts["strict"] = (s < u)
    parts["incl"] = (s <= u)
    parts["blk"] = (p // CH == t // CH)
    parts["blkmean"] = (p // CH == t // CH) / CH
    k, h = np.arange(KT)[None, :, None], np.arange(HEADS)[None, None, :]
    parts["sel"] = (2 * k + np.arange(P)[:, None, None] // CH == h).reshape(P, -1)
    f = np.arange(P)[None, None, :]
    selt = (2 * np.arange(KT)[None, :, None] + f // CH == np.arange(P)[:, None, None])
    parts["selt"] = selt.reshape(P, -1)
    where, at = {}, 0
    for name, a in parts.items():
        where[name] = (at, at + a.shape[1])
        at += a.shape[1]
    return np.concatenate([np.asarray(a, np.float32) for a in parts.values()], axis=1), where


def setup(nc, g, ins):
    f = g.view
    with nc.sbuf_tensor("rows", [P, P], FP32) as rows, nc.Block() as block:
        singles = []
        for at, name, index in ((V_MIX0, "mix_norm", 0), (V_MIX1, "mix_norm", 1)):
            singles.append((rows[at:at + 8, :], ins[name][index].rearrange("(k p) -> k p", p=P)))
        singles.append((rows[V_MU:V_MU + 48, :], ins["rwkv_mix"][0].rearrange("j (k p) -> (j k) p", p=P)))
        for at, name in ((V_W0, "rwkv_decay_w0"), (V_A0, "rwkv_iclr_a0"), (V_KK, "rwkv_k_k"), (V_KA, "rwkv_k_a"),
                         (V_RK, "rwkv_r_k"), (V_LNW, "rwkv_ln_w"), (V_LNB, "rwkv_ln_b")):
            singles.append((rows[at:at + 8, :], ins[name][0].rearrange("(k p) -> k p", p=P)))
        for at, src, n in ((V_DQ, ins["diff_q_norm"], 32), (V_DK, ins["diff_k_norm"], 32),
                           (V_NQ, ins["nsa_q_norm"], 64), (V_NK0, ins["nsa_k_norm"][:, 0], 64),
                           (V_NK1, ins["nsa_k_norm"][:, 1], 64), (V_NK2, ins["nsa_k_norm"][:, 2], 64),
                           (V_SUB, ins["diff_subln"], 64)):
            for r in range(P // n):
                singles.append((rows[at:at + 1, r * n:(r + 1) * n], src))

        @block.sync
        def _(sp):
            sp.dma_start(g.const[:], ins["const"]).then_inc(g.sig["const_in"], 16)
            for dst, src in singles[::2]:
                sp.dma_start(dst, src).then_inc(g.sig["vec_in"], 16)

        @block.scalar
        def _(act):
            act.dma_start(g.x[:], ins["x"][0].rearrange("(t p) d -> p t d", p=P)).then_inc(g.x_in, 16)
            for dst, src in singles[1::2]:
                act.dma_start(dst, src).then_inc(g.sig["vec_in"], 16)
            act.wait_ge(g.sig["vec_t"], 1)
            nc.scalar.activation(g.vec[:], g.ps[:, 0, 0:V_ROWS], ACT.Copy).then_inc(g.sig["vec_ready"], 1)

        @block.vector
        def _(dve):
            dve.wait_ge(g.sig["const_in"], 16)
            nc.vector.tensor_copy(g.identb[:], f("ident")).then_inc(g.sig["const_b"], 1)
            nc.vector.tensor_copy(g.negb[:], f("neg")).then_inc(g.sig["const_b"], 1)
            nc.vector.tensor_copy(g.cnegb[:], f("cneg")).then_inc(g.sig["const_b"], 1)

        @block.tensor
        def _(pe):
            pe.wait_ge(g.sig["const_in"], 16)
            pe.wait_ge(g.sig["vec_in"], 16 * len(singles))
            nc.tensor.transpose(g.ps[:, 0, 0:V_ROWS], rows[0:V_ROWS, :], f("ident")[0:V_ROWS, 0:V_ROWS]).then_inc(g.sig["vec_t"], 1)


def normalise(nc, g, xs, x_t, gains, strided, store=()):
    n = g.norms
    g.norms += 1
    with nc.sbuf_tensor(f"nsq{n}", [P, 2, D], FP32) as sq, nc.sbuf_tensor(f"nst{n}", [P, 3, TT], FP32) as st, \
            nc.Block() as block:

        @block.scalar
        def _(act):
            if n == 0:
                act.wait_ge(g.x_in, 16)
            for t in range(TT):
                if t >= 2:
                    act.wait_ge(g.n_sum, TT * n + t - 1)
                nc.scalar.activation(sq[:, t % 2, :], g.x[:, t, :], ACT.Square,
                                     accum_out=st[:, 0, t:t + 1]).then_inc(g.n_sum, 1)
            act.wait_ge(g.n_ms, n + 1)
            nc.scalar.activation(st[:, 2, :], st[:, 1, :], ACT.Sqrt).then_inc(g.n_rms, 1)
            for k in range(0, KT, 2):
                act.wait_ge(g.n_tr, KT * n + k + 1)
                nc.scalar.activation(x_t[:, k, :], g.ps[:, k, :], ACT.Copy,
                                     scale=gains[:, k:k + 1]).then_inc(g.n_ev, 1)

        @block.vector
        def _(dve):
            dve.wait_ge(g.n_sum, TT * (n + 1))
            nc.vector.tensor_scalar(st[:, 1, :], st[:, 0, :], 1.0 / D, EPS, ALU.mult, ALU.add).then_inc(g.n_ms, 1)
            dve.wait_ge(g.n_rms, n + 1)
            nc.vector.reciprocal(st[:, 0, :], st[:, 2, :]).then_inc(g.n_rs, 1)
            dve.wait_ge(g.n_rs, n + 1)
            for t in range(TT):
                nc.vector.tensor_scalar(xs[:, t, :], g.x[:, t, :], st[:, 0, t:t + 1], None, ALU.mult).then_inc(g.n_xs, 1)
            for k in range(1, KT, 2):
                dve.wait_ge(g.n_tr, KT * n + k + 1)
                nc.vector.tensor_scalar(x_t[:, k, :], g.ps[:, k, :], gains[:, k:k + 1], None, ALU.mult).then_inc(g.n_ev, 1)

        @block.tensor
        def _(pe):
            for t in range(TT):
                pe.wait_ge(g.n_xs, TT * n + t + 1)
                for k in range(KT):
                    src = xs[:, t, k:D:KT] if strided else xs[:, t, k * P:(k + 1) * P]
                    last = nc.tensor.transpose(g.ps[:, k, t * P:(t + 1) * P], src, g.view("ident"))
                    if t == TT - 1:
                        last.then_inc(g.n_tr, 1)

        @block.sync
        def _(sp):
            sp.wait_ge(g.n_ev, KT * (n + 1))
            if store:
                sp.wait_ge(g.n_xs, TT * (n + 1))
                for dst in store:
                    sp.dma_start(dst.rearrange("(t p) d -> p t d", p=P), xs[:]).then_inc(g.sig["xs_out"], 16)


def project_in(nc, g, w, x_t, h):
    w_v = w.rearrange("(k p) (c n) -> c p k n", p=P, n=IN_CHUNK)
    with nc.sbuf_tensor("w_in", [P, 2, KT, IN_CHUNK], FP32) as wt, nc.Block() as block:

        @block.sync
        def _(sp):
            for b in range(2):
                sp.dma_start(wt[:, b], w_v[b]).then_inc(g.sig["win_in"][b], 16)
            with sp.Fori(1, 4) as i:
                for b in range(2):
                    sp.wait_ge(g.sig["win_done"][b], 4 * i)
                    sp.dma_start(wt[:, b], w_v[2 * i + b]).then_inc(g.sig["win_in"][b], 16)

        @block.tensor
        def _(pe):
            with pe.Fori(0, 4) as i:
                for b in range(2):
                    pe.wait_ge(g.sig["win_in"][b], 16 * i + 16)
                    for t in range(TT):
                        pe.wait_ge(g.sig["win_free"][b], i * 4 + t + 1)
                        for k in range(KT):
                            last = nc.tensor.matmul(g.ps[:, 4 * b + t, 0:IN_CHUNK], x_t[:, k, t * P:(t + 1) * P],
                                                    wt[:, b, k, :], start=(k == 0), stop=(k == KT - 1))
                        last.then_inc(g.sig["win_done"][b], 1)

        def copies(eng, run, b):
            with eng.Fori(0, 4) as i:
                for t in range(TT):
                    eng.wait_ge(g.sig["win_done"][b], i * 4 + t + 1)
                    run(h[:, t, bass.ds((2 * i + b) * IN_CHUNK, IN_CHUNK)], g.ps[:, 4 * b + t, 0:IN_CHUNK]).then_inc(g.sig["win_free"][b], 1)

        @block.scalar
        def _(act):
            for _ in range(4):
                nc.scalar.nop().then_inc(g.sig["win_free"][0], 1)
            copies(act, lambda o, i: nc.scalar.activation(o, i, ACT.Copy), 0)

        @block.vector
        def _(dve):
            for _ in range(4):
                nc.vector.nop().then_inc(g.sig["win_free"][1], 1)
            copies(dve, nc.vector.tensor_copy, 1)


def head_norms(nc, g, h, ins, kt_sel, kt_win, kc_t, vc, rs, gates, lamv, qg):
    f = g.view
    with ExitStack() as mem:
        def sb(name, shape, dt=FP32):
            return mem.enter_context(nc.sbuf_tensor(name, shape, dt))

        sq = sb("hn_sq", [P, 2, 2304])
        ss = sb("hn_ss", [P, TT, 52])
        rms = sb("hn_rms", [P, TT, 52])
        kst = sb("hn_k", [P, 2, TT, P])
        gb = sb("hn_gb", [P, 24])
        gz = sb("hn_gz", [P, TT, 24])
        lp = sb("hn_lp", [P, 4, 32])
        lq = sb("hn_lq", [P, 2, 32])
        ls = sb("hn_ls", [P, 4])
        pe_rows = sb("hn_per", [64, P])
        pe_t = sb("hn_pet", [P, 2, 32])
        w1 = sb("hn_w1", [P, 2, 32, 64])
        w2 = sb("hn_w2", [P, 2, 64])
        blk = sb("hn_blk", [P, 2, 2, 32, 16])
        hid = sb("hn_hid", [P, 2, NCMP])
        hu = sb("hn_hu", [P, 2, NCMP])
        kc = sb("hn_kc", [NCMP, 2, 64])
        kq = sb("hn_kq", [NCMP, 2, 64])
        kr = sb("hn_kr", [NCMP, 3, 2])
        pe_src = ins["nsa_cmp_pe"][0].rearrange("v l d -> (v l) d")
        w1_src = ins["nsa_cmp_w1"][0].rearrange("v (l d) o -> v d l o", d=64)
        w2_src = ins["nsa_cmp_w2"][0].rearrange("v d o -> d v o")
        block = mem.enter_context(nc.Block())

        @block.sync
        def _(sp):
            sp.dma_start(gb[:], ins["attn_gate_bias"][0].partition_broadcast(P)).then_inc(g.sig["hn_small"], 16)
            sp.dma_start(lp[:], ins["diff_lambda"][0].partition_broadcast(P)).then_inc(g.sig["hn_small"], 16)
            for grp in range(2):
                sp.dma_start(pe_rows[:, 64 * grp:64 * grp + 64], pe_src).then_inc(g.sig["hn_pe"], 16)
                sp.dma_start(w2[64 * grp:64 * grp + 64], w2_src).then_inc(g.sig["hn_w"], 16)
                for v in range(2):
                    sp.dma_start(w1[64 * grp:64 * grp + 64, v], w1_src[v]).then_inc(g.sig["hn_w"], 16)

        @block.scalar
        def _(act):
            for t in range(TT):
                if t >= 2:
                    act.wait_ge(g.sig["hn_sum"], 2 * t - 2)
                nc.scalar.activation(sq[:, t % 2, 0:1024], h[:, t, 0:1024], ACT.Square).then_inc(g.sig["hn_sq"], 1)
                nc.scalar.activation(sq[:, t % 2, 1024:2304], h[:, t, NQ0:GT0], ACT.Square).then_inc(g.sig["hn_sq"], 1)
            act.wait_ge(g.sig["hn_ms"], 2)
            nc.scalar.activation(rms[:], ss[:], ACT.Sqrt).then_inc(g.sig["hn_rms"], 1)
            act.wait_ge(g.sig["hn_gz"], 3)
            nc.scalar.activation(gates[:], gz[:], ACT.Exp, scale=-1.0).then_inc(g.sig["hn_exp"], 1)
            nc.scalar.activation(ls[:, 2:4], ls[:, 0:2], ACT.Exp).then_inc(g.sig["hn_exp"], 1)
            act.wait_ge(g.sig["hn_kt"], 2)
            nc.scalar.activation(kt_sel[:], g.ps[:, 0, :], ACT.Copy, scale=g.vec[:, V_NK1:V_NK1 + 1]).then_inc(g.sig["hn_kev"], 1)
            nc.scalar.activation(kt_win[:], g.ps[:, 1, :], ACT.Copy, scale=g.vec[:, V_NK2:V_NK2 + 1]).then_inc(g.sig["hn_kev"], 1)
            for grp in range(2):
                act.wait_ge(g.sig["hn_hid"], grp + 1)
                q = slice(64 * grp, 64 * grp + 64)
                nc.scalar.activation(hid[q], g.ps[q, 5 + grp, 0:2 * NCMP].rearrange("p (v c) -> p v c", v=2),
                                     ACT.Copy).then_inc(g.sig["hn_hs"], 1)
            act.wait_ge(g.sig["hn_gu"], 1)
            nc.scalar.activation(hu[:], hu[:], ACT.Tanh, scale=0.7978845608028654).then_inc(g.sig["hn_th"], 1)
            for grp in range(2):
                act.wait_ge(g.sig["hn_cmp"], grp + 1)
                o = g.ps[0:NCMP, 7 - 3 * grp, 0:128].rearrange("p (v d) -> p v d", v=2)
                nc.scalar.activation(kc[:, grp, :], o[:, 0, :], ACT.Copy).then_inc(g.sig["hn_kc"], 1)
                nc.scalar.activation(vc[:, grp, :], o[:, 1, :], ACT.Copy).then_inc(g.sig["hn_kc"], 1)
            act.wait_ge(g.sig["hn_kms"], 1)
            nc.scalar.activation(kr[:, 1], kr[:, 0], ACT.Sqrt).then_inc(g.sig["hn_krm"], 1)
            act.wait_ge(g.sig["hn_kct"], 1)
            nc.scalar.activation(kc_t[:], g.ps[:, 5, 0:NCMP], ACT.Copy, scale=g.vec[:, V_NK0:V_NK0 + 1]).then_inc(g.sig["hn_kct2"], 1)

        @block.vector
        def _(dve):
            link = Link(dve, g.sig["hn_link"])
            for t in range(TT):
                dve.wait_ge(g.sig["hn_sq"], 2 * t + 2)
                nc.vector.tensor_reduce(ss[:, t, 0:32], sq[:, t % 2, 0:1024].rearrange("p (s d) -> p s d", d=32),
                                        AX.X, ALU.add).then_inc(g.sig["hn_sum"], 1)
                nc.vector.tensor_reduce(ss[:, t, 32:52], sq[:, t % 2, 1024:2304].rearrange("p (s d) -> p s d", d=64),
                                        AX.X, ALU.add).then_inc(g.sig["hn_sum"], 1)
            dve.wait_ge(g.sig["hn_sum"], 2 * TT)
            nc.vector.tensor_scalar(ss[:, :, 0:32], ss[:, :, 0:32], 1.0 / 32, EPS, ALU.mult, ALU.add).then_inc(g.sig["hn_ms"], 1)
            nc.vector.tensor_scalar(ss[:, :, 32:52], ss[:, :, 32:52], 1.0 / 64, EPS, ALU.mult, ALU.add).then_inc(g.sig["hn_ms"], 1)
            dve.wait_ge(g.sig["hn_small"], 32)
            nc.vector.tensor_tensor(gz[:], h[:, :, GT0:IN_COLS], gb[:].unsqueeze(1).to_broadcast([P, TT, 24]),
                                    ALU.add).then_inc(g.sig["hn_gz"], 1)
            link(nc.vector.tensor_tensor(lq[:], lp[:, 0:4:2], lp[:, 1:4:2], ALU.mult))
            nc.vector.tensor_reduce(ls[:, 0:2], lq[:], AX.X, ALU.add).then_inc(g.sig["hn_gz"], 1)
            nc.vector.tensor_scalar(qg[:, 0:1], g.vec[:, V_DQ:V_DQ + 1], 32.0 ** -0.5, None, ALU.mult).then_inc(g.sig["hn_gz"], 1)
            link(nc.vector.tensor_scalar(qg[:, 1:2], g.vec[:, V_NQ:V_NQ + 1], 64.0 ** -0.5, None, ALU.mult))
            dve.wait_ge(g.sig["hn_rms"], 1)
            link(nc.vector.reciprocal(rs[:], rms[:]))
            for b in range(2):
                c0 = KV0 + 256 * (b + 1)
                s0 = 32 + (c0 - NQ0) // 64
                for t in range(TT):
                    r = rs[:, t, s0:s0 + 2].unsqueeze(2).to_broadcast([P, 2, 64])
                    nc.vector.tensor_tensor(kst[:, b, t].rearrange("p (g d) -> p g d", g=2),
                                            h[:, t, c0:c0 + P].rearrange("p (g d) -> p g d", g=2), r,
                                            ALU.mult).then_inc(g.sig["hn_kst"], 1)
            dve.wait_ge(g.sig["hn_exp"], 2)
            link(nc.vector.tensor_scalar(gates[:], gates[:], 1.0, None, ALU.add))
            link(nc.vector.reciprocal(gates[:], gates[:]))
            link(nc.vector.memset(lamv[:], 1.0))
            link(nc.vector.tensor_tensor(ls[:, 0:1], ls[:, 3:4], ls[:, 2:3], ALU.subtract))
            for m in (1, 3):
                link(nc.vector.tensor_scalar(lamv[:, m:m + 1], ls[:, 0:1], LAMBDA_INIT, None, ALU.subtract))
            dve.wait_ge(g.sig["hn_pet"], 1)
            link(nc.vector.tensor_copy(pe_t[:], g.ps[:, 4, 0:64].rearrange("p (v l) -> p v l", v=2)))
            for v in range(2):
                dve.wait_ge(g.sig["hn_raw"], v + 1)
                for half in range(2):
                    nc.vector.tensor_tensor(blk[:, v, half], g.ps[:, 2 + v, :].rearrange("p (c l) -> p c l", l=16),
                                            pe_t[:, v, 16 * half:16 * half + 16].unsqueeze(1).to_broadcast([P, 32, 16]),
                                            ALU.add).then_inc(g.sig["hn_blk"], 1)
            dve.wait_ge(g.sig["hn_hs"], 2)
            link(nc.vector.tensor_tensor(hu[:], hid[:], hid[:], ALU.mult))
            link(nc.vector.tensor_scalar(hu[:], hu[:], 0.044715, 1.0, ALU.mult, ALU.add))
            nc.vector.tensor_tensor(hu[:], hu[:], hid[:], ALU.mult).then_inc(g.sig["hn_gu"], 1)
            dve.wait_ge(g.sig["hn_th"], 1)
            link(nc.vector.tensor_scalar(hu[:], hu[:], 1.0, 0.5, ALU.add, ALU.mult))
            nc.vector.tensor_tensor(hid[:], hu[:], hid[:], ALU.mult).then_inc(g.sig["hn_gel"], 1)
            dve.wait_ge(g.sig["hn_kc"], 4)
            link(nc.vector.tensor_tensor(kq[:], kc[:], kc[:], ALU.mult))
            link(nc.vector.tensor_reduce(kr[:, 2], kq[:], AX.X, ALU.add))
            nc.vector.tensor_scalar(kr[:, 0], kr[:, 2], 1.0 / 64, EPS, ALU.mult, ALU.add).then_inc(g.sig["hn_kms"], 1)
            dve.wait_ge(g.sig["hn_krm"], 1)
            link(nc.vector.reciprocal(kr[:, 2], kr[:, 1]))
            nc.vector.tensor_tensor(kq[:], kc[:], kr[:, 2].unsqueeze(2).to_broadcast([NCMP, 2, 64]), ALU.mult).then_inc(g.sig["hn_kn"], 1)

        @block.tensor
        def _(pe):
            pe.wait_ge(g.sig["hn_pe"], 32)
            nc.tensor.transpose(g.ps[:, 4, 0:64], pe_rows[:], f("ident")[0:64, 0:64]).then_inc(g.sig["hn_pet"], 1)
            for v in range(2):
                for t in range(TT):
                    last = nc.tensor.transpose(g.ps[:, 2 + v, t * P:(t + 1) * P],
                                               h[:, t, KV0 + v * P:KV0 + (v + 1) * P], f("ident"))
                last.then_inc(g.sig["hn_raw"], 1)
            for b in range(2):
                for t in range(TT):
                    pe.wait_ge(g.sig["hn_kst"], TT * b + t + 1)
                    last = nc.tensor.transpose(g.ps[:, b, t * P:(t + 1) * P], kst[:, b, t], f("ident"))
                last.then_inc(g.sig["hn_kt"], 1)
            pe.wait_ge(g.sig["hn_w"], 96)
            pe.wait_ge(g.sig["hn_blk"], 4)
            for grp in range(2):
                q = slice(64 * grp, 64 * grp + 64)
                for v in range(2):
                    for l in range(32):
                        src = blk[q, v, 0, 0:NCMP, l] if l < 16 else blk[q, v, 1, 1:NCMP + 1, l - 16]
                        last = nc.tensor.matmul(g.ps[q, 5 + grp, v * NCMP:(v + 1) * NCMP], w1[q, v, l], src,
                                                start=(l == 0), stop=(l == 31))
                last.then_inc(g.sig["hn_hid"], 1)
            pe.wait_ge(g.sig["hn_gel"], 1)
            for grp in range(2):
                q = slice(64 * grp, 64 * grp + 64)
                for v in range(2):
                    last = nc.tensor.matmul(g.ps[0:NCMP, 7 - 3 * grp, 64 * v:64 * v + 64], hid[q, v], w2[q, v],
                                            start=True, stop=True)
                last.then_inc(g.sig["hn_cmp"], 1)
            pe.wait_ge(g.sig["hn_kn"], 1)
            nc.tensor.transpose(g.ps[:, 5, 0:NCMP], kq[:].rearrange("p g d -> p (g d)"),
                                f("ident")[0:NCMP, 0:NCMP]).then_inc(g.sig["hn_kct"], 1)


def attention(nc, g, tag, sems, h, ocat, rs, qg, units, n_maps, kt_of, v_of, coef_of, stage, store):
    f = g.view
    U = len(units)
    per = n_maps
    sc, mx, ex, tp, pt, pv, stg, qt_t, kq_ev, cm, o_free = sems
    both = kt_of is None
    n_stage = 8 if both else 4
    n_links = stage["links"] + 4 * store["links"]
    with ExitStack() as mem:
        def sb(name, shape, dt=FP32):
            return mem.enter_context(nc.sbuf_tensor(tag + name, shape, dt))

        qs = sb("qs", [P, TT, P])
        ks = sb("ks", [P, TT, P]) if both else None
        q_t = sb("qt", [P, S])
        k_t = sb("kt", [P, S]) if both else None
        prob = sb("prob", [P, 2, S])
        prt = sb("prt", [P, 2, S])
        nmax = sb("nmax", [P, U])
        sums = sb("sums", [P, U])
        rec = sb("rec", [P, U])
        tmp = sb("tmp", [P, per, 64])
        block = mem.enter_context(nc.Block())

        def keys(u):
            qt, m, br = units[u]
            return NCMP if br == "cmp" else (qt + 1) * P

        def copy_on_act(u):
            return u % 2 == 0

        def copy_out(eng, run, i, u):
            eng.wait_ge(tp, i * U + u + 1)
            if u >= 2:
                eng.wait_ge(pv, i * U + u - 1)
            rows = slice(0, NCMP) if units[u][2] == "cmp" else slice(0, P)
            cols = P if units[u][2] == "cmp" else keys(u)
            run(prt[rows, u % 2, 0:cols], g.ps[rows, 4 + u % 2, 0:cols]).then_inc(pt[u % 2], 1)

        n_even, n_odd = (U + 1) // 2, U // 2

        @block.tensor
        def _(pe):
            with pe.Fori(0, 4) as i:
                for a, (src, dst) in enumerate([(qs, 0), (ks, 1)][:2 if both else 1]):
                    for t in range(TT):
                        pe.wait_ge(stg, i * n_stage + TT * a + t + 1)
                        last = nc.tensor.transpose(g.ps[:, dst, t * P:(t + 1) * P], src[:, t], f("ident"))
                    last.then_inc(qt_t, 1)

                def score(u):
                    qt, m, br = units[u]
                    q0, n = (32 * m, 32) if both else (64 * m, 64)
                    keys_t = k_t if both else kt_of[br]
                    bank = g.ps[:, 2 + u % 2, :]
                    if u >= 2:
                        pe.wait_ge(ex, i * U + u - 1)
                    nc.tensor.matmul(bank[:, 0:keys(u)], q_t[q0:q0 + n, qt * P:(qt + 1) * P],
                                     keys_t[q0:q0 + n, 0:keys(u)], start=True, stop=True)
                    if br == "cmp":
                        mask, at = g.cnegb[:, qt * NCMP:(qt + 1) * NCMP], bank[:, 0:NCMP]
                    else:
                        mask, at = g.negb[:], bank[:, qt * P:(qt + 1) * P]
                    nc.tensor.matmul(at, g.identb[:], mask, start=False, stop=True, skip_group_check=True).then_inc(sc, 1)

                def turn(u):
                    if units[u][2] == "cmp":
                        pe.wait_ge(cm, i * store["n_cmp"] + sum(x[2] == "cmp" for x in units[:u]) + 1)
                    else:
                        pe.wait_ge(ex, i * U + u + 1)
                    if u >= 2:
                        pe.wait_ge(pt[u % 2], i * (n_odd if u % 2 else n_even) + u // 2)
                    if units[u][2] == "cmp":
                        last = nc.tensor.transpose(g.ps[0:NCMP, 4 + u % 2, 0:P], prob[:, u % 2, 0:NCMP], f("ident"))
                    else:
                        for b in range(units[u][0] + 1):
                            last = nc.tensor.transpose(g.ps[:, 4 + u % 2, b * P:(b + 1) * P],
                                                       prob[:, u % 2, b * P:(b + 1) * P], f("ident"))
                    last.then_inc(tp, 1)

                def values(u):
                    qt, m, br = units[u]
                    slot = u % per
                    if slot == 0 and qt >= 2:
                        pe.wait_ge(o_free, i * TT + qt - 1)
                    pe.wait_ge(pt[u % 2], i * (n_odd if u % 2 else n_even) + u // 2 + 1)
                    out = g.ps[:, 6 + qt % 2, slot * 64:slot * 64 + 64]
                    if br == "cmp":
                        last = nc.tensor.matmul(out, prt[0:NCMP, u % 2, 0:P], v_of(i, 0, m, br), start=True, stop=True)
                    else:
                        for b in range(qt + 1):
                            last = nc.tensor.matmul(out, prt[:, u % 2, b * P:(b + 1) * P], v_of(i, b, m, br),
                                                    start=(b == 0), stop=(b == qt))
                    last.then_inc(pv, 1)

                pe.wait_ge(kq_ev, i * (2 if both else 1) + (2 if both else 1))
                score(0)
                for u in range(U):
                    if u + 1 < U:
                        score(u + 1)
                    turn(u)
                    if u >= 1:
                        values(u - 1)
                values(U - 1)

        @block.scalar
        def _(act):
            with act.Fori(0, 4) as i:
                act.wait_ge(qt_t, i * (2 if both else 1) + 1)
                nc.scalar.activation(q_t[:], g.ps[:, 0, :], ACT.Copy, scale=qg).then_inc(kq_ev, 1)
                if both:
                    act.wait_ge(qt_t, i * 2 + 2)
                    nc.scalar.activation(k_t[:], g.ps[:, 1, :], ACT.Copy, scale=g.vec[:, V_DK:V_DK + 1]).then_inc(kq_ev, 1)

                def exp(u):
                    act.wait_ge(mx, i * U + u + 1)
                    if u >= 2:
                        act.wait_ge(tp, i * U + u - 1)
                    nc.scalar.activation(prob[:, u % 2, 0:keys(u)], g.ps[:, 2 + u % 2, 0:keys(u)], ACT.Exp,
                                         bias=nmax[:, u:u + 1], accum_out=sums[:, u:u + 1]).then_inc(ex, 1)

                exp(0)
                for u in range(U):
                    if u + 1 < U:
                        exp(u + 1)
                    if copy_on_act(u):
                        copy_out(act, lambda o, x: nc.scalar.activation(o, x, ACT.Copy), i, u)

        @block.vector
        def _(dve):
            with dve.Fori(0, 4) as i:
                link = Link(dve, g.sig["att_link"], g.att_base[0] + i * n_links)
                for op in stage["ops"](i, qs, ks):
                    op().then_inc(stg, 1)

                def top(u):
                    dve.wait_ge(sc, i * U + u + 1)
                    nc.vector.tensor_reduce(nmax[:, u:u + 1], g.ps[:, 2 + u % 2, 0:keys(u)], AX.X, ALU.max,
                                            negate=True).then_inc(mx, 1)

                def combine(qt):
                    dve.wait_ge(pv, i * U + per * (qt + 1))
                    if not both:
                        dve.wait_ge(ex, i * U + per * (qt + 1))
                    c = slice(per * qt, per * qt + per)
                    link(nc.vector.tensor_scalar(rec[:, c], sums[:, c], 1e-30, None, ALU.max))
                    link(nc.vector.reciprocal(rec[:, c], rec[:, c]))
                    link(coef_of(i, qt, rec[:, c]))
                    nc.vector.tensor_tensor(tmp[:], g.ps[:, 6 + qt % 2, 0:per * 64].rearrange("p (m d) -> p m d", d=64),
                                            rec[:, c].unsqueeze(2).to_broadcast([P, per, 64]), ALU.mult).then_inc(o_free, 1)
                    dve.wait_ge(o_free, i * TT + qt + 1)
                    for ins in store["ops"](i, qt, tmp):
                        link(ins())

                top(0)
                for u in range(U):
                    if u + 1 < U:
                        top(u + 1)
                    if units[u][2] == "cmp":
                        dve.wait_ge(ex, i * U + u + 1)
                        nc.vector.scalar_tensor_tensor(prob[:, u % 2, 0:NCMP], prob[:, u % 2, 0:NCMP], 1.0,
                                                       f("cok")[:, units[u][0] * NCMP:(units[u][0] + 1) * NCMP],
                                                       ALU.mult, ALU.mult, accum_out=sums[:, u:u + 1]).then_inc(cm, 1)
                    if not copy_on_act(u):
                        copy_out(dve, nc.vector.tensor_copy, i, u)
                    if u >= 1 and u % per == 0:
                        combine(u // per - 1)
                combine(TT - 1)
        g.att_base[0] += 4 * n_links


def diff_attention(nc, g, h, ocat, rs, qg, lamv):
    units = [(qt, m, "diff") for qt in range(TT) for m in range(4)]

    def stage_ops(i, qs, ks):
        for dst, c0, s0 in ((qs, DQ0, 0), (ks, DK0, 16)):
            for t in range(TT):
                yield lambda dst=dst, c0=c0, s0=s0, t=t: nc.vector.tensor_tensor(
                    dst[:, t].rearrange("p (m d) -> p m d", d=32),
                    h[:, t, bass.ds(c0 + i * P, P)].rearrange("p (m d) -> p m d", d=32),
                    rs[:, t, bass.ds(s0 + i * 4, 4)].unsqueeze(2).to_broadcast([P, 4, 32]), ALU.mult)

    def store_ops(i, qt, tmp):
        out = ocat[:, qt, bass.ds(i * P, P)].rearrange("p (m d) -> p m d", d=64)
        yield lambda: nc.vector.tensor_tensor(out, tmp[:, 0:4:2], tmp[:, 1:4:2], ALU.add)

    attention(nc, g, "da_", g.da, h, ocat, rs, qg[:, 0:1], units, 4, None,
              lambda i, b, m, br: h[:, b, bass.ds(DV0 + i * P + 64 * (m // 2), 64)],
              lambda i, qt, rec: nc.vector.tensor_tensor(rec, rec, lamv[:], ALU.mult),
              dict(ops=stage_ops, links=0), dict(ops=store_ops, links=4, n_cmp=0))


def nsa_attention(nc, g, h, ocat, rs, qg, gates, kt_sel, kt_win, kc_t, vc):
    units = [(qt, grp, br) for qt in range(TT) for grp in range(2) for br in ("cmp", "sel", "win")]

    def stage_ops(i, qs, ks):
        q = h[:, :, NQ0:KV0].rearrange("p t (g j d) -> p t g j d", g=2, j=4)
        r = rs[:, :, 32:40].rearrange("p t (g j) -> p t g j", g=2)
        for t in range(TT):
            yield lambda t=t: nc.vector.tensor_tensor(
                qs[:, t].rearrange("p (g d) -> p g d", g=2), q[:, t, :, bass.ds(i, 1), :].squeeze(2),
                r[:, t, :, bass.ds(i, 1)].to_broadcast([P, 2, 64]), ALU.mult)

    def value(i, b, m, br):
        if br == "cmp":
            return vc[:, m]
        c0 = KV0 + (256 if br == "sel" else 512) + P + 64 * m
        return h[:, b, c0:c0 + 64]

    def coef(i, qt, rec):
        gate = gates[:, qt].rearrange("p (g j b) -> p g j b", g=2, j=4)[:, :, bass.ds(i, 1), :].squeeze(2)
        r = rec.rearrange("p (g b) -> p g b", g=2)
        return nc.vector.tensor_tensor(r, r, gate, ALU.mult)

    def store_ops(i, qt, tmp):
        out = ocat[:, qt, 512:1024].rearrange("p (g j d) -> p g j d", g=2, j=4)[:, :, bass.ds(i, 1), :].squeeze(2)
        br = tmp[:].rearrange("p (g b) d -> p g b d", g=2)
        yield lambda: nc.vector.tensor_tensor(br[:, :, 0], br[:, :, 0], br[:, :, 1], ALU.add)
        yield lambda: nc.vector.tensor_tensor(out, br[:, :, 0], br[:, :, 2], ALU.add)

    attention(nc, g, "na_", g.na, h, ocat, rs, qg[:, 1:2], units, 6, dict(cmp=kc_t, sel=kt_sel, win=kt_win),
              value, coef, dict(ops=stage_ops, links=0), dict(ops=store_ops, links=5, n_cmp=8))


def project_out(nc, g, n, w, src, src_t, scales):
    w_v = w.rearrange("(k p) (c n) -> c p k n", p=P, n=S)
    f = g.view
    with nc.sbuf_tensor(f"wo{n}", [P, 2, KT, S], FP32) as wt, nc.Block() as block:

        @block.sync
        def _(sp):
            for c in range(2):
                sp.dma_start(wt[:, c], w_v[c]).then_inc(g.sig["po_in"][c], 16)

        @block.tensor
        def _(pe):
            if src is not None:
                for k in range(KT):
                    for t in range(TT):
                        last = nc.tensor.transpose(g.ps[:, k, t * P:(t + 1) * P], src[:, t, k * P:(k + 1) * P], f("ident"))
                    last.then_inc(g.sig["po_tr"], 1)
                pe.wait_ge(g.sig["po_ev"][0], KT // 2)
                pe.wait_ge(g.sig["po_ev"][1], KT // 2)
            for c in range(2):
                pe.wait_ge(g.sig["po_in"][c], 16)
                for t in range(TT):
                    for k in range(KT):
                        last = nc.tensor.matmul(g.ps[:, TT * c + t, :], src_t[:, k, t * P:(t + 1) * P], wt[:, c, k, :],
                                                start=(k == 0), stop=(k == KT - 1))
                    last.then_inc(g.sig["po_mm"], 1)

        @block.scalar
        def _(act):
            if src is not None:
                for k in range(0, KT, 2):
                    act.wait_ge(g.sig["po_tr"], k + 1)
                    nc.scalar.activation(src_t[:, k], g.ps[:, k, :], ACT.Copy, scale=scales[k]).then_inc(g.sig["po_ev"][0], 1)

        @block.vector
        def _(dve):
            if src is not None:
                for k in range(1, KT, 2):
                    dve.wait_ge(g.sig["po_tr"], k + 1)
                    nc.vector.tensor_scalar(src_t[:, k], g.ps[:, k, :], scales[k], None, ALU.mult).then_inc(g.sig["po_ev"][1], 1)
            for c in range(2):
                for t in range(TT):
                    dve.wait_ge(g.sig["po_mm"], TT * c + t + 1)
                    xv = g.x[:, t, c * S:(c + 1) * S]
                    nc.vector.tensor_tensor(xv, g.ps[:, TT * c + t, :], xv, ALU.add).then_inc(g.sig["po_done"], 1)


def sub_norm(nc, g, ocat):
    with nc.sbuf_tensor("sn_sq", [P, TT, 512], FP32) as sq, nc.sbuf_tensor("sn_st", [P, 2, TT, 8], FP32) as st, \
            nc.sbuf_tensor("sn_rms", [P, TT, 8], FP32) as rms, nc.Block() as block:

        @block.scalar
        def _(act):
            nc.scalar.activation(sq[:], ocat[:, :, 0:512], ACT.Square).then_inc(g.sig["sn_sq"], 1)
            act.wait_ge(g.sig["sn_ms"], 1)
            nc.scalar.activation(rms[:], st[:, 1], ACT.Sqrt).then_inc(g.sig["sn_rms"], 1)
            nc.scalar.activation(g.subg[:, 0:1], g.vec[:, V_SUB:V_SUB + 1], ACT.Copy, scale=1.0 - LAMBDA_INIT).then_inc(g.sig["sn_rms"], 1)

        @block.vector
        def _(dve):
            link = Link(dve, g.sig["sn_link"])
            link(nc.vector.memset(g.subg[:, 1:2], 1.0))
            dve.wait_ge(g.sig["sn_sq"], 1)
            link(nc.vector.tensor_reduce(st[:, 0], sq[:].rearrange("p t (s d) -> p t s d", d=64), AX.X, ALU.add))
            nc.vector.tensor_scalar(st[:, 1], st[:, 0], 1.0 / 64, EPS, ALU.mult, ALU.add).then_inc(g.sig["sn_ms"], 1)
            dve.wait_ge(g.sig["sn_rms"], 1)
            link(nc.vector.reciprocal(st[:, 0], rms[:]))
            for t in range(TT):
                o = ocat[:, t, 0:512].rearrange("p (s d) -> p s d", d=64)
                link(nc.vector.tensor_tensor(o, o, st[:, 0, t].unsqueeze(2).to_broadcast([P, 8, 64]), ALU.mult))


def moe(nc, g, L, ins, out=None):
    f = g.view
    pairs = 2 * S
    xs_dram, y_dram, table = g.xs_dram[L], g.y_dram[L], g.table[L]
    with ExitStack() as mem:
        def sb(name, shape, dt=FP32):
            return mem.enter_context(nc.sbuf_tensor(f"m{L}_{name}", shape, dt))

        wg = [sb(f"wg{b}", [P, KT, DE]) for b in range(4)]
        wu = [sb(f"wu{b}", [P, KT, DE]) for b in range(4)]
        wd = [sb(f"wd{b}", [P, 2, D]) for b in range(4)]
        gain = sb("gain", [P, KT])
        idx_all = sb("idx_all", [CAP, NE], I32)
        n_max = sb("n_max", [P, 1], I32)
        gate = sb("gate", [P, 2, TT])
        wg_v = ins["expert_w_gate"][L].rearrange("e (p k) f -> e p k f", k=KT)
        wu_v = ins["expert_w_up"][L].rearrange("e (p k) f -> e p k f", k=KT)
        wd_v = ins["expert_w_down"][L].rearrange("e (j p) d -> e p j d", p=P)

        def load_expert(sp, e, b, sem):
            sp.dma_start(wg[b][:], wg_v[e]).then_inc(sem[b], 16)
            sp.dma_start(wu[b][:], wu_v[e]).then_inc(sem[b], 16)
            sp.dma_start(wd[b][:], wd_v[e]).then_inc(sem[b], 16)

        with nc.Block() as block:
            @block.sync
            def _(sp):
                sp.dma_start(gain[:], ins["ffn_norm"][L].rearrange("(p k) -> p k", k=KT)).then_inc(g.sig["gain_in"], 16)
                sp.wait_ge(g.sig["gain_in"], 16)
                for b in range(4):
                    load_expert(sp, b, b, g.sig["w_in"])

        with nc.sbuf_tensor(f"m{L}_xs", [P, TT, D], FP32) as xs, nc.sbuf_tensor(f"m{L}_xt", [P, KT, S], FP32) as x_t:
            normalise(nc, g, xs, x_t, gain[:], True, store=(xs_dram[0:S], xs_dram[S:2 * S]))
            route(nc, g, L, ins, x_t, gate, n_max, table)
        with nc.Block() as block:
            @block.gpsimd
            def _(pool):
                pool.wait_ge(g.sig["xs_out"], 32)
                pool.dma_start(idx_all[:], table[0:NE * CAP].rearrange("(p e) a -> p (e a)", e=NE)).then_inc(g.idx_in, 16)
                pool.wait_ge(g.idx_in, 16)

        xg = [sb(f"xg{b}", [CAP, D]) for b in range(4)]
        ids_g = [sb(f"ids_g{b}", [CAP, 1], I32) for b in range(4)]
        ids_s = [sb(f"ids_s{b}", [CAP, 1], I32) for b in range(4)]
        xg_t = [sb(f"xgt{b}", [P, KT, CAP]) for b in range(2)]
        act_g = [sb(f"ag{b}", [P, 2, CAP]) for b in range(2)]
        hid = [sb(f"hid{b}", [P, 2, CAP]) for b in range(2)]
        ysb = [sb(f"ysb{b}", [CAP, D]) for b in range(4)]
        m = dict(wg=wg, wu=wu, wd=wd, gain=gain, xg=xg, ids_g=ids_g, ids_s=ids_s, xg_t=xg_t, act_g=act_g, hid=hid,
                            ysb=ysb, xs_dram=xs_dram, y_dram=y_dram, table=table, load_expert=load_expert, idx_all=idx_all)
        experts(nc, g, L, None, m)
        experts(nc, g, L, n_max, m)
        combine(nc, g, L, gate, y_dram, out)


def route(nc, g, L, ins, x_t, gate, n_max, table):
    f = g.view
    with ExitStack() as mem:
        def sb(name, shape, dt=FP32):
            return mem.enter_context(nc.sbuf_tensor(f"r{L}_{name}", shape, dt))

        wr = sb("w", [P, KT, NG + NE])
        br = sb("b", [P, NG + NE])
        lg = sb("lg", [P, TT, NG + NE])
        eg = sb("eg", [P, TT, NG])
        cand4 = sb("cand4", [P, TT, NG])
        one_g = sb("one_g", [P, TT, NG])
        ml = sb("ml", [P, TT, NE])
        cand = sb("cand", [P, TT, NE])
        pick = [sb(f"pick{c}", [P, TT, NE]) for c in range(2)]
        both = sb("both", [P, TT, NE])
        st = sb("st", [P, 12, TT])
        rank = sb("rank", [P, TT, NE])
        slot = sb("slot", [P, 2, TT])
        slot_i = sb("slot_i", [P, 2, TT], I32)
        pair_i = sb("pair_i", [P, 2, TT], I32)
        top = sb("top", [P, 1])
        fill = sb("fill", [P, ROUNDS * NE * CAP // P], I32)
        block = mem.enter_context(nc.Block())

        @block.sync
        def _(sp):
            sp.dma_start(wr[:, :, 0:NG], ins["router_group_w"][L].rearrange("(p k) e -> p k e", k=KT)).then_inc(g.sig["r_in"], 16)
            sp.dma_start(wr[:, :, NG:], ins["router_expert_w"][L].rearrange("(p k) e -> p k e", k=KT)).then_inc(g.sig["r_in"], 16)
            sp.dma_start(br[:, 0:NG], ins["router_group_b"][L].partition_broadcast(P)).then_inc(g.sig["r_in"], 16)
            sp.dma_start(br[:, NG:], ins["router_expert_b"][L].partition_broadcast(P)).then_inc(g.sig["r_in"], 16)

        @block.tensor
        def _(pe):
            pe.wait_ge(g.sig["r_in"], 64)
            for t in range(TT):
                for k in range(KT):
                    last = nc.tensor.matmul(g.ps[:, 0, t * 64:t * 64 + NG + NE], x_t[:, k, t * P:(t + 1) * P], wr[:, k, :],
                                            start=(k == 0), stop=(k == KT - 1))
            last.then_inc(g.sig["r_lg"], 1)
            pe.wait_ge(g.sig["r_both"], 1)
            for t in range(TT):
                for u in range(t + 1):
                    last = nc.tensor.matmul(g.ps[:, 1, t * NE:(t + 1) * NE], f("upper") if u == t else f("ones"), both[:, u],
                                            start=(u == 0), stop=(u == t))
            for u in range(TT):
                last = nc.tensor.matmul(g.ps[:, 2, 0:NE], f("ones"), both[:, u], start=(u == 0), stop=(u == TT - 1))
            last.then_inc(g.sig["r_rank"], 1)

        @block.scalar
        def _(act):
            act.wait_ge(g.sig["r_sub"], 1)
            nc.scalar.activation(eg[:], eg[:], ACT.Exp).then_inc(g.sig["r_exp"], 1)
            act.wait_ge(g.sig["r_sub"], 2)
            nc.scalar.activation(st[:, 5], st[:, 4], ACT.Exp).then_inc(g.sig["r_exp"], 1)

        @block.vector
        def _(dve):
            link = Link(dve, g.sig["r_link"])

            def col(t_, n):
                return t_.unsqueeze(2).to_broadcast([P, TT, n])

            def first_max(src, n, iota, far, c_, onehot, m):
                link(nc.vector.tensor_reduce(m, src, AX.X, ALU.max))
                link(nc.vector.tensor_tensor(c_, src, col(m, n), ALU.is_ge))
                link(nc.vector.scalar_tensor_tensor(c_, c_, -far, f(iota).unsqueeze(1).to_broadcast([P, TT, n]), ALU.mult, ALU.add))
                link(nc.vector.tensor_reduce(st[:, 11], c_, AX.X, ALU.min))
                link(nc.vector.tensor_tensor(onehot, c_, col(st[:, 11], n), ALU.is_equal))

            dve.wait_ge(g.sig["r_in"], 64)
            dve.wait_ge(g.sig["r_lg"], 1)
            link(nc.vector.tensor_tensor(lg[:], g.ps[:, 0, 0:256].rearrange("p (t e) -> p t e", e=64)[:, :, 0:NG + NE],
                                         br[:].unsqueeze(1).to_broadcast([P, TT, NG + NE]), ALU.add))
            first_max(lg[:, :, 0:NG], NG, "iota4", 8.0, cand4[:], one_g[:], st[:, 0])
            nc.vector.tensor_tensor(eg[:], lg[:, :, 0:NG], col(st[:, 0], NG), ALU.subtract).then_inc(g.sig["r_sub"], 1)
            og = one_g[:].unsqueeze(3).to_broadcast([P, TT, NG, EPG])
            ml4, lg4 = (v.rearrange("p t (g e) -> p t g e", g=NG) for v in (ml[:], lg[:, :, NG:]))
            c4 = cand[:].rearrange("p t (g e) -> p t g e", g=NG)
            for t in range(TT):
                link(nc.vector.tensor_tensor(ml4[:, t], lg4[:, t], og[:, t], ALU.mult))
                link(nc.vector.tensor_scalar(c4[:, t], og[:, t], -1.0, BIG, ALU.add, ALU.mult))
            link(nc.vector.tensor_tensor(ml[:], ml[:], cand[:], ALU.add))
            first_max(ml[:], NE, "iota32", 64.0, cand[:], pick[0][:], st[:, 2])
            link(nc.vector.scalar_tensor_tensor(ml[:], pick[0][:], -2.0 * BIG, ml[:], ALU.mult, ALU.add))
            first_max(ml[:], NE, "iota32", 64.0, cand[:], pick[1][:], st[:, 3])
            nc.vector.tensor_tensor(both[:], pick[0][:], pick[1][:], ALU.add).then_inc(g.sig["r_both"], 1)
            nc.vector.tensor_tensor(st[:, 4], st[:, 3], st[:, 2], ALU.subtract).then_inc(g.sig["r_sub"], 1)
            dve.wait_ge(g.sig["r_exp"], 2)
            link(nc.vector.tensor_reduce(st[:, 6], eg[:], AX.X, ALU.add))
            link(nc.vector.tensor_scalar(st[:, 7], st[:, 5], 1.0, None, ALU.add))
            link(nc.vector.tensor_tensor(st[:, 8], st[:, 6], st[:, 7], ALU.mult))
            link(nc.vector.reciprocal(gate[:, 0], st[:, 8]))
            link(nc.vector.tensor_tensor(gate[:, 1], gate[:, 0], st[:, 5], ALU.mult))
            dve.wait_ge(g.sig["r_rank"], 1)
            link(nc.vector.tensor_copy(rank[:], g.ps[:, 1, 0:TT * NE].rearrange("p (t e) -> p t e", t=TT)))
            link(nc.vector.tensor_reduce(top[:], g.ps[:, 2, 0:NE], AX.X, ALU.max))
            link(nc.vector.tensor_copy(n_max[:], top[:]))
            link(nc.vector.scalar_tensor_tensor(rank[:], rank[:], float(NE), f("iota32").unsqueeze(1).to_broadcast([P, TT, NE]),
                                                ALU.mult, ALU.add))
            for c in range(2):
                link(nc.vector.tensor_tensor(cand[:], rank[:], pick[c][:], ALU.mult))
                link(nc.vector.tensor_reduce(slot[:, c], cand[:], AX.X, ALU.add))
            link(nc.vector.tensor_copy(pair_i[:], f("pair").rearrange("p (c t) -> p c t", c=2)))
            nc.vector.tensor_copy(slot_i[:], slot[:]).then_inc(g.sig["r_slot"], 1)

        @block.gpsimd
        def _(pool):
            nc.gpsimd.memset(fill[:], 2 * S).then_inc(g.sig["r_fill"], 1)
            pool.wait_ge(g.sig["r_fill"], 1)
            pool.dma_start(table.rearrange("(p n) a -> p (n a)", p=P), fill[:]).then_inc(g.r_tab, 16)
            pool.wait_ge(g.r_tab, 16)
            pool.wait_ge(g.sig["r_slot"], 1)
            for c in range(2):
                for t in range(TT):
                    pool.indirect_dma_start(out=table, out_offset=bass.IndirectOffsetOnAxis(ap=slot_i[:, c, t:t + 1], axis=0),
                                            in_=pair_i[:, c, t:t + 1], in_offset=None).then_inc(g.r_tab, 16)
            pool.wait_ge(g.r_tab, 16 * 9)


def experts(nc, g, L, n_max, m):
    f = g.view
    wg, wu, wd, gain, xg, ids_g, ids_s, xg_t = m["wg"], m["wu"], m["wd"], m["gain"], m["xg"], m["ids_g"], m["ids_s"], m["xg_t"]
    act_g, hid, ysb, xs_dram, y_dram, table, load_expert, idx_all = (
        m["act_g"], m["hid"], m["ysb"], m["xs_dram"], m["y_dram"], m["table"], m["load_expert"], m["idx_all"])
    more = n_max is not None
    s = g.ex[more]
    PASSES = NE // 4

    def passes(eng, run, r):
        with eng.Fori(0, PASSES) as i:
            run(i + (r - 1) * PASSES if more else i, i)

    def rounds(eng, one_round):
        if not more:
            one_round(0)
        else:
            top = eng.value_load(n_max[0:1, 0:1], min_val=0, max_val=S)
            for r in range(1, ROUNDS):
                with eng.If(top > r * CAP):
                    one_round(r)

    with nc.Block() as block:

        @block.sync
        def _(sp):
            def run(i, e4):
                for b in range(4):
                    sp.wait_ge(s["down"][b], i + (0 if not more else 1))
                    load_expert(sp, 4 * e4 + b, b, s["w"])
            if not more:
                with sp.Fori(1, PASSES) as i:
                    run(i, i)
            else:
                for b in range(4):
                    sp.nop().then_inc(s["down"][b], 1)
                rounds(sp, lambda r: passes(sp, run, r))

        @block.gpsimd
        def _(pool):
            held = Held(pool, s["held"])

            def gather(n, e4, b):
                nc.gpsimd.tensor_copy(ids_g[b][:], idx_all[:, bass.ds(4 * e4 + b, 1)]).then_inc(s["ids"][b], 1)
                pool.wait_ge(s["ids"][b], n + 1)
                held()
                pool.indirect_dma_start(out=xg[b][:], out_offset=None, in_=xs_dram,
                                        in_offset=bass.IndirectOffsetOnAxis(ap=ids_g[b][:, 0:1], axis=0),
                                        bounds_check=2 * S - 1, oob_is_err=False).then_inc(s["rows"][b], 16)

            def ready(i, e4, b, first, last):
                if not first:
                    pool.wait_ge(s["scat"][b], 16 * i)
                nc.gpsimd.tensor_copy(ids_s[b][:], idx_all[:, bass.ds(4 * e4 + b, 1)]).then_inc(s["y_free"][b], 1)
                if not last:
                    pool.wait_ge(s["turn"], 8 * i + 2 * b + 2)
                    gather(i + 1, e4 + 1, b)

            def scatter(i, b):
                pool.wait_ge(s["y_free"][b], i + 1)
                pool.wait_ge(s["y"][b], 2 * i + 2)
                held()
                pool.indirect_dma_start(out=y_dram, out_offset=bass.IndirectOffsetOnAxis(ap=ids_s[b][:, 0:1], axis=0),
                                        in_=ysb[b][:], in_offset=None,
                                        bounds_check=2 * S - 1, oob_is_err=False).then_inc(s["scat"][b], 16)

            def one_pass(i, e4, first=False, last=False):
                ready(i, e4, 0, first, last)
                for b in range(1, 4):
                    ready(i, e4, b, first, last)
                    scatter(i, b - 1)
                scatter(i, 3)

            def one_round(r):
                base = (r - 1) * PASSES if more else 0
                if more:
                    if r > 1:
                        for b in range(4):
                            pool.wait_ge(s["scat"][b], 16 * base)
                    pool.dma_start(idx_all[:], table[r * NE * CAP:(r + 1) * NE * CAP].rearrange("(p e) a -> p (e a)", e=NE))\
                        .then_inc(g.idx_in, 16)
                    pool.wait_ge(g.idx_in, 16 * (r + 1))
                for b in range(4):
                    gather(base, 0, b)
                one_pass(base, 0, first=True)
                with pool.Fori(1, PASSES - 1) as e4:
                    one_pass(e4 + base, e4)
                one_pass(base + PASSES - 1, PASSES - 1, last=True)
                for b in range(4):
                    pool.wait_ge(s["scat"][b], 16 * (base + PASSES))

            if not more:
                for b in range(4):
                    nc.gpsimd.memset(xg[b][:], 0.0).then_inc(s["zero"], 1)
                pool.wait_ge(s["zero"], 4)
            rounds(pool, one_round)

        @block.tensor
        def _(pe):
            def turn(i, b):
                pe.wait_ge(s["rows"][b], 16 * i + 16)
                if b >= 2:
                    pe.wait_ge(s["up"], 4 * i + b - 1)
                    pe.wait_ge(s["xt"][b % 2], 4 * i + 2)
                for k in range(KT):
                    last = nc.tensor.transpose(g.ps[:, 2 * (b % 2) + k // 4, (k % 4) * CAP:(k % 4 + 1) * CAP],
                                               xg[b][:, k:D:KT], f("ident")[0:CAP, 0:CAP])
                    if k % 4 == 3:
                        last.then_inc(s["turn"], 1)

            def up(i, b):
                pe.wait_ge(s["w"][b], 48 * i + 48)
                pe.wait_ge(s["xt"][b % 2], 4 * i + 2 * (b // 2) + 2)
                if b >= 2:
                    pe.wait_ge(s["hid"], 4 * i + b - 1)
                bank = g.ps[:, 4 + b % 2, :]
                for n, w in enumerate((wg[b], wu[b])):
                    for j in range(2):
                        for k in range(KT):
                            last = nc.tensor.matmul(bank[:, (2 * n + j) * CAP:(2 * n + j + 1) * CAP], w[:, k, j * P:(j + 1) * P],
                                                    xg_t[b % 2][:, k, :], start=(k == 0), stop=(k == KT - 1))
                last.then_inc(s["up"], 1)

            def down(i, b):
                pe.wait_ge(s["hid"], 4 * i + b + 1)
                if b >= 1:
                    pe.wait_ge(s["y"][b - 1], 2 * i + 2)
                for c in range(2):
                    for j in range(2):
                        last = nc.tensor.matmul(g.ps[0:CAP, 6 + c, :], hid[b % 2][:, j, :], wd[b][:, j, c * S:(c + 1) * S],
                                                start=(j == 0), stop=(j == 1))
                    if c == 0:
                        last.then_inc(s["half"], 1)
                last.then_inc(s["down"][b], 1)

            def run(i, e4):
                turn(i, 0)
                turn(i, 1)
                up(i, 0)
                for b in range(1, 4):
                    if b + 1 < 4:
                        turn(i, b + 1)
                    up(i, b)
                    down(i, b - 1)
                down(i, 3)

            rounds(pe, lambda r: passes(pe, run, r))

        def xt_out(eng, i, b, half):
            eng.wait_ge(s["turn"], 8 * i + 2 * b + half + 1)
            if b >= 2:
                eng.wait_ge(s["up"], 4 * i + b - 1)
            gn = gain[:, 4 * half:4 * half + 4].unsqueeze(2).to_broadcast([P, 4, CAP])
            nc.vector.tensor_tensor(xg_t[b % 2][:, 4 * half:4 * half + 4, :],
                                    g.ps[:, 2 * (b % 2) + half, 0:4 * CAP].rearrange("p (k n) -> p k n", n=CAP), gn,
                                    ALU.mult).then_inc(s["xt"][b % 2], 1)

        @block.scalar
        def _(act):
            def silu(i, b):
                act.wait_ge(s["up"], 4 * i + b + 1)
                if b >= 2:
                    act.wait_ge(s["hid"], 4 * i + b - 1)
                nc.scalar.activation(act_g[b % 2][:], g.ps[:, 4 + b % 2, 0:2 * CAP].rearrange("p (j n) -> p j n", j=2),
                                     ACT.Silu).then_inc(s["silu"], 1)

            def y_out(i, b):
                act.wait_ge(s["y_free"][b], i + 1)
                act.wait_ge(s["half"], 4 * i + b + 1)
                nc.scalar.activation(ysb[b][:, 0:S], g.ps[0:CAP, 6, :], ACT.Copy).then_inc(s["y"][b], 1)
                act.wait_ge(s["down"][b], i + (2 if more else 1))
                nc.scalar.activation(ysb[b][:, S:D], g.ps[0:CAP, 7, :], ACT.Copy).then_inc(s["y"][b], 1)

            def run(i, e4):
                silu(i, 0)
                for b in range(1, 4):
                    silu(i, b)
                    y_out(i, b - 1)
                y_out(i, 3)

            rounds(act, lambda r: passes(act, run, r))

        @block.vector
        def _(dve):
            def mix(i, b):
                dve.wait_ge(s["silu"], 4 * i + b + 1)
                if b >= 2:
                    dve.wait_ge(s["half"], 4 * i + b - 1)
                    dve.wait_ge(s["down"][b - 2], i + (2 if more else 1))
                nc.vector.tensor_tensor(hid[b % 2][:], act_g[b % 2][:],
                                        g.ps[:, 4 + b % 2, 2 * CAP:4 * CAP].rearrange("p (j n) -> p j n", j=2),
                                        ALU.mult).then_inc(s["hid"], 1)

            def run(i, e4):
                for b in range(2):
                    for half in range(2):
                        xt_out(dve, i, b, half)
                mix(i, 0)
                for b in range(1, 4):
                    if b + 1 < 4:
                        for half in range(2):
                            xt_out(dve, i, b + 1, half)
                    mix(i, b)

            rounds(dve, lambda r: passes(dve, run, r))


def combine(nc, g, L, gate, y_dram, out):
    with nc.sbuf_tensor(f"c{L}_y", [P, 2, TT, D], FP32) as y, nc.Block() as block:

        @block.sync
        def _(sp):
            src = y_dram.rearrange("(c t p) d -> p c t d", p=P, c=2)
            for t in range(TT):
                for c in range(2):
                    sp.dma_start(y[:, c, t], src[:, c, t]).then_inc(g.sig["y_in"][t], 16)
            if out is not None:
                dst = out[0].rearrange("(t p) d -> p t d", p=P)
                for t in range(TT):
                    sp.wait_ge(g.sig["y_add"], 2 * t + 2)
                    sp.dma_start(dst[:, t], g.x[:, t]).then_inc(g.sig["out_done"], 16)
                sp.wait_ge(g.sig["out_done"], 16 * TT)

        @block.vector
        def _(dve):
            for t in range(TT):
                dve.wait_ge(g.sig["y_in"][t], 32)
                for c in range(2):
                    nc.vector.scalar_tensor_tensor(g.x[:, t], y[:, c, t], gate[:, c, t:t + 1], g.x[:, t], ALU.mult,
                                                   ALU.add).then_inc(g.sig["y_add"], 1)
                    dve.wait_ge(g.sig["y_add"], 2 * t + c + 1)


def rwkv_layer(nc, g, ins):
    with signals(nc, "rw_", RWKV_SIGNALS, RWKV_GROUPS) as g.sig, ExitStack() as mem:
        def sb(name, shape, dt=FP32):
            return mem.enter_context(nc.sbuf_tensor("rw_" + name, shape, dt))

        g.c_stage = dict(zip("ABKVR", g.sig["c_staged"]))
        a = Shared()
        a.r, a.k, a.v, a.kk, a.b = (sb(n, [P, KT, S]) for n in ("r", "k", "v", "kk", "b"))
        a.cs = g.x[:].rearrange("p t (h s) -> p (t h) s", s=S)
        with ExitStack() as proj:
            x_t = proj.enter_context(nc.sbuf_tensor("rw_xt", [P, KT, S], FP32))
            with nc.sbuf_tensor("rw_xs", [P, TT, D], FP32) as xs:
                normalise(nc, g, xs, x_t, g.vec[:, V_MIX1:V_MIX1 + 8], False)
            x0 = proj.enter_context(nc.sbuf_tensor("rw_x0", [P, KT, S], FP32))
            rwkv_project(nc, g, ins, a, x_t, x0)
            rwkv_keys(nc, g, a, x0, x_t)
        rwkv_chunks(nc, g, a)
        rwkv_finish(nc, g, a)
        project_out(nc, g, "r", ins["rwkv_w_o"][0], None, a.r, None)


def rwkv_project(nc, g, ins, a, x_t, x0):
    ORDER = [1, 4, 5, 0, 3, 2]
    xj = [x0, a.kk]
    f = g.view
    with ExitStack() as mem:
        def sb(name, shape, dt=FP32):
            return mem.enter_context(nc.sbuf_tensor("rp_" + name, shape, dt))

        wt = sb("w", [P, 2, KT, 256])
        omm = sb("omm", [P, 48])
        w1 = {1: sb("w1", [P, KT, 64]), 4: sb("a1", [P, KT, 64]), 5: sb("g1", [P, KT, LORA_G])}
        w2 = {1: sb("w2", [64, D]), 4: sb("a2", [64, D])}
        g2 = [sb("g2a", [P, D]), sb("g2b", [LORA_G - P, D])]
        hid = {1: sb("hw", [64, S]), 4: sb("ha", [64, S])}
        hg = [sb("hga", [P, S]), sb("hgb", [LORA_G - P, S])]
        stage = sb("st", [P, 2, S])
        block = mem.enter_context(nc.Block())
        big = {0: ("rwkv_w_r", a.r), 3: ("rwkv_w_v", a.v), 2: ("rwkv_w_k", a.k)}
        chunks = [(j, c) for j in ORDER[3:] for c in range(4)]
        outs = [("h", 1, 0), ("h", 4, 0)] + [("z", 1, k) for k in range(KT)] + [("h", 5, 0), ("h", 5, 1)]
        outs += [("z", 4, k) for k in range(KT)] + [("p", 0, k) for k in range(KT)] + [("z", 5, k) for k in range(KT)]
        outs += [("p", 3, k) for k in range(KT)] + [("p", 2, k) for k in range(KT)]
        at = {o: n for n, o in enumerate(outs)}

        @block.sync
        def _(sp):
            sp.dma_start(g.x_dram, g.x[:]).then_inc(g.sig["x_saved"], 16)
            for j, n1, n2 in ((1, "rwkv_decay_w1", "rwkv_decay_w2"), (4, "rwkv_iclr_a1", "rwkv_iclr_a2")):
                sp.dma_start(w1[j][:], ins[n1][0].rearrange("(k p) n -> p k n", p=P)).then_inc(g.sig["lo_in"], 16)
                sp.dma_start(w2[j][:], ins[n2][0]).then_inc(g.sig["lo_in"], 16)
            sp.dma_start(w1[5][:], ins["rwkv_gate_g1"][0].rearrange("(k p) n -> p k n", p=P)).then_inc(g.sig["lo_in"], 16)
            sp.dma_start(g2[0][:], ins["rwkv_gate_g2"][0][0:P]).then_inc(g.sig["lo_in"], 16)
            sp.dma_start(g2[1][:], ins["rwkv_gate_g2"][0][P:LORA_G]).then_inc(g.sig["lo_in"], 16)
            for n, (j, c) in enumerate(chunks):
                if n >= 2:
                    last = at["p", chunks[n - 2][0], 2 * chunks[n - 2][1] + 1]
                    sp.wait_ge(g.sig["pj_mm"], last + 1)
                src = ins[big[j][0]][0].rearrange("(k p) (c n) -> c p k n", p=P, n=256)[c]
                sp.dma_start(wt[:, n % 2], src).then_inc(g.sig["wt_in"][n % 2], 16)

        @block.tensor
        def _(pe):
            pe.wait_ge(g.sig["lo_in"], 16 * 7)
            for n, (kind, j, k) in enumerate(outs):
                bank = g.ps[:, n % 8, :]
                if n >= 8:
                    pe.wait_ge(g.sig["pj_ev"], n - 7)
                if kind == "h":
                    src = xj[ORDER.index(j) % 2]
                    pe.wait_ge(g.sig["xj_mix"], KT * (ORDER.index(j) + 1))
                    m0, m1 = (k * P, min((k + 1) * P, w1[j].shape[2]))
                    for d in range(KT):
                        last = nc.tensor.matmul(bank[0:m1 - m0], w1[j][:, d, m0:m1], src[:, d, :], start=(d == 0), stop=(d == KT - 1))
                elif kind == "z" and j != 5:
                    pe.wait_ge(g.sig["pj_ev"], at["h", j, 0] + 1)
                    last = nc.tensor.matmul(bank, w2[j][:, k * P:(k + 1) * P], hid[j][:], start=True, stop=True)
                elif kind == "z":
                    pe.wait_ge(g.sig["pj_ev"], at["h", 5, 1] + 1)
                    for part in range(2):
                        last = nc.tensor.matmul(bank, g2[part][:, k * P:(k + 1) * P], hg[part][:], start=(part == 0), stop=(part == 1))
                else:
                    src = xj[ORDER.index(j) % 2]
                    c = chunks.index((j, k // 2))
                    pe.wait_ge(g.sig["xj_mix"], KT * (ORDER.index(j) + 1))
                    pe.wait_ge(g.sig["wt_in"][c % 2], 16 * (c // 2 + 1))
                    for d in range(KT):
                        last = nc.tensor.matmul(bank, wt[:, c % 2, d, (k % 2) * P:(k % 2 + 1) * P], src[:, d, :],
                                                start=(d == 0), stop=(d == KT - 1))
                last.then_inc(g.sig["pj_mm"], 1)

        def used(n):
            j = ORDER[n]
            return at[("h", j, 1 if j == 5 else 0) if n < 3 else ("p", j, KT - 1)] + 1

        @block.scalar
        def _(act):
            def scaled(n):
                act.wait_ge(g.sig["omm"], 1)
                if n >= 2:
                    act.wait_ge(g.sig["pj_mm"], used(n - 2))
                for k in range(KT):
                    c = 8 * ORDER[n] + k
                    nc.scalar.activation(xj[n % 2][:, k], x_t[:, k], ACT.Copy, scale=omm[:, c:c + 1]).then_inc(g.sig["xj_scaled"], 1)

            scaled(0)
            scaled(1)
            nth = 2
            for n, (kind, j, k) in enumerate(outs):
                if nth < 6 and used(nth - 2) <= n:
                    scaled(nth)
                    nth += 1
                act.wait_ge(g.sig["pj_mm"], n + 1)
                bank = g.ps[:, n % 8, :]
                if kind == "h" and j != 5:
                    ins_ = nc.scalar.activation(hid[j][:], bank[0:64], ACT.Tanh if j == 1 else ACT.Copy)
                elif kind == "h":
                    ins_ = nc.scalar.activation(hg[k][:], bank[0:P if k == 0 else LORA_G - P], ACT.Sigmoid)
                elif kind == "z" and j == 1:
                    ins_ = nc.scalar.activation(a.r[:, k], bank, ACT.Sigmoid, bias=g.vec[:, V_W0 + k:V_W0 + k + 1])
                elif kind == "z" and j == 4:
                    ins_ = nc.scalar.activation(a.b[:, k], bank, ACT.Sigmoid, bias=g.vec[:, V_A0 + k:V_A0 + k + 1])
                elif kind == "z":
                    if k >= 2:
                        act.wait_ge(g.sig["gate_out"][k % 2], 16 * (k // 2))
                    ins_ = nc.scalar.activation(stage[:, k % 2], bank, ACT.Copy)
                else:
                    if j == 0:
                        act.wait_ge(g.sig["scanned"], KT)
                    ins_ = nc.scalar.activation(big[j][1][:, k], bank, ACT.Copy)
                ins_.then_inc(g.sig["pj_ev"], 1)
                if kind == "z" and j == 5:
                    act.wait_ge(g.sig["pj_ev"], n + 1)
                    act.dma_start(g.gate_dram[k], stage[:, k % 2]).then_inc(g.sig["gate_out"][k % 2], 16)
            act.wait_ge(g.sig["gate_out"][0], 16 * 4)
            act.wait_ge(g.sig["gate_out"][1], 16 * 4)

        @block.vector
        def _(dve):
            nc.vector.tensor_scalar(omm[:], g.vec[:, V_MU:V_MU + 48], -1.0, 1.0, ALU.mult, ALU.add).then_inc(g.sig["omm"], 1)

            def mixed(n):
                for k in range(KT):
                    c = V_MU + 8 * ORDER[n] + k
                    dve.wait_ge(g.sig["xj_scaled"], KT * n + k + 1)
                    to = xj[n % 2][:, k, 1:S]
                    nc.vector.scalar_tensor_tensor(to, x_t[:, k, 0:S - 1], g.vec[:, c:c + 1], to, ALU.mult, ALU.add).then_inc(g.sig["xj_mix"], 1)

            for n in range(3):
                mixed(n)
            dve.wait_ge(g.sig["x_saved"], 16)
            for k in range(KT):
                dve.wait_ge(g.sig["pj_ev"], at["z", 1, k] + 1)
                nc.vector.tensor_tensor_scan(a.cs[:, k], f("scan"), a.r[:, k], 0.0, ALU.mult, ALU.add).then_inc(g.sig["scanned"], 1)
            for n in range(3, 6):
                mixed(n)


def rwkv_keys(nc, g, a, tmp, tmp2):
    f = g.view
    with ExitStack() as mem:
        def sb(name, shape, dt=FP32):
            return mem.enter_context(nc.sbuf_tensor("rk_" + name, shape, dt))

        omka = sb("omka", [P, KT])
        norm = sb("norm", [HEADS, 3, S])
        bon = sb("bon", [P, 2, S])
        block = mem.enter_context(nc.Block())

        @block.vector
        def _(dve):
            nc.vector.tensor_scalar(omka[:], g.vec[:, V_KA:V_KA + 8], -1.0, 1.0, ALU.mult, ALU.add).then_inc(g.sig["k_om"], 1)
            for k in range(KT):
                nc.vector.tensor_scalar(a.kk[:, k], a.k[:, k], g.vec[:, V_KK + k:V_KK + k + 1], None, ALU.mult).then_inc(g.sig["k_raw"], 1)
            dve.wait_ge(g.sig["k_norm"], 1)
            nc.vector.tensor_scalar(norm[:, 1], norm[:, 0], 1e-12, None, ALU.max).then_inc(g.sig["k_max"], 1)
            dve.wait_ge(g.sig["k_max"], 1)
            nc.vector.reciprocal(norm[:, 2], norm[:, 1]).then_inc(g.sig["k_inv"], 1)
            for k in range(KT):
                dve.wait_ge(g.sig["k_bc"], k + 1)
                nc.vector.tensor_tensor(a.kk[:, k], a.kk[:, k], g.ps[:, 1 + k % 3, :], ALU.mult).then_inc(g.sig["k_kk"], 1)
                dve.wait_ge(g.sig["k_new"], 2 * k + 2)
                dve.wait_ge(g.sig["k_kk"], k + 1)
                nc.vector.scalar_tensor_tensor(a.b[:, k], a.kk[:, k], -1.0, a.b[:, k], ALU.mult, ALU.mult).then_inc(g.sig["k_b"], 1)
                nc.vector.scalar_tensor_tensor(tmp2[:, k], a.r[:, k], g.vec[:, V_RK + k:V_RK + k + 1], a.k[:, k], ALU.mult,
                                               ALU.mult).then_inc(g.sig["k_rk"], 1)
            for k in range(KT):
                dve.wait_ge(g.sig["k_bon"], k + 1)
                if k >= 2:
                    dve.wait_ge(g.sig["bon_out"][k % 2], 16 * (k // 2))
                nc.vector.tensor_tensor(bon[:, k % 2], a.v[:, k], g.ps[:, 4 + k % 4, :], ALU.mult).then_inc(g.sig["k_bv"], 1)

        @block.gpsimd
        def _(pool):
            pool.wait_ge(g.sig["k_om"], 1)
            pool.wait_ge(g.sig["k_raw"], KT)
            for k in range(KT):
                pool.wait_ge(g.sig["k_sqmm"], 1)
                nc.gpsimd.tensor_scalar(tmp[:, k], a.b[:, k], g.vec[:, V_KA + k:V_KA + k + 1], omka[:, k:k + 1],
                                        ALU.mult, ALU.add).then_inc(g.sig["k_new"], 1)
                pool.wait_ge(g.sig["k_new"], 2 * k + 1)
                nc.gpsimd.tensor_tensor(a.k[:, k], a.k[:, k], tmp[:, k], ALU.mult).then_inc(g.sig["k_new"], 1)

        @block.scalar
        def _(act):
            for k in range(KT):
                act.wait_ge(g.sig["k_raw"], k + 1)
                nc.scalar.activation(tmp[:, k], a.kk[:, k], ACT.Square).then_inc(g.sig["k_sq"], 1)
            act.wait_ge(g.sig["k_sqmm"], 1)
            nc.scalar.activation(norm[:, 0], g.ps[0:HEADS, 0, :], ACT.Sqrt).then_inc(g.sig["k_norm"], 1)

        @block.tensor
        def _(pe):
            for k in range(KT):
                pe.wait_ge(g.sig["k_sq"], k + 1)
                last = nc.tensor.matmul(g.ps[0:HEADS, 0, :], f("sel")[:, k * HEADS:(k + 1) * HEADS], tmp[:, k],
                                        start=(k == 0), stop=(k == KT - 1))
            last.then_inc(g.sig["k_sqmm"], 1)
            pe.wait_ge(g.sig["k_inv"], 1)
            for k in range(KT):
                if k >= 3:
                    pe.wait_ge(g.sig["k_kk"], k - 2)
                nc.tensor.matmul(g.ps[:, 1 + k % 3, :], f("selt")[0:HEADS, k * P:(k + 1) * P], norm[:, 2],
                                 start=True, stop=True).then_inc(g.sig["k_bc"], 1)
            for k in range(KT):
                pe.wait_ge(g.sig["k_rk"], k + 1)
                if k >= 4:
                    pe.wait_ge(g.sig["k_bv"], k - 3)
                nc.tensor.matmul(g.ps[:, 4 + k % 4, :], f("blk"), tmp2[:, k], start=True, stop=True).then_inc(g.sig["k_bon"], 1)

        @block.sync
        def _(sp):
            for k in range(KT):
                sp.wait_ge(g.sig["k_bv"], k + 1)
                sp.dma_start(g.bonus_dram[k], bon[:, k % 2]).then_inc(g.sig["bon_out"][k % 2], 16)
            sp.wait_ge(g.sig["bon_out"][0], 64)
            sp.wait_ge(g.sig["bon_out"][1], 64)


LEVELS = (2, 4, 8, 16, 32)
CHUNK_STEPS = [("At", "act"), ("Bt", "act"), ("Kt", "act"), ("Vt", "act"), ("MT", "act"), ("M", "dve"), ("NT", "dve"),
               ("RBT", "dve"), ("RKT", "dve")]
for _n in LEVELS:
    CHUNK_STEPS += [(f"Y{_n}", "act")] + ([(f"Z{_n}", "dve")] if _n < 32 else []) + [(f"ZT{_n}", "dve")]
CHUNK_STEPS += [("NV", "act"), ("Vh", "act"), ("Ah", "act")]
STEP_AT = {name: n for n, (name, _) in enumerate(CHUNK_STEPS)}


def steps_of(who, upto):
    return sum(w == who for _, w in CHUNK_STEPS[:STEP_AT[upto] + 1])


def rwkv_chunks(nc, g, a):
    f = g.view
    N_ACT = sum(w == "act" for _, w in CHUNK_STEPS)
    N_DVE = sum(w == "dve" for _, w in CHUNK_STEPS)
    N = len(CHUNK_STEPS)
    with ExitStack() as mem:
        def sb(name, shape, dt=FP32):
            return mem.enter_context(nc.sbuf_tensor("rc_" + name, shape, dt))

        e_s = sb("e", [P, 2 * KT, CH + 1])
        A, B, K, R = (sb(n, [P, KT, P]) for n in "ABKR")
        tA, tB, tK, tV = (sb("t" + n, [P, 2 * KT, CH]) for n in "ABKV")
        MT, T, TT_, F, Y, NT, RBT, RKT, U, Ah = (sb(n, [P, 2, KT, CH]) for n in
                                                 ("MT", "T", "TT", "F", "Y", "NT", "RBT", "RKT", "U", "Ah"))
        state = sb("S", [P, KT, CH])
        ysb = sb("y", [P, KT, CH])
        V, e_i = (m[:].rearrange("p a k c -> p (a k c)").rearrange("p (k s) -> p k s", s=P) for m in (F, Y))
        NV, Vh = A[:].rearrange("p k s -> p (k s)").rearrange("p (a k c) -> p a k c", a=2, c=CH), MT
        block = mem.enter_context(nc.Block())

        def pair(ap, i):
            return ap[:, :, bass.ds(i * P, P)]

        def rows(c):
            return slice(CH * c, CH * c + CH)

        def all16(ap):
            return ap[:].rearrange("p a k c -> p (a k) c")

        def two_banks(step):
            b = 2 * (STEP_AT[step] % 4)
            return g.ps[:, b:b + 2, :].rearrange("p a (k c) -> p a k c", c=CH)

        def after(eng, i, step):
            who = CHUNK_STEPS[STEP_AT[step]][1]
            sem, n = (g.sig["c_act"], N_ACT) if who == "act" else (g.sig["c_dve"], N_DVE)
            eng.wait_ge(sem, 2 * (i * n + steps_of(who, step)))

        @block.tensor
        def _(pe):
            pe.wait_ge(g.sig["c_state"], 1)
            held = Held(pe, g.sig["c_held"])

            def begin(i, step, *read):
                n = STEP_AT[step]
                wanted = [*read] + ([CHUNK_STEPS[n - 4][0]] if n >= 4 else [])
                for who in ("act", "dve"):
                    its = [w for w in wanted if CHUNK_STEPS[STEP_AT[w]][1] == who]
                    if its:
                        after(pe, i, max(its, key=STEP_AT.get))
                held()

            def turned(i, step, src, ready):
                begin(i, step)
                pe.wait_ge(g.c_stage[ready], i + 1)
                bank = g.ps[:, 2 * (STEP_AT[step] % 4):2 * (STEP_AT[step] % 4) + 2, :]
                for k in range(KT):
                    last = nc.tensor.transpose(bank[:, k // 4, (k % 4) * P:(k % 4 + 1) * P], src[:, k, :], f("ident"))
                    if k % 4 == 3:
                        last.then_inc(g.sig["c_mm"], 1)

            def from_features(i, step, lhs, rhs):
                begin(i, step)
                out = two_banks(step)
                for par in range(2):
                    q = rows(par)
                    for c in range(2):
                        for k in range(KT):
                            last = nc.tensor.matmul(out[rows(c), par, k], lhs[q, k, rows(c)], rhs[q, k, rows(c)], start=True, stop=True)
                    last.then_inc(g.sig["c_mm"], 1)

            def from_tokens(i, step, lhs, rhs, *read):
                begin(i, step, *read)
                out = two_banks(step)
                for c in range(2):
                    for par in range(2):
                        for k in range(KT):
                            last = nc.tensor.matmul(out[rows(c), par, k], lhs(rows(c), par, k), rhs(rows(c), par, k), start=True, stop=True)
                        if c == 1:
                            last.then_inc(g.sig["c_mm"], 1)

            def of(m):
                return lambda q, par, k: m[q, par, k]

            def tok(m):
                return lambda q, par, k: m[q, 2 * k + par]

            with pe.Fori(0, 4) as i:
                turned(i, "At", A, "A")
                turned(i, "Bt", B, "B")
                turned(i, "Kt", K, "K")
                turned(i, "Vt", V, "V")
                from_features(i, "MT", B, A)
                from_features(i, "M", A, B)
                from_features(i, "NT", K, A)
                pe.wait_ge(g.c_stage["R"], i + 1)
                from_features(i, "RBT", B, R)
                from_features(i, "RKT", K, R)
                for n in LEVELS:
                    pe.wait_ge(g.sig["c_f"], 5 * i + LEVELS.index(n) + 1)
                    if n == 2:
                        pe.wait_ge(g.sig["c_t0"], i + 1)
                    half = [] if n == 2 else [f"Z{n // 2}"]
                    from_tokens(i, f"Y{n}", of(F), of(T), *half)
                    half = [] if n == 2 else [f"ZT{n // 2}"]
                    if n < 32:
                        from_tokens(i, f"Z{n}", of(TT_), of(Y), f"Y{n}", *half)
                    from_tokens(i, f"ZT{n}", of(Y), of(TT_), f"Y{n}", *half)
                from_tokens(i, "NV", of(NT), tok(tV), "NT", "Vt")
                from_tokens(i, "Vh", of(TT_), of(NV), "ZT32", "NV")
                begin(i, "Ah", "At", "ZT32")
                out = two_banks("Ah")
                for c in range(2):
                    for par in range(2):
                        for k in range(KT):
                            last = nc.tensor.matmul(out[rows(par), c, k], tA[rows(c), 2 * k + par], TT_[rows(c), par, k], start=True, stop=True)
                    last.then_inc(g.sig["c_mm"], 1)
                after(pe, i, "RKT")
                after(pe, i, "Ah")
                for c in range(2):
                    t = 2 * i + c
                    if c == 1:
                        pe.wait_ge(g.sig["c_st2"], t + 0)
                    held()
                    for par in range(2):
                        for k in range(KT):
                            last = nc.tensor.matmul(g.ps[rows(c), par, k * CH:(k + 1) * CH], Ah[rows(par), c, k], state[rows(par), k],
                                                    start=True, stop=True)
                    last.then_inc(g.sig["c_u"], 1)
                    if c == 1:
                        pe.wait_ge(g.sig["c_ys2"], 2 * t)
                    held()
                    for par in range(2):
                        for k in range(KT):
                            last = nc.tensor.matmul(g.ps[rows(par), 2 + par, k * CH:(k + 1) * CH], state[rows(par), k],
                                                    R[rows(par), k, rows(c)], start=True, stop=True)
                        last.then_inc(g.sig["c_ys"], 1)
                    pe.wait_ge(g.sig["c_u2"], 2 * t + 2)
                    held()
                    for par in range(2):
                        for k in range(KT):
                            o = g.ps[rows(par), 4, k * CH:(k + 1) * CH]
                            nc.tensor.matmul(o, tB[rows(c), 2 * k + par], U[rows(c), par, k], start=True, stop=False)
                            last = nc.tensor.matmul(o, tK[rows(c), 2 * k + par], tV[rows(c), 2 * k + par], start=False, stop=True)
                    last.then_inc(g.sig["c_su"], 1)
                    if c == 1:
                        pe.wait_ge(g.sig["c_y"], t)
                    held()
                    for par in range(2):
                        for k in range(KT):
                            o = g.ps[rows(par), 5, k * CH:(k + 1) * CH]
                            nc.tensor.matmul(o, U[rows(c), par, k], RBT[rows(c), par, k], start=True, stop=False)
                            last = nc.tensor.matmul(o, tV[rows(c), 2 * k + par], RKT[rows(c), par, k], start=False, stop=True)
                    last.then_inc(g.sig["c_yu"], 1)
                pe.wait_ge(g.sig["c_y"], 2 * i + 2)
                held()

        @block.scalar
        def _(act):
            def copy(i, step, dst):
                for half in range(2):
                    act.wait_ge(g.sig["c_mm"], 2 * (i * N + STEP_AT[step]) + half + 1)
                    b = 2 * (STEP_AT[step] % 4) + half
                    nc.scalar.activation(dst(half), g.ps[:, b, :].rearrange("p (k c) -> p k c", c=CH), ACT.Copy).then_inc(g.sig["c_act"], 1)

            def of(m):
                return lambda half: m[:, half]

            def tok(m):
                return lambda half: m[:, 8 * half:8 * half + 8]

            with act.Fori(0, 4) as i:
                cs = pair(a.cs, i)
                nc.scalar.activation(e_s[:, :, 1:].rearrange("p (k c) s -> p k c s", c=2),
                                     cs.rearrange("p k (c s) -> p k c s", c=2), ACT.Exp, scale=-DECAY).then_inc(g.sig["c_exp"], 1)
                nc.scalar.activation(e_i, cs, ACT.Exp, scale=DECAY).then_inc(g.sig["c_exp"], 1)
                nc.scalar.activation(V, pair(a.v, i), ACT.Copy).then_inc(g.c_stage["V"], 1)
                for step, dst in (("At", tok(tA)), ("Bt", tok(tB)), ("Kt", tok(tK)), ("Vt", tok(tV)), ("MT", of(MT))):
                    copy(i, step, dst)
                for n in LEVELS:
                    copy(i, f"Y{n}", of(Y))
                copy(i, "NV", of(NV))
                copy(i, "Vh", of(Vh))
                copy(i, "Ah", of(Ah))
                for c in range(2):
                    t = 2 * i + c
                    if c == 1:
                        act.wait_ge(g.sig["c_y"], t)
                    for par in range(2):
                        act.wait_ge(g.sig["c_ys"], 2 * t + par + 1)
                        nc.scalar.activation(ysb[rows(par)], g.ps[rows(par), 2 + par, :].rearrange("p (k c) -> p k c", c=CH),
                                             ACT.Copy).then_inc(g.sig["c_ys2"], 1)
                act.wait_ge(g.sig["c_y"], 2 * i + 2)

        @block.gpsimd
        def _(pool):
            nc.gpsimd.memset(state[:], 0.0).then_inc(g.sig["c_zero"], 1)
            nc.gpsimd.memset(e_s[:, :, 0:1], 1.0).then_inc(g.sig["c_zero"], 1)
            pool.wait_ge(g.sig["c_zero"], 2)
            pool.nop().then_inc(g.sig["c_state"], 1)
            link_n = 1
            with pool.Fori(0, 4) as i:
                pool.wait_ge(g.sig["c_exp"], 2 * i + 1)
                nc.gpsimd.tensor_tensor(R[:].rearrange("p k (c s) -> p k c s", c=2), pair(a.r, i).rearrange("p k (c s) -> p k c s", c=2),
                                        e_s[:, :, 1:].rearrange("p (k c) s -> p k c s", c=2), ALU.mult).then_inc(g.c_stage["R"], 1)
                for n in LEVELS:
                    after(pool, i, "MT")
                    if n == 2:
                        after(pool, i, "Vt")
                    else:
                        after(pool, i, f"Y{n // 2}")
                    nc.gpsimd.tensor_tensor(all16(F), all16(MT), f(f"lev{n}").unsqueeze(1).to_broadcast([P, 2 * KT, CH]),
                                            ALU.mult).then_inc(g.sig["c_f"], 1)
                pool.wait_ge(g.sig["c_y"], 2 * i + 2)

        @block.vector
        def _(dve):
            with dve.Fori(0, 4) as i:
                def quad(ap):
                    return ap.rearrange("p k (c s) -> p k c s", c=2)

                before = e_s[:, :, 0:CH].rearrange("p (k c) s -> p k c s", c=2)
                dve.wait_ge(g.sig["c_state"], 1)
                dve.wait_ge(g.sig["c_exp"], 2 * i + 1)
                nc.vector.tensor_tensor(quad(A[:]), quad(pair(a.kk, i)), before, ALU.mult).then_inc(g.c_stage["A"], 1)
                dve.wait_ge(g.sig["c_exp"], 2 * i + 2)
                nc.vector.tensor_tensor(B[:], pair(a.b, i), e_i, ALU.mult).then_inc(g.c_stage["B"], 1)
                nc.vector.tensor_tensor(K[:], pair(a.k, i), e_i, ALU.mult).then_inc(g.c_stage["K"], 1)
                after(dve, i, "MT")
                lev1, eye = (f(n).unsqueeze(1).to_broadcast([P, 2 * KT, CH]) for n in ("lev1", "eye64"))
                nc.vector.tensor_tensor(all16(TT_), all16(MT), lev1, ALU.mult).then_inc(g.sig["c_l"], 1)
                dve.wait_ge(g.sig["c_l"], 3 * i + 1)
                nc.vector.tensor_tensor(all16(TT_), all16(TT_), eye, ALU.add).then_inc(g.sig["c_l"], 1)

                def masked(step, dst, mask):
                    for half in range(2):
                        dve.wait_ge(g.sig["c_mm"], 2 * (i * N + STEP_AT[step]) + half + 1)
                        b = 2 * (STEP_AT[step] % 4) + half
                        nc.vector.tensor_tensor(dst[:, half], g.ps[:, b, :].rearrange("p (k c) -> p k c", c=CH),
                                                f(mask).unsqueeze(1).to_broadcast([P, KT, CH]), ALU.mult).then_inc(g.sig["c_dve"], 1)

                masked("M", T, "lev1t")
                dve.wait_ge(g.sig["c_l"], 3 * i + 2)
                after(dve, i, "M")
                nc.vector.tensor_tensor(all16(T), all16(T), eye, ALU.add).then_inc(g.sig["c_l"], 1)
                dve.wait_ge(g.sig["c_l"], 3 * i + 3)
                nc.vector.nop().then_inc(g.sig["c_t0"], 1)
                masked("NT", NT, "strict")
                masked("RBT", RBT, "incl")
                masked("RKT", RKT, "incl")
                for n in LEVELS:
                    for step, dst in ((f"Z{n}", T), (f"ZT{n}", TT_)):
                        if step not in STEP_AT:
                            continue
                        for half in range(2):
                            dve.wait_ge(g.sig["c_mm"], 2 * (i * N + STEP_AT[step]) + half + 1)
                            b = 2 * (STEP_AT[step] % 4) + half
                            nc.vector.tensor_tensor(dst[:, half], g.ps[:, b, :].rearrange("p (k c) -> p k c", c=CH), dst[:, half],
                                                    ALU.add).then_inc(g.sig["c_dve"], 1)
                after(dve, i, "Vh")
                for c in range(2):
                    t = 2 * i + c
                    dve.wait_ge(g.sig["c_u"], t + 1)
                    for par in range(2):
                        nc.vector.tensor_tensor(U[rows(c), par], g.ps[rows(c), par, :].rearrange("p (k c) -> p k c", c=CH),
                                                Vh[rows(c), par], ALU.add).then_inc(g.sig["c_u2"], 1)
                    dve.wait_ge(g.sig["c_su"], t + 1)
                    nc.vector.tensor_tensor(state[:], g.ps[:, 4, :].rearrange("p (k c) -> p k c", c=CH), state[:], ALU.add).then_inc(g.sig["c_st1"], 1)
                    dve.wait_ge(g.sig["c_st1"], t + 1)
                    end = e_s[:, c:2 * KT:2, CH:CH + 1].to_broadcast([P, KT, CH])
                    nc.vector.tensor_tensor(state[:], state[:], end, ALU.mult).then_inc(g.sig["c_st2"], 1)
                    dve.wait_ge(g.sig["c_yu"], t + 1)
                    dve.wait_ge(g.sig["c_ys2"], 2 * t + 2)
                    nc.vector.tensor_tensor(a.r[:, :, bass.ds(i * P + c * CH, CH)], g.ps[:, 5, :].rearrange("p (k c) -> p k c", c=CH),
                                            ysb[:], ALU.add).then_inc(g.sig["c_y"], 1)


def rwkv_finish(nc, g, a):
    f = g.view
    with ExitStack() as mem:
        def sb(name, shape, dt=FP32):
            return mem.enter_context(nc.sbuf_tensor("rf_" + name, shape, dt))

        sq = sb("sq", [P, 2, S])
        norm = sb("norm", [HEADS, 3, S])
        block = mem.enter_context(nc.Block())
        y, gate, bonus = a.r, a.k, a.v

        @block.sync
        def _(sp):
            sp.dma_start(gate[:], g.gate_dram.rearrange("k p s -> p k s")).then_inc(g.sig["f_gate"], 16)
            sp.dma_start(bonus[:], g.bonus_dram.rearrange("k p s -> p k s")).then_inc(g.sig["f_bonus"], 16)
            sp.dma_start(g.x[:], g.x_dram).then_inc(g.sig["x_back"], 16)
            sp.wait_ge(g.sig["x_back"], 16)

        @block.tensor
        def _(pe):
            for k in range(KT):
                if k >= 3:
                    pe.wait_ge(g.sig["f_c"], k - 2)
                nc.tensor.matmul(g.ps[:, 1 + k % 3, :], f("blkmean"), y[:, k], start=True, stop=True).then_inc(g.sig["f_mean"], 1)
            for k in range(KT):
                pe.wait_ge(g.sig["f_sq"], k + 1)
                last = nc.tensor.matmul(g.ps[0:HEADS, 0, :], f("sel")[:, k * HEADS:(k + 1) * HEADS], sq[:, k % 2],
                                        start=(k == 0), stop=(k == KT - 1))
                last.then_inc(g.sig["f_var"], 1)
            pe.wait_ge(g.sig["f_inv"], 1)
            for k in range(KT):
                if k >= 4:
                    pe.wait_ge(g.sig["f_n"], k - 3)
                nc.tensor.matmul(g.ps[:, 4 + k % 4, :], f("selt")[0:HEADS, k * P:(k + 1) * P], norm[:, 2],
                                 start=True, stop=True).then_inc(g.sig["f_bc"], 1)

        @block.scalar
        def _(act):
            for k in range(KT):
                act.wait_ge(g.sig["f_c"], k + 1)
                if k >= 2:
                    act.wait_ge(g.sig["f_var"], k - 1)
                nc.scalar.activation(sq[:, k % 2], y[:, k], ACT.Square).then_inc(g.sig["f_sq"], 1)
            act.wait_ge(g.sig["f_ms"], 1)
            nc.scalar.activation(norm[:, 1], norm[:, 0], ACT.Sqrt).then_inc(g.sig["f_std"], 1)
            for k in range(KT):
                act.wait_ge(g.sig["f_n"], k + 1)
                nc.scalar.activation(y[:, k], y[:, k], ACT.Identity, bias=g.vec[:, V_LNB + k:V_LNB + k + 1],
                                     scale=g.vec[:, V_LNW + k:V_LNW + k + 1]).then_inc(g.sig["f_ln"], 1)

        @block.vector
        def _(dve):
            for k in range(KT):
                dve.wait_ge(g.sig["f_mean"], k + 1)
                nc.vector.tensor_tensor(y[:, k], y[:, k], g.ps[:, 1 + k % 3, :], ALU.subtract).then_inc(g.sig["f_c"], 1)
            dve.wait_ge(g.sig["f_var"], KT)
            nc.vector.tensor_scalar(norm[:, 0], g.ps[0:HEADS, 0, :], 1.0 / CH, 64e-5, ALU.mult, ALU.add).then_inc(g.sig["f_ms"], 1)
            dve.wait_ge(g.sig["f_std"], 1)
            nc.vector.reciprocal(norm[:, 2], norm[:, 1]).then_inc(g.sig["f_inv"], 1)
            for k in range(KT):
                dve.wait_ge(g.sig["f_bc"], k + 1)
                nc.vector.tensor_tensor(y[:, k], y[:, k], g.ps[:, 4 + k % 4, :], ALU.mult).then_inc(g.sig["f_n"], 1)
            dve.wait_ge(g.sig["f_gate"], 16)
            for k in range(KT):
                dve.wait_ge(g.sig["f_b"], k + 1)
                nc.vector.tensor_tensor(y[:, k], y[:, k], gate[:, k], ALU.mult).then_inc(g.sig["f_y"], 1)

        @block.gpsimd
        def _(pool):
            pool.wait_ge(g.sig["f_bonus"], 16)
            for k in range(KT):
                pool.wait_ge(g.sig["f_ln"], k + 1)
                nc.gpsimd.tensor_tensor(y[:, k], y[:, k], bonus[:, k], ALU.add).then_inc(g.sig["f_b"], 1)


@contextmanager
def signals(nc, tag, names, groups=()):
    made = []

    def new(name):
        made.append(nc.alloc_semaphore(name=tag + name))
        return made[-1]

    yield {**{name: new(name) for name in names}, **{name: [new(f"{name}{b}") for b in range(n)] for name, n in groups}}
    with nc.Block() as block:
        @block.gpsimd
        def _(pool):
            for s in made:
                pool.sem_clear(s)
    for s in made:
        nc.release_semaphore(s)


ATTENTION_SIGNALS = (
    "const_in", "vec_in", "vec_t", "vec_ready", "const_b",
    "hn_small", "hn_pe", "hn_w", "hn_sum", "hn_sq", "hn_ms", "hn_rms", "hn_gz", "hn_exp",
    "hn_kt", "hn_kev", "hn_hid", "hn_hs", "hn_gu", "hn_th", "hn_cmp", "hn_kc", "hn_kms", "hn_krm",
    "hn_kct", "hn_kct2", "hn_link", "hn_kst", "hn_pet", "hn_raw", "hn_blk", "hn_gel", "hn_kn",
    "att_link", "sn_sq", "sn_ms", "sn_rms", "sn_link", "po_tr", "po_mm", "po_done")
MOE_SIGNALS = ("gain_in", "r_in", "r_both", "r_sub", "r_exp", "r_lg", "r_rank", "r_fill", "r_slot",
               "r_link", "xs_out", "y_add", "out_done")
RWKV_SIGNALS = (
    "po_tr", "po_mm", "po_done", "x_saved", "lo_in", "pj_mm", "pj_ev", "xj_mix", "xj_scaled", "omm", "scanned",
    "k_om", "k_raw", "k_norm", "k_max", "k_inv", "k_bc", "k_kk", "k_new", "k_b", "k_rk", "k_bon", "k_bv", "k_sqmm", "k_sq",
    "c_mm", "c_act", "c_dve", "c_state", "c_zero", "c_exp", "c_f", "c_t0", "c_l", "c_u", "c_u2", "c_ys", "c_ys2", "c_su",
    "c_yu", "c_y", "c_st1", "c_st2", "c_held", "f_gate", "f_bonus", "x_back", "f_c", "f_mean", "f_sq", "f_var", "f_inv", "f_n",
    "f_bc", "f_ms", "f_std", "f_ln", "f_b", "f_y")
RWKV_GROUPS = (("po_in", 2), ("po_ev", 2), ("wt_in", 2), ("gate_out", 2), ("bon_out", 2), ("c_staged", 5))
EXPERT_SIGNALS = ("held", "up", "hid", "silu", "half", "turn", "zero")
EXPERT_GROUPS = (("down", 4), ("ids", 4), ("y", 4), ("y_free", 4), ("xt", 2))


def build(nc, ins, out):
    _, where = const_table()
    g = Shared()
    g.norms = 0
    with ExitStack() as mem:
        def sb(name, shape, dt=FP32):
            return mem.enter_context(nc.sbuf_tensor(name, shape, dt))

        g.const = sb("const", [P, max(b for _, b in where.values())])
        g.view = lambda name: g.const[:, where[name][0]:where[name][1]]
        g.identb, g.negb, g.cnegb = sb("identb", [P, P], BF16), sb("negb", [P, P], BF16), sb("cnegb", [P, TT * NCMP], BF16)
        g.x = sb("x", [P, TT, D])
        g.vec = sb("vec", [P, V_ROWS])
        g.subg = sb("subg", [P, 2])
        g.ps = mem.enter_context(nc.psum_tensor("ps", [P, 8, S], FP32))
        g.xs_dram = [nc.dram_tensor(f"xs_dram{L}", (2 * S, D), FP32, kind="Internal").ap() for L in range(2)]
        g.y_dram = [nc.dram_tensor(f"y_dram{L}", (2 * S, D), FP32, kind="Internal").ap() for L in range(2)]
        g.table = [nc.dram_tensor(f"table{L}", (ROUNDS * NE * CAP, 1), I32, kind="Internal").ap() for L in range(2)]
        g.x_dram = nc.dram_tensor("x_dram", (P, TT, D), FP32, kind="Internal").ap()
        g.gate_dram = nc.dram_tensor("gate_dram", (KT, P, S), FP32, kind="Internal").ap()
        g.bonus_dram = nc.dram_tensor("bonus_dram", (KT, P, S), FP32, kind="Internal").ap()
        g.x_in, g.n_sum, g.n_ms, g.n_rms, g.n_rs, g.n_xs, g.n_tr, g.n_ev = (
            mem.enter_context(nc.semaphore(name)) for name in ("x_in", "n_sum", "n_ms", "n_rms", "n_rs", "n_xs", "n_tr", "n_ev"))
        g.table_sems = [[mem.enter_context(nc.semaphore(f"{name}{L}")) for name in ("idx_in", "r_tab")] for L in range(2)]
        g.row_sems, g.scat_sems = (
            [[[mem.enter_context(nc.semaphore(f"{name}{L}{more}{b}")) for b in range(4)] for more in range(2)] for L in range(2)]
            for name in ("rows", "scat"))
        attention_layer(nc, g, ins)
        moe_layer(nc, g, 0, ins)
        rwkv_layer(nc, g, ins)
        moe_layer(nc, g, 1, ins, out)


def attention_layer(nc, g, ins):
    groups = [("win_in", 2), ("win_done", 2), ("win_free", 2), ("po_in", 2), ("po_ev", 2), ("da", 12), ("na", 12)]
    with signals(nc, "att_", ATTENTION_SIGNALS, groups) as g.sig, ExitStack() as layer:
        g.da, g.na = ((*s[:4], (s[4], s[5]), *s[6:]) for s in (g.sig["da"], g.sig["na"]))
        g.att_base = [0]
        setup(nc, g, ins)

        def lb(name, shape, dt=FP32):
            return layer.enter_context(nc.sbuf_tensor(name, shape, dt))

        ocat = lb("ocat", [P, TT, D])
        with ExitStack() as att:
            def ab(name, shape, dt=FP32):
                return att.enter_context(nc.sbuf_tensor(name, shape, dt))

            h = ab("h", [P, TT, IN_COLS])
            with nc.sbuf_tensor("xs0", [P, TT, D], FP32) as xs, nc.sbuf_tensor("xt0", [P, KT, S], FP32) as x_t:
                normalise(nc, g, xs, x_t, g.vec[:, V_MIX0:V_MIX0 + 8], False)
                project_in(nc, g, ins["attn_w_in"][0], x_t, h)
            kt_sel, kt_win, kc_t = ab("kt_sel", [P, S]), ab("kt_win", [P, S]), ab("kc_t", [P, NCMP])
            vc = ab("vc", [NCMP, 2, 64])
            rs, gates, lamv, qg = ab("rs", [P, TT, 52]), ab("gates", [P, TT, 24]), ab("lamv", [P, 4]), ab("qg", [P, 2])
            head_norms(nc, g, h, ins, kt_sel, kt_win, kc_t, vc, rs, gates, lamv, qg)
            diff_attention(nc, g, h, ocat, rs, qg, lamv)
            nsa_attention(nc, g, h, ocat, rs, qg, gates, kt_sel, kt_win, kc_t, vc)
        sub_norm(nc, g, ocat)
        o_t = lb("o_t", [P, KT, S])
        scales = [g.subg[:, 0:1]] * 4 + [g.subg[:, 1:2]] * 4
        project_out(nc, g, "a", ins["attn_w_out"][0], ocat, o_t, scales)


def moe_layer(nc, g, L, ins, out=None):
    g.idx_in, g.r_tab = g.table_sems[L]
    with signals(nc, f"moe{L}_", MOE_SIGNALS, [("w_in", 4), ("y_in", TT)]) as g.sig:
        g.ex = []
        with ExitStack() as experts_signals:
            for more in range(2):
                s = experts_signals.enter_context(signals(nc, f"moe{L}_{more}_", EXPERT_SIGNALS, EXPERT_GROUPS + (() if not more else (("w", 4),))))
                s["rows"], s["scat"] = g.row_sems[L][more], g.scat_sems[L][more]
                if not more:
                    s["w"] = g.sig["w_in"]
                g.ex.append(s)
            moe(nc, g, L, ins, out)


INPUTS = ["x", "mix_norm", "attn_w_in", "attn_gate_bias", "diff_q_norm", "diff_k_norm", "diff_lambda", "diff_subln",
          "nsa_q_norm", "nsa_k_norm", "nsa_cmp_pe", "nsa_cmp_w1", "nsa_cmp_w2", "attn_w_out", "rwkv_mix", "rwkv_w_r",
          "rwkv_w_k", "rwkv_w_v", "rwkv_decay_w0", "rwkv_decay_w1", "rwkv_decay_w2", "rwkv_iclr_a0", "rwkv_iclr_a1",
          "rwkv_iclr_a2", "rwkv_gate_g1", "rwkv_gate_g2", "rwkv_k_k", "rwkv_k_a", "rwkv_r_k", "rwkv_ln_w", "rwkv_ln_b",
          "rwkv_w_o", "ffn_norm", "router_group_w", "router_group_b", "router_expert_w", "router_expert_b",
          "expert_w_gate", "expert_w_up", "expert_w_down"]


def kernel(**inputs):
    import concourse.bacc as bacc
    from concourse.bass_utils import run_bass_kernel_spmd

    nc = bacc.Bacc("TRN2", target_bir_lowering=False, num_devices=1)
    arrays, ins = {}, {}
    for name in INPUTS:
        a = np.ascontiguousarray(inputs[name])
        arrays[f"in_{name}"] = a
        ins[name] = nc.dram_tensor(f"in_{name}", a.shape, FP32, kind="ExternalInput").ap()
    arrays["in_const"] = const_table()[0]
    ins["const"] = nc.dram_tensor("in_const", arrays["in_const"].shape, FP32, kind="ExternalInput").ap()
    out = nc.dram_tensor("out", (1, S, D), FP32, kind="ExternalOutput").ap()
    build(nc, ins, out)
    result = run_bass_kernel_spmd(nc, [arrays], core_ids=[0])
    return result.results[0]["out"]
```

```python
import numpy as np
from contextlib import ExitStack, contextmanager

import concourse.bass as bass
from concourse import mybir

FP32 = mybir.dt.float32
BF16 = mybir.dt.bfloat16
I32 = mybir.dt.int32
U32 = mybir.dt.uint32
ALU = mybir.AluOpType
ACT = mybir.ActivationFunctionType
AX = mybir.AxisListType

P = 128
S = 512
D = 1024
TT = S // P
KT = D // P
EPS = 1e-6
BIG = 1e30

DQ0, DK0, DV0, NQ0, KV0, GT0, IN_COLS = 0, 512, 1024, 1536, 2048, 2816, 2840
IN_CHUNK = IN_COLS // 8
NCMP = 31
LAMBDA_INIT = 0.8 - 0.6

NE, NG, EPG, DE = 32, 4, 8, 256
CAP = 96
ROUNDS = -(-S // CAP)
LORA_G = 160
HEADS = 16
CH = 64
DECAY = float(np.exp(-0.5))

V_MIX0, V_MIX1, V_MU, V_W0, V_A0, V_KK, V_KA, V_RK, V_LNW, V_LNB = 0, 8, 16, 64, 72, 80, 88, 96, 104, 112
V_DQ, V_DK, V_NQ, V_NK0, V_NK1, V_NK2, V_SUB, V_ROWS = 120, 121, 122, 123, 124, 125, 126, 127


class Link:

    def __init__(self, eng, sem, base=0):
        self.eng, self.sem, self.base, self.n = eng, sem, base, 0

    def __call__(self, ins):
        self.n += 1
        ins.then_inc(self.sem, 1)
        self.eng.wait_ge(self.sem, self.base + self.n)


class Held:

    def __init__(self, eng, sem):
        self.eng, self.sem = eng, sem

    def __call__(self):
        self.eng.sem_inc(self.sem, 1)


class Shared:
    pass


def const_table():
    p, t = np.arange(P)[:, None], np.arange(P)[None, :]
    parts = {"ident": (p == t), "neg": np.where(t > p, -BIG, 0.0)}
    c = np.arange(NCMP)[None, None, :]
    pos = (np.arange(TT)[None, :, None] * P + np.arange(P)[:, None, None])
    ok = (16 * c + 31 <= pos)
    parts["cneg"] = np.where(ok, 0.0, -BIG).reshape(P, -1)
    parts["cok"] = ok.reshape(P, -1)
    parts["upper"] = (p < t)
    parts["ones"] = np.ones((P, P))
    parts["iota4"] = np.broadcast_to(np.arange(NG), (P, NG))
    parts["iota32"] = np.broadcast_to(np.arange(NE), (P, NE))
    parts["pair"] = (np.arange(2)[None, :, None] * S + np.arange(TT)[None, None, :] * P
                     + np.arange(P)[:, None, None]).reshape(P, -1)
    parts["scan"] = np.broadcast_to((np.arange(S) % CH != 0), (P, S))
    s, u = (np.arange(P) % CH)[:, None], np.arange(CH)[None, :]
    for n in (1, 2, 4, 8, 16, 32):
        parts[f"lev{n}"] = (s // (2 * n) == u // (2 * n)) & (u % (2 * n) >= n) & (s % (2 * n) < n)
    parts["lev1t"] = (s // 2 == u // 2) & (s % 2 == 1) & (u % 2 == 0)
    parts["eye64"] = (s == u)
    parts["strict"] = (s < u)
    parts["incl"] = (s <= u)
    parts["blk"] = (p // CH == t // CH)
    parts["blkmean"] = (p // CH == t // CH) / CH
    k, h = np.arange(KT)[None, :, None], np.arange(HEADS)[None, None, :]
    parts["sel"] = (2 * k + np.arange(P)[:, None, None] // CH == h).reshape(P, -1)
    f = np.arange(P)[None, None, :]
    selt = (2 * np.arange(KT)[None, :, None] + f // CH == np.arange(P)[:, None, None])
    parts["selt"] = selt.reshape(P, -1)
    where, at = {}, 0
    for name, a in parts.items():
        where[name] = (at, at + a.shape[1])
        at += a.shape[1]
    return np.concatenate([np.asarray(a, np.float32) for a in parts.values()], axis=1), where


def setup(nc, g, ins):
    f = g.view
    with nc.sbuf_tensor("rows", [P, P], FP32) as rows, nc.Block() as block:
        singles = []
        for at, name, index in ((V_MIX0, "mix_norm", 0), (V_MIX1, "mix_norm", 1)):
            singles.append((rows[at:at + 8, :], ins[name][index].rearrange("(k p) -> k p", p=P)))
        singles.append((rows[V_MU:V_MU + 48, :], ins["rwkv_mix"][0].rearrange("j (k p) -> (j k) p", p=P)))
        for at, name in ((V_W0, "rwkv_decay_w0"), (V_A0, "rwkv_iclr_a0"), (V_KK, "rwkv_k_k"), (V_KA, "rwkv_k_a"),
                         (V_RK, "rwkv_r_k"), (V_LNW, "rwkv_ln_w"), (V_LNB, "rwkv_ln_b")):
            singles.append((rows[at:at + 8, :], ins[name][0].rearrange("(k p) -> k p", p=P)))
        for at, src, n in ((V_DQ, ins["diff_q_norm"], 32), (V_DK, ins["diff_k_norm"], 32),
                           (V_NQ, ins["nsa_q_norm"], 64), (V_NK0, ins["nsa_k_norm"][:, 0], 64),
                           (V_NK1, ins["nsa_k_norm"][:, 1], 64), (V_NK2, ins["nsa_k_norm"][:, 2], 64),
                           (V_SUB, ins["diff_subln"], 64)):
            singles.append((rows[at:at + 1, :].rearrange("p (r n) -> p r n", n=n), src.unsqueeze(1).to_broadcast([1, P // n, n])))

        @block.sync
        def _(sp):
            sp.dma_start(g.const[:], ins["const"]).then_inc(g.sig["const_in"], 16)
            for dst, src in singles[::2]:
                sp.dma_start(dst, src).then_inc(g.sig["vec_in"], 16)

        @block.scalar
        def _(act):
            act.dma_start(g.x[:], ins["x"][0].rearrange("(t p) d -> p t d", p=P)).then_inc(g.x_in, 16)
            for dst, src in singles[1::2]:
                act.dma_start(dst, src).then_inc(g.sig["vec_in"], 16)
            act.wait_ge(g.sig["vec_t"], 1)
            nc.scalar.activation(g.vec[:], g.ps[:, 0, 0:V_ROWS], ACT.Copy).then_inc(g.sig["vec_ready"], 1)

        @block.vector
        def _(dve):
            dve.wait_ge(g.sig["const_in"], 16)
            nc.vector.tensor_copy(g.identb[:], f("ident")).then_inc(g.sig["const_b"], 1)
            nc.vector.tensor_copy(g.negb[:], f("neg")).then_inc(g.sig["const_b"], 1)
            nc.vector.tensor_copy(g.cnegb[:], f("cneg")).then_inc(g.sig["const_b"], 1)

        @block.tensor
        def _(pe):
            pe.wait_ge(g.sig["const_in"], 16)
            pe.wait_ge(g.sig["vec_in"], 16 * len(singles))
            nc.tensor.transpose(g.ps[:, 0, 0:V_ROWS], rows[0:V_ROWS, :], f("ident")[0:V_ROWS, 0:V_ROWS]).then_inc(g.sig["vec_t"], 1)


def normalise(nc, g, xs, x_t, gains, strided, store=(), ready=None, besides=None):
    n = g.norms
    g.norms += 1
    with nc.sbuf_tensor(f"nsq{n}", [P, 2, D], FP32) as sq, nc.sbuf_tensor(f"nst{n}", [P, 3, TT], FP32) as st, \
            nc.Block() as block:
        if besides is not None:
            besides(block)

        @block.scalar
        def _(act):
            if n == 0:
                act.wait_ge(g.x_in, 16)
            for t in (0, 2):
                if t == 2:
                    act.wait_ge(g.n_sum[0], 2 * n + 1)
                nc.scalar.activation(sq[:, 0, :], g.x[:, t, :], ACT.Square,
                                     accum_out=st[:, 0, t:t + 1]).then_inc(g.n_sum[0], 1)
            act.wait_ge(g.n_ms, n + 1)
            nc.scalar.activation(st[:, 2, :], st[:, 1, :], ACT.Sqrt).then_inc(g.n_rms, 1)
            if store:
                act.wait_ge(g.n_xs, TT * (n + 1))
            for k in range(0, KT, 2):
                if ready and k == 0:
                    act.wait_ge(*ready)
                act.wait_ge(g.n_tr, KT * n + k + 1)
                nc.scalar.activation(x_t[:, k, :], g.ps[:, k, :], ACT.Copy,
                                     scale=gains[:, k:k + 1]).then_inc(g.n_ev, 1)
            for dst in store:
                act.dma_start(dst.rearrange("(t p) d -> p t d", p=P), xs[:]).then_inc(g.sig["xs_out"], 16)

        @block.vector
        def _(dve):
            if n == 0:
                dve.wait_ge(g.x_in, 16)
            for t in (1, 3):
                if t == 3:
                    dve.wait_ge(g.n_sum[1], 2 * n + 1)
                nc.vector.scalar_tensor_tensor(sq[:, 1, :], g.x[:, t, :], 1.0, g.x[:, t, :], ALU.mult, ALU.mult,
                                               accum_out=st[:, 0, t:t + 1]).then_inc(g.n_sum[1], 1)
            for both in range(2):
                dve.wait_ge(g.n_sum[both], 2 * n + 2)
            nc.vector.tensor_scalar(st[:, 1, :], st[:, 0, :], 1.0 / D, EPS, ALU.mult, ALU.add).then_inc(g.n_ms, 1)
            dve.wait_ge(g.n_rms, n + 1)
            nc.vector.reciprocal(st[:, 0, :], st[:, 2, :]).then_inc(g.n_rs, 1)
            dve.wait_ge(g.n_rs, n + 1)
            for t in range(TT):
                nc.vector.tensor_scalar(xs[:, t, :], g.x[:, t, :], st[:, 0, t:t + 1], None, ALU.mult).then_inc(g.n_xs, 1)
            if ready:
                dve.wait_ge(*ready)
            for k in range(1, KT, 2):
                dve.wait_ge(g.n_tr, KT * n + k + 1)
                nc.vector.tensor_scalar(x_t[:, k, :], g.ps[:, k, :], gains[:, k:k + 1], None, ALU.mult).then_inc(g.n_ev, 1)

        @block.tensor
        def _(pe):
            for t in range(TT):
                pe.wait_ge(g.n_xs, TT * n + t + 1)
                for k in range(KT):
                    src = xs[:, t, k:D:KT] if strided else xs[:, t, k * P:(k + 1) * P]
                    last = nc.tensor.transpose(g.ps[:, k, t * P:(t + 1) * P], src, g.view("ident"))
                    if t == TT - 1:
                        last.then_inc(g.n_tr, 1)


def load_in(sp, g, w, wt, b, c):
    sp.dma_start(wt[:, b], w.rearrange("(k p) (c n) -> c p k n", p=P, n=IN_CHUNK)[c]).then_inc(g.sig["win_in"][b], 16)


def project_in(nc, g, w, wt, x_t, h):
    with nc.Block() as block:

        @block.sync
        def _(sp):
            with sp.Fori(1, 4) as i:
                for b in range(2):
                    sp.wait_ge(g.sig["win_done"][b], 4 * i)
                    load_in(sp, g, w, wt, b, 2 * i + b)

        @block.tensor
        def _(pe):
            with pe.Fori(0, 4) as i:
                for b in range(2):
                    pe.wait_ge(g.sig["win_in"][b], 16 * i + 16)
                    for t in range(TT):
                        pe.wait_ge(g.sig["win_free"][b], i * 4 + t + 1)
                        for k in range(KT):
                            last = nc.tensor.matmul(g.ps[:, 4 * b + t, 0:IN_CHUNK], x_t[:, k, t * P:(t + 1) * P],
                                                    wt[:, b, k, :], start=(k == 0), stop=(k == KT - 1))
                        last.then_inc(g.sig["win_done"][b], 1)

        def copies(eng, run, b):
            with eng.Fori(0, 4) as i:
                for t in range(TT):
                    eng.wait_ge(g.sig["win_done"][b], i * 4 + t + 1)
                    run(h[:, t, bass.ds((2 * i + b) * IN_CHUNK, IN_CHUNK)], g.ps[:, 4 * b + t, 0:IN_CHUNK]).then_inc(g.sig["win_free"][b], 1)

        @block.scalar
        def _(act):
            for _ in range(4):
                nc.scalar.nop().then_inc(g.sig["win_free"][0], 1)
            copies(act, lambda o, i: nc.scalar.activation(o, i, ACT.Copy), 0)

        @block.vector
        def _(dve):
            for _ in range(4):
                nc.vector.nop().then_inc(g.sig["win_free"][1], 1)
            copies(dve, nc.vector.tensor_copy, 1)


def head_norms(nc, g, h, ins, kt_sel, kt_win, kc_t, vc, rs, gates, lamv, qg, w_out):
    f = g.view
    with ExitStack() as mem:
        def sb(name, shape, dt=FP32):
            return mem.enter_context(nc.sbuf_tensor(name, shape, dt))

        sq = sb("hn_sq", [P, 2, 2304])
        ss = sb("hn_ss", [P, TT, 52])
        rms = sb("hn_rms", [P, TT, 52])
        kst = sb("hn_k", [P, 2, TT, P])
        gb = sb("hn_gb", [P, 24])
        gz = sb("hn_gz", [P, TT, 24])
        lp = sb("hn_lp", [P, 4, 32])
        lq = sb("hn_lq", [P, 2, 32])
        ls = sb("hn_ls", [P, 4])
        pe_rows = sb("hn_per", [64, P])
        pe_t = sb("hn_pet", [P, 2, 32])
        w1 = sb("hn_w1", [P, 2, 32, 64])
        w2 = sb("hn_w2", [P, 2, 64])
        blk = sb("hn_blk", [P, 2, 2, 32, 16])
        hid = sb("hn_hid", [P, 2, NCMP])
        hu = sb("hn_hu", [P, 2, NCMP])
        kc = sb("hn_kc", [NCMP, 2, 64])
        kq = sb("hn_kq", [NCMP, 2, 64])
        kr = sb("hn_kr", [NCMP, 3, 2])
        pe_src = ins["nsa_cmp_pe"][0].rearrange("v l d -> (v l) d")
        w1_src = ins["nsa_cmp_w1"][0].rearrange("v (l d) o -> v d l o", d=64)
        w2_src = ins["nsa_cmp_w2"][0].rearrange("v d o -> d v o")
        block = mem.enter_context(nc.Block())

        @block.sync
        def _(sp):
            sp.dma_start(gb[:], ins["attn_gate_bias"][0].partition_broadcast(P)).then_inc(g.sig["hn_small"], 16)
            sp.dma_start(lp[:], ins["diff_lambda"][0].partition_broadcast(P)).then_inc(g.sig["hn_small"], 16)
            for grp in range(2):
                sp.dma_start(pe_rows[:, 64 * grp:64 * grp + 64], pe_src).then_inc(g.sig["hn_pe"], 16)
                sp.dma_start(w2[64 * grp:64 * grp + 64], w2_src).then_inc(g.sig["hn_w"], 16)
                for v in range(2):
                    sp.dma_start(w1[64 * grp:64 * grp + 64, v], w1_src[v]).then_inc(g.sig["hn_w"], 16)
            load_out(sp, g, ins["attn_w_out"][0], w_out)

        @block.scalar
        def _(act):
            for t in range(TT):
                if t >= 2:
                    act.wait_ge(g.sig["hn_sum"], 2 * t - 2)
                nc.scalar.activation(sq[:, t % 2, 0:1024], h[:, t, 0:1024], ACT.Square).then_inc(g.sig["hn_sq"], 1)
                nc.scalar.activation(sq[:, t % 2, 1024:2304], h[:, t, NQ0:GT0], ACT.Square).then_inc(g.sig["hn_sq"], 1)
            act.wait_ge(g.sig["hn_ms"], 2)
            nc.scalar.activation(rms[:], ss[:], ACT.Sqrt).then_inc(g.sig["hn_rms"], 1)
            act.wait_ge(g.sig["hn_gz"], 3)
            nc.scalar.activation(gates[:], gz[:], ACT.Exp, scale=-1.0).then_inc(g.sig["hn_exp"], 1)
            nc.scalar.activation(ls[:, 2:4], ls[:, 0:2], ACT.Exp).then_inc(g.sig["hn_exp"], 1)
            act.wait_ge(g.sig["hn_kt"], 2)
            nc.scalar.activation(kt_sel[:], g.ps[:, 0, :], ACT.Copy, scale=g.vec[:, V_NK1:V_NK1 + 1]).then_inc(g.sig["hn_kev"], 1)
            nc.scalar.activation(kt_win[:], g.ps[:, 1, :], ACT.Copy, scale=g.vec[:, V_NK2:V_NK2 + 1]).then_inc(g.sig["hn_kev"], 1)
            for grp in range(2):
                act.wait_ge(g.sig["hn_hid"], grp + 1)
                q = slice(64 * grp, 64 * grp + 64)
                nc.scalar.activation(hid[q], g.ps[q, 5 + grp, 0:2 * NCMP].rearrange("p (v c) -> p v c", v=2),
                                     ACT.Copy).then_inc(g.sig["hn_hs"], 1)
            act.wait_ge(g.sig["hn_gu"], 1)
            nc.scalar.activation(hu[:], hu[:], ACT.Tanh, scale=0.7978845608028654).then_inc(g.sig["hn_th"], 1)
            for grp in range(2):
                act.wait_ge(g.sig["hn_cmp"], grp + 1)
                o = g.ps[0:NCMP, 7 - 3 * grp, 0:128].rearrange("p (v d) -> p v d", v=2)
                nc.scalar.activation(kc[:, grp, :], o[:, 0, :], ACT.Copy).then_inc(g.sig["hn_kc"], 1)
                nc.scalar.activation(vc[:, grp, :], o[:, 1, :], ACT.Copy).then_inc(g.sig["hn_kc"], 1)
            act.wait_ge(g.sig["hn_kms"], 1)
            nc.scalar.activation(kr[:, 1], kr[:, 0], ACT.Sqrt).then_inc(g.sig["hn_krm"], 1)
            act.wait_ge(g.sig["hn_kct"], 1)
            nc.scalar.activation(kc_t[:], g.ps[:, 5, 0:NCMP], ACT.Copy, scale=g.vec[:, V_NK0:V_NK0 + 1]).then_inc(g.sig["hn_kct2"], 1)

        @block.vector
        def _(dve):
            link = Link(dve, g.sig["hn_link"])
            dve.wait_ge(g.sig["hn_pet"], 1)
            link(nc.vector.tensor_copy(pe_t[:], g.ps[:, 4, 0:64].rearrange("p (v l) -> p v l", v=2)))
            for v in range(2):
                dve.wait_ge(g.sig["hn_raw"], v + 1)
                for half in range(2):
                    nc.vector.tensor_tensor(blk[:, v, half], g.ps[:, 2 + v, :].rearrange("p (c l) -> p c l", l=16),
                                            pe_t[:, v, 16 * half:16 * half + 16].unsqueeze(1).to_broadcast([P, 32, 16]),
                                            ALU.add).then_inc(g.sig["hn_blk"], 1)
            for t in range(TT):
                dve.wait_ge(g.sig["hn_sq"], 2 * t + 2)
                nc.vector.tensor_reduce(ss[:, t, 0:32], sq[:, t % 2, 0:1024].rearrange("p (s d) -> p s d", d=32),
                                        AX.X, ALU.add).then_inc(g.sig["hn_sum"], 1)
                nc.vector.tensor_reduce(ss[:, t, 32:52], sq[:, t % 2, 1024:2304].rearrange("p (s d) -> p s d", d=64),
                                        AX.X, ALU.add).then_inc(g.sig["hn_sum"], 1)
            dve.wait_ge(g.sig["hn_sum"], 2 * TT)
            nc.vector.tensor_scalar(ss[:, :, 0:32], ss[:, :, 0:32], 1.0 / 32, EPS, ALU.mult, ALU.add).then_inc(g.sig["hn_ms"], 1)
            nc.vector.tensor_scalar(ss[:, :, 32:52], ss[:, :, 32:52], 1.0 / 64, EPS, ALU.mult, ALU.add).then_inc(g.sig["hn_ms"], 1)
            dve.wait_ge(g.sig["hn_small"], 32)
            nc.vector.tensor_tensor(gz[:], h[:, :, GT0:IN_COLS], gb[:].unsqueeze(1).to_broadcast([P, TT, 24]),
                                    ALU.add).then_inc(g.sig["hn_gz"], 1)
            link(nc.vector.tensor_tensor(lq[:], lp[:, 0:4:2], lp[:, 1:4:2], ALU.mult))
            nc.vector.tensor_reduce(ls[:, 0:2], lq[:], AX.X, ALU.add).then_inc(g.sig["hn_gz"], 1)
            nc.vector.tensor_scalar(qg[:, 0:1], g.vec[:, V_DQ:V_DQ + 1], 32.0 ** -0.5, None, ALU.mult).then_inc(g.sig["hn_gz"], 1)
            link(nc.vector.tensor_scalar(qg[:, 1:2], g.vec[:, V_NQ:V_NQ + 1], 64.0 ** -0.5, None, ALU.mult))
            dve.wait_ge(g.sig["hn_rms"], 1)
            link(nc.vector.reciprocal(rs[:], rms[:]))
            for b in range(2):
                c0 = KV0 + 256 * (b + 1)
                s0 = 32 + (c0 - NQ0) // 64
                for t in range(TT):
                    r = rs[:, t, s0:s0 + 2].unsqueeze(2).to_broadcast([P, 2, 64])
                    nc.vector.tensor_tensor(kst[:, b, t].rearrange("p (g d) -> p g d", g=2),
                                            h[:, t, c0:c0 + P].rearrange("p (g d) -> p g d", g=2), r,
                                            ALU.mult).then_inc(g.sig["hn_kst"], 1)
            dve.wait_ge(g.sig["hn_exp"], 2)
            link(nc.vector.tensor_scalar(gates[:], gates[:], 1.0, None, ALU.add))
            link(nc.vector.reciprocal(gates[:], gates[:]))
            link(nc.vector.memset(lamv[:], 1.0))
            link(nc.vector.tensor_tensor(ls[:, 0:1], ls[:, 3:4], ls[:, 2:3], ALU.subtract))
            for m in (1, 3):
                link(nc.vector.tensor_scalar(lamv[:, m:m + 1], ls[:, 0:1], LAMBDA_INIT, None, ALU.subtract))
            dve.wait_ge(g.sig["hn_hs"], 2)
            link(nc.vector.tensor_tensor(hu[:], hid[:], hid[:], ALU.mult))
            link(nc.vector.tensor_scalar(hu[:], hu[:], 0.044715, 1.0, ALU.mult, ALU.add))
            nc.vector.tensor_tensor(hu[:], hu[:], hid[:], ALU.mult).then_inc(g.sig["hn_gu"], 1)
            dve.wait_ge(g.sig["hn_th"], 1)
            link(nc.vector.tensor_scalar(hu[:], hu[:], 1.0, 0.5, ALU.add, ALU.mult))
            nc.vector.tensor_tensor(hid[:], hu[:], hid[:], ALU.mult).then_inc(g.sig["hn_gel"], 1)
            dve.wait_ge(g.sig["hn_kc"], 4)
            link(nc.vector.tensor_tensor(kq[:], kc[:], kc[:], ALU.mult))
            link(nc.vector.tensor_reduce(kr[:, 2], kq[:], AX.X, ALU.add))
            nc.vector.tensor_scalar(kr[:, 0], kr[:, 2], 1.0 / 64, EPS, ALU.mult, ALU.add).then_inc(g.sig["hn_kms"], 1)
            dve.wait_ge(g.sig["hn_krm"], 1)
            link(nc.vector.reciprocal(kr[:, 2], kr[:, 1]))
            nc.vector.tensor_tensor(kq[:], kc[:], kr[:, 2].unsqueeze(2).to_broadcast([NCMP, 2, 64]), ALU.mult).then_inc(g.sig["hn_kn"], 1)

        @block.tensor
        def _(pe):
            pe.wait_ge(g.sig["hn_pe"], 32)
            nc.tensor.transpose(g.ps[:, 4, 0:64], pe_rows[:], f("ident")[0:64, 0:64]).then_inc(g.sig["hn_pet"], 1)
            for v in range(2):
                for t in range(TT):
                    last = nc.tensor.transpose(g.ps[:, 2 + v, t * P:(t + 1) * P],
                                               h[:, t, KV0 + v * P:KV0 + (v + 1) * P], f("ident"))
                last.then_inc(g.sig["hn_raw"], 1)
            pe.wait_ge(g.sig["hn_w"], 96)
            pe.wait_ge(g.sig["hn_blk"], 4)
            for grp in range(2):
                q = slice(64 * grp, 64 * grp + 64)
                for v in range(2):
                    for l in range(32):
                        src = blk[q, v, 0, 0:NCMP, l] if l < 16 else blk[q, v, 1, 1:NCMP + 1, l - 16]
                        last = nc.tensor.matmul(g.ps[q, 5 + grp, v * NCMP:(v + 1) * NCMP], w1[q, v, l], src,
                                                start=(l == 0), stop=(l == 31))
                last.then_inc(g.sig["hn_hid"], 1)
            for b in range(2):
                for t in range(TT):
                    pe.wait_ge(g.sig["hn_kst"], TT * b + t + 1)
                    last = nc.tensor.transpose(g.ps[:, b, t * P:(t + 1) * P], kst[:, b, t], f("ident"))
                last.then_inc(g.sig["hn_kt"], 1)
            pe.wait_ge(g.sig["hn_gel"], 1)
            for grp in range(2):
                q = slice(64 * grp, 64 * grp + 64)
                for v in range(2):
                    last = nc.tensor.matmul(g.ps[0:NCMP, 7 - 3 * grp, 64 * v:64 * v + 64], hid[q, v], w2[q, v],
                                            start=True, stop=True)
                last.then_inc(g.sig["hn_cmp"], 1)
            pe.wait_ge(g.sig["hn_kn"], 1)
            nc.tensor.transpose(g.ps[:, 5, 0:NCMP], kq[:].rearrange("p g d -> p (g d)"),
                                f("ident")[0:NCMP, 0:NCMP]).then_inc(g.sig["hn_kct"], 1)


def attention(nc, g, tag, sems, h, ocat, rs, qg, units, n_maps, kt_of, v_of, coef_of, stage, store):
    f = g.view
    U = len(units)
    per = n_maps
    sc, mx, ex, tp, pt, pv, stg, qt_t, kq_ev, cm, o_free = sems
    n_links = stage["links"] + 4 * store["links"]
    with ExitStack() as mem:
        def sb(name, shape, dt=FP32):
            return mem.enter_context(nc.sbuf_tensor(tag + name, shape, dt))

        qs = sb("qs", [P, TT, P])
        q_t = sb("qt", [P, S])
        prob = sb("prob", [P, 2, S])
        prt = sb("prt", [P, 2, S])
        nmax = sb("nmax", [P, U])
        sums = sb("sums", [P, U])
        rec = sb("rec", [P, U])
        tmp = sb("tmp", [P, per, 64])
        block = mem.enter_context(nc.Block())

        def keys(u):
            qt, m, br = units[u]
            return NCMP if br == "cmp" else (qt + 1) * P

        def scores_at(u):
            return g.ps[:, (2, 3, 0, 1)[u % 4], :]

        def copy_on_act(u):
            return u % 2 == 0

        def copy_out(eng, run, i, u):
            eng.wait_ge(tp, i * U + u + 1)
            if u >= 2:
                eng.wait_ge(pv, i * U + u - 1)
            rows = slice(0, NCMP) if units[u][2] == "cmp" else slice(0, P)
            cols = P if units[u][2] == "cmp" else keys(u)
            run(prt[rows, u % 2, 0:cols], g.ps[rows, 4 + u % 2, 0:cols]).then_inc(pt[u % 2], 1)

        n_even, n_odd = (U + 1) // 2, U // 2

        @block.tensor
        def _(pe):
            with pe.Fori(0, 4) as i:
                for t in range(TT):
                    pe.wait_ge(stg, i * TT + t + 1)
                    last = nc.tensor.transpose(g.ps[:, 0, t * P:(t + 1) * P], qs[:, t], f("ident"))
                last.then_inc(qt_t, 1)

                def score(u):
                    qt, m, br = units[u]
                    q0, n = 64 * m, 64
                    keys_t = kt_of[br]
                    bank = scores_at(u)
                    if u >= 4:
                        pe.wait_ge(ex, i * U + u - 3)
                    nc.tensor.matmul(bank[:, 0:keys(u)], q_t[q0:q0 + n, qt * P:(qt + 1) * P],
                                     keys_t[q0:q0 + n, 0:keys(u)], start=True, stop=True)
                    if br == "cmp":
                        mask, at = g.cnegb[:, qt * NCMP:(qt + 1) * NCMP], bank[:, 0:NCMP]
                    else:
                        mask, at = g.negb[:], bank[:, qt * P:(qt + 1) * P]
                    nc.tensor.matmul(at, g.identb[:], mask, start=False, stop=True, skip_group_check=True).then_inc(sc, 1)

                def turn(u):
                    if units[u][2] == "cmp":
                        pe.wait_ge(cm, i * store["n_cmp"] + sum(x[2] == "cmp" for x in units[:u]) + 1)
                    else:
                        pe.wait_ge(ex, i * U + u + 1)
                    if u >= 2:
                        pe.wait_ge(pt[u % 2], i * (n_odd if u % 2 else n_even) + u // 2)
                    if units[u][2] == "cmp":
                        last = nc.tensor.transpose(g.ps[0:NCMP, 4 + u % 2, 0:P], prob[:, u % 2, 0:NCMP], f("ident"))
                    else:
                        for b in range(units[u][0] + 1):
                            last = nc.tensor.transpose(g.ps[:, 4 + u % 2, b * P:(b + 1) * P],
                                                       prob[:, u % 2, b * P:(b + 1) * P], f("ident"))
                    last.then_inc(tp, 1)

                def values(u):
                    qt, m, br = units[u]
                    slot = u % per
                    if slot == 0 and qt >= 2:
                        pe.wait_ge(o_free, i * TT + qt - 1)
                    pe.wait_ge(pt[u % 2], i * (n_odd if u % 2 else n_even) + u // 2 + 1)
                    out = g.ps[:, 6 + qt % 2, slot * 64:slot * 64 + 64]
                    if br == "cmp":
                        last = nc.tensor.matmul(out, prt[0:NCMP, u % 2, 0:P], v_of(i, 0, m, br), start=True, stop=True)
                    else:
                        for b in range(qt + 1):
                            last = nc.tensor.matmul(out, prt[:, u % 2, b * P:(b + 1) * P], v_of(i, b, m, br),
                                                    start=(b == 0), stop=(b == qt))
                    last.then_inc(pv, 1)

                pe.wait_ge(kq_ev, i + 1)
                for u in range(3):
                    score(u)
                for u in range(U):
                    if u + 3 < U:
                        score(u + 3)
                    turn(u)
                    if u >= 1:
                        values(u - 1)
                values(U - 1)

        @block.scalar
        def _(act):
            with act.Fori(0, 4) as i:
                act.wait_ge(qt_t, i + 1)
                nc.scalar.activation(q_t[:], g.ps[:, 0, :], ACT.Copy, scale=qg).then_inc(kq_ev, 1)

                def exp(u):
                    act.wait_ge(mx, i * U + u + 1)
                    if u >= 2:
                        act.wait_ge(tp, i * U + u - 1)
                    nc.scalar.activation(prob[:, u % 2, 0:keys(u)], scores_at(u)[:, 0:keys(u)], ACT.Exp,
                                         bias=nmax[:, u:u + 1], accum_out=sums[:, u:u + 1]).then_inc(ex, 1)

                exp(0)
                for u in range(U):
                    if u + 1 < U:
                        exp(u + 1)
                    if copy_on_act(u):
                        copy_out(act, lambda o, x: nc.scalar.activation(o, x, ACT.Copy), i, u)

        @block.vector
        def _(dve):
            def staged(i):
                for op in stage["ops"](i, qs):
                    op().then_inc(stg, 1)

            staged(0)
            with dve.Fori(0, 4) as i:
                link = Link(dve, g.sig["att_link"], g.att_base[0] + i * n_links)

                def top(u):
                    dve.wait_ge(sc, i * U + u + 1)
                    nc.vector.tensor_reduce(nmax[:, u:u + 1], scores_at(u)[:, 0:keys(u)], AX.X, ALU.max,
                                            negate=True).then_inc(mx, 1)

                def combine(qt):
                    dve.wait_ge(pv, i * U + per * (qt + 1))
                    dve.wait_ge(ex, i * U + per * (qt + 1))
                    c = slice(per * qt, per * qt + per)
                    link(nc.vector.tensor_scalar(rec[:, c], sums[:, c], 1e-30, None, ALU.max))
                    link(nc.vector.reciprocal(rec[:, c], rec[:, c]))
                    link(coef_of(i, qt, rec[:, c]))
                    nc.vector.tensor_tensor(tmp[:], g.ps[:, 6 + qt % 2, 0:per * 64].rearrange("p (m d) -> p m d", d=64),
                                            rec[:, c].unsqueeze(2).to_broadcast([P, per, 64]), ALU.mult).then_inc(o_free, 1)
                    dve.wait_ge(o_free, i * TT + qt + 1)
                    for ins in store["ops"](i, qt, tmp):
                        link(ins())

                top(0)
                top(1)
                for u in range(U):
                    if u + 2 < U:
                        top(u + 2)
                    if u == U // 2:
                        staged((i + 1) % 4)
                    if units[u][2] == "cmp":
                        dve.wait_ge(ex, i * U + u + 1)
                        nc.vector.scalar_tensor_tensor(prob[:, u % 2, 0:NCMP], prob[:, u % 2, 0:NCMP], 1.0,
                                                       f("cok")[:, units[u][0] * NCMP:(units[u][0] + 1) * NCMP],
                                                       ALU.mult, ALU.mult, accum_out=sums[:, u:u + 1]).then_inc(cm, 1)
                    if not copy_on_act(u):
                        copy_out(dve, nc.vector.tensor_copy, i, u)
                    if u >= 1 and u % per == 0:
                        combine(u // per - 1)
                combine(TT - 1)
        g.att_base[0] += 4 * n_links


def diff_attention(nc, g, h, ocat, rs, qg, lamv):
    f = g.view
    units = [(qt, m) for qt in range(TT) for m in range(4)]
    U, PAIRS = len(units), len(units) // 2
    sc, mx, ex, tp, pt, pv, stg, qt_t, kq_ev, mixed, o_free = g.da
    n_links = 2 * PAIRS + TT
    with ExitStack() as mem:
        def sb(name, shape, dt=FP32):
            return mem.enter_context(nc.sbuf_tensor("da_" + name, shape, dt))

        qs, ks = sb("qs", [P, TT, P]), sb("ks", [P, TT, P])
        q_t, k_t = sb("qt", [P, S]), sb("kt", [P, S])
        prob = sb("prob", [P, 4, S])
        prt = sb("prt", [P, 2, S])
        nmax, sums = sb("nmax", [P, U]), sb("sums", [P, U])
        inv, ratio = sb("inv", [P, PAIRS]), sb("ratio", [P, PAIRS])
        rec = sb("rec", [P, PAIRS])
        block = mem.enter_context(nc.Block())

        def keys(u):
            return (units[u][0] + 1) * P

        def scores_at(u):
            return g.ps[:, (2, 3, 0, 1)[u % 4], :]

        def copy_out(eng, run, i, p):
            eng.wait_ge(tp, i * PAIRS + p + 1)
            if p >= 2:
                eng.wait_ge(pv, i * PAIRS + p - 1)
            n = keys(2 * p)
            run(prt[:, p % 2, 0:n], g.ps[:, 4 + p % 2, 0:n]).then_inc(pt[p % 2], 1)

        @block.tensor
        def _(pe):
            with pe.Fori(0, 4) as i:
                for dst, src in enumerate((qs, ks)):
                    for t in range(TT):
                        pe.wait_ge(stg, i * 2 * TT + TT * dst + t + 1)
                        last = nc.tensor.transpose(g.ps[:, dst, t * P:(t + 1) * P], src[:, t], f("ident"))
                    last.then_inc(qt_t, 1)

                def score(u):
                    qt, m = units[u]
                    q = slice(32 * m, 32 * m + 32)
                    bank = scores_at(u)
                    if u >= 4:
                        pe.wait_ge(ex, i * U + u - 3)
                    nc.tensor.matmul(bank[:, 0:keys(u)], q_t[q, qt * P:(qt + 1) * P], k_t[q, 0:keys(u)], start=True, stop=True)
                    nc.tensor.matmul(bank[:, qt * P:(qt + 1) * P], g.identb[:], g.negb[:], start=False, stop=True,
                                     skip_group_check=True).then_inc(sc, 1)

                def turn(p):
                    pe.wait_ge(mixed, i * PAIRS + p + 1)
                    if p >= 2:
                        pe.wait_ge(pt[p % 2], i * (PAIRS // 2) + p // 2)
                    for b in range(units[2 * p][0] + 1):
                        last = nc.tensor.transpose(g.ps[:, 4 + p % 2, b * P:(b + 1) * P],
                                                   prob[:, 2 * (p % 2), b * P:(b + 1) * P], f("ident"))
                    last.then_inc(tp, 1)

                def values(p):
                    qt, head = p // 2, p % 2
                    if head == 0 and qt >= 2:
                        pe.wait_ge(o_free, i * TT + qt - 1)
                    pe.wait_ge(pt[p % 2], i * (PAIRS // 2) + p // 2 + 1)
                    for b in range(qt + 1):
                        last = nc.tensor.matmul(g.ps[:, 6 + qt % 2, head * 64:head * 64 + 64], prt[:, p % 2, b * P:(b + 1) * P],
                                                h[:, b, bass.ds(DV0 + i * P + 64 * head, 64)], start=(b == 0), stop=(b == qt))
                    last.then_inc(pv, 1)

                pe.wait_ge(kq_ev, i * 2 + 2)
                score(0)
                score(1)
                for p in range(PAIRS):
                    if p + 1 < PAIRS:
                        score(2 * p + 2)
                        score(2 * p + 3)
                    if p >= 1:
                        values(p - 1)
                    turn(p)
                values(PAIRS - 1)

        @block.scalar
        def _(act):
            with act.Fori(0, 4) as i:
                act.wait_ge(qt_t, i * 2 + 1)
                nc.scalar.activation(q_t[:], g.ps[:, 0, :], ACT.Copy, scale=qg[:, 0:1]).then_inc(kq_ev, 1)
                act.wait_ge(qt_t, i * 2 + 2)
                nc.scalar.activation(k_t[:], g.ps[:, 1, :], ACT.Copy, scale=g.vec[:, V_DK:V_DK + 1]).then_inc(kq_ev, 1)

                def exp(u):
                    act.wait_ge(mx, i * U + u + 1)
                    if u >= 4:
                        act.wait_ge(tp, i * PAIRS + u // 2 - 1)
                    nc.scalar.activation(prob[:, u % 4, 0:keys(u)], scores_at(u)[:, 0:keys(u)], ACT.Exp,
                                         bias=nmax[:, u:u + 1], accum_out=sums[:, u:u + 1]).then_inc(ex, 1)

                exp(0)
                exp(1)
                for p in range(PAIRS):
                    if p + 1 < PAIRS:
                        exp(2 * p + 2)
                        exp(2 * p + 3)
                    if p % 2 == 0:
                        copy_out(act, lambda o, x: nc.scalar.activation(o, x, ACT.Copy), i, p)

        @block.vector
        def _(dve):
            def staged(i):
                for dst, c0, s0 in ((qs, DQ0, 0), (ks, DK0, 16)):
                    for t in range(TT):
                        nc.vector.tensor_tensor(dst[:, t].rearrange("p (m d) -> p m d", d=32),
                                                h[:, t, bass.ds(c0 + i * P, P)].rearrange("p (m d) -> p m d", d=32),
                                                rs[:, t, bass.ds(s0 + i * 4, 4)].unsqueeze(2).to_broadcast([P, 4, 32]),
                                                ALU.mult).then_inc(stg, 1)

            staged(0)
            with dve.Fori(0, 4) as i:
                link = Link(dve, g.sig["att_link"], g.att_base[0] + i * n_links)

                def top(u):
                    dve.wait_ge(sc, i * U + u + 1)
                    nc.vector.tensor_reduce(nmax[:, u:u + 1], scores_at(u)[:, 0:keys(u)], AX.X, ALU.max,
                                            negate=True).then_inc(mx, 1)

                def mix(p):
                    dve.wait_ge(ex, i * U + 2 * p + 2)
                    u, b, n = 2 * p, 2 * (p % 2), keys(2 * p)
                    link(nc.vector.reciprocal(inv[:, p:p + 1], sums[:, u + 1:u + 2]))
                    link(nc.vector.tensor_scalar(ratio[:, p:p + 1], sums[:, u:u + 1], inv[:, p:p + 1], lamv[:, 1:2], ALU.mult, ALU.mult))
                    nc.vector.scalar_tensor_tensor(prob[:, b, 0:n], prob[:, b + 1, 0:n], ratio[:, p:p + 1], prob[:, b, 0:n],
                                                   ALU.mult, ALU.add).then_inc(mixed, 1)

                def store(qt):
                    dve.wait_ge(pv, i * PAIRS + 2 * (qt + 1))
                    link(nc.vector.reciprocal(rec[:, 2 * qt:2 * qt + 2], sums[:, 4 * qt:4 * qt + 4:2]))
                    nc.vector.tensor_tensor(ocat[:, qt, bass.ds(i * P, P)].rearrange("p (m d) -> p m d", d=64),
                                            g.ps[:, 6 + qt % 2, 0:P].rearrange("p (m d) -> p m d", d=64),
                                            rec[:, 2 * qt:2 * qt + 2].unsqueeze(2).to_broadcast([P, 2, 64]), ALU.mult).then_inc(o_free, 1)

                top(0)
                top(1)
                for p in range(PAIRS):
                    mix(p)
                    if p + 1 < PAIRS:
                        top(2 * p + 2)
                        top(2 * p + 3)
                    if p == PAIRS // 2:
                        staged((i + 1) % 4)
                    if p % 2 == 1:
                        copy_out(dve, nc.vector.tensor_copy, i, p)
                    if p >= 2 and p % 2 == 0:
                        store(p // 2 - 1)
                store(TT - 1)
        g.att_base[0] += 4 * n_links


def nsa_attention(nc, g, h, ocat, rs, qg, gates, kt_sel, kt_win, kc_t, vc):
    units = [(qt, grp, br) for qt in range(TT) for grp in range(2) for br in ("cmp", "sel", "win")]

    def stage_ops(i, qs):
        q = h[:, :, NQ0:KV0].rearrange("p t (g j d) -> p t g j d", g=2, j=4)
        r = rs[:, :, 32:40].rearrange("p t (g j) -> p t g j", g=2)
        for t in range(TT):
            yield lambda t=t: nc.vector.tensor_tensor(
                qs[:, t].rearrange("p (g d) -> p g d", g=2), q[:, t, :, bass.ds(i, 1), :].squeeze(2),
                r[:, t, :, bass.ds(i, 1)].to_broadcast([P, 2, 64]), ALU.mult)

    def value(i, b, m, br):
        if br == "cmp":
            return vc[:, m]
        c0 = KV0 + (256 if br == "sel" else 512) + P + 64 * m
        return h[:, b, c0:c0 + 64]

    def coef(i, qt, rec):
        gate = gates[:, qt].rearrange("p (g j b) -> p g j b", g=2, j=4)[:, :, bass.ds(i, 1), :].squeeze(2)
        r = rec.rearrange("p (g b) -> p g b", g=2)
        return nc.vector.tensor_tensor(r, r, gate, ALU.mult)

    def store_ops(i, qt, tmp):
        out = ocat[:, qt, 512:1024].rearrange("p (g j d) -> p g j d", g=2, j=4)[:, :, bass.ds(i, 1), :].squeeze(2)
        br = tmp[:].rearrange("p (g b) d -> p g b d", g=2)
        yield lambda: nc.vector.tensor_tensor(br[:, :, 0], br[:, :, 0], br[:, :, 1], ALU.add)
        yield lambda: nc.vector.tensor_tensor(out, br[:, :, 0], br[:, :, 2], ALU.add)

    attention(nc, g, "na_", g.na, h, ocat, rs, qg[:, 1:2], units, 6, dict(cmp=kc_t, sel=kt_sel, win=kt_win),
              value, coef, dict(ops=stage_ops, links=0), dict(ops=store_ops, links=5, n_cmp=8))


def load_out(sp, g, w, wt):
    w_v = w.rearrange("(k p) (c n) -> c p k n", p=P, n=S)
    for c in range(2):
        sp.dma_start(wt[:, c], w_v[c]).then_inc(g.sig["po_in"][c], 16)


def project_out(nc, g, wt, src, src_t, scales, norm=None):
    f = g.view
    order = [4, 5, 6, 7, 0, 1, 2, 3] if norm else list(range(KT))
    with nc.Block() as block:

        @block.tensor
        def _(pe):
            if src is not None:
                for k in order:
                    if norm and k == 0:
                        pe.wait_ge(*norm[2])
                    for t in range(TT):
                        last = nc.tensor.transpose(g.ps[:, k, t * P:(t + 1) * P], src[:, t, k * P:(k + 1) * P], f("ident"))
                    last.then_inc(g.sig["po_tr"], 1)
                pe.wait_ge(g.sig["po_ev"][0], KT // 2)
                pe.wait_ge(g.sig["po_ev"][1], KT // 2)
            for c in range(2):
                pe.wait_ge(g.sig["po_in"][c], 16)
                for t in range(TT):
                    for k in range(KT):
                        last = nc.tensor.matmul(g.ps[:, TT * c + t, :], src_t[:, k, t * P:(t + 1) * P], wt[:, c, k, :],
                                                start=(k == 0), stop=(k == KT - 1))
                    last.then_inc(g.sig["po_mm"], 1)

        @block.scalar
        def _(act):
            if norm:
                norm[0](act)
            if src is not None:
                for n, k in list(enumerate(order))[0::2]:
                    act.wait_ge(g.sig["po_tr"], n + 1)
                    nc.scalar.activation(src_t[:, k], g.ps[:, k, :], ACT.Copy, scale=scales[k]).then_inc(g.sig["po_ev"][0], 1)

        @block.vector
        def _(dve):
            if norm:
                norm[1](dve)
            if src is not None:
                for n, k in list(enumerate(order))[1::2]:
                    dve.wait_ge(g.sig["po_tr"], n + 1)
                    nc.vector.tensor_scalar(src_t[:, k], g.ps[:, k, :], scales[k], None, ALU.mult).then_inc(g.sig["po_ev"][1], 1)
            for c in range(2):
                for t in range(TT):
                    dve.wait_ge(g.sig["po_mm"], TT * c + t + 1)
                    xv = g.x[:, t, c * S:(c + 1) * S]
                    nc.vector.tensor_tensor(xv, g.ps[:, TT * c + t, :], xv, ALU.add).then_inc(g.sig["po_done"], 1)


def sub_norm(nc, g, ocat, sq, st, rms):

    def on_act(act):
        nc.scalar.activation(sq[:], ocat[:, :, 0:512], ACT.Square).then_inc(g.sig["sn_sq"], 1)
        act.wait_ge(g.sig["sn_ms"], 1)
        nc.scalar.activation(rms[:], st[:, 1], ACT.Sqrt).then_inc(g.sig["sn_rms"], 1)
        nc.scalar.activation(g.subg[:, 0:1], g.vec[:, V_SUB:V_SUB + 1], ACT.Copy, scale=1.0 - LAMBDA_INIT).then_inc(g.sig["sn_rms"], 1)
        act.wait_ge(g.sig["sn_rms"], 2)
        act.wait_ge(g.sig["sn_link"], 1)

    def on_dve(dve):
        link = Link(dve, g.sig["sn_link"])
        link(nc.vector.memset(g.subg[:, 1:2], 1.0))
        dve.wait_ge(g.sig["sn_sq"], 1)
        link(nc.vector.tensor_reduce(st[:, 0], sq[:].rearrange("p t (s d) -> p t s d", d=64), AX.X, ALU.add))
        nc.vector.tensor_scalar(st[:, 1], st[:, 0], 1.0 / 64, EPS, ALU.mult, ALU.add).then_inc(g.sig["sn_ms"], 1)
        dve.wait_ge(g.sig["sn_rms"], 2)
        link(nc.vector.reciprocal(st[:, 0], rms[:]))
        for t in range(TT):
            o = ocat[:, t, 0:512].rearrange("p (s d) -> p s d", d=64)
            link(nc.vector.tensor_tensor(o, o, st[:, 0, t].unsqueeze(2).to_broadcast([P, 8, 64]), ALU.mult))

    return on_act, on_dve, (g.sig["sn_link"], 3 + TT)


def moe(nc, g, L, ins, out=None):
    f = g.view
    pairs = 2 * S
    xs_dram, y_dram, table = g.xs_dram[L], g.y_dram[L], g.table[L]
    with ExitStack() as mem:
        def sb(name, shape, dt=FP32):
            return mem.enter_context(nc.sbuf_tensor(f"m{L}_{name}", shape, dt))

        wg = [sb(f"wg{b}", [P, KT, DE]) for b in range(4)]
        wu = [sb(f"wu{b}", [P, KT, DE]) for b in range(4)]
        wd = [sb(f"wd{b}", [P, 2, D]) for b in range(4)]
        gain = sb("gain", [P, KT])
        idx_all = sb("idx_all", [CAP, NE], I32)
        n_max = sb("n_max", [P, 1], I32)
        gate = sb("gate", [P, 2, TT])
        wg_v = ins["expert_w_gate"][L].rearrange("e (p k) f -> e p k f", k=KT)
        wu_v = ins["expert_w_up"][L].rearrange("e (p k) f -> e p k f", k=KT)
        wd_v = ins["expert_w_down"][L].rearrange("e (j p) d -> e p j d", p=P)

        def load_expert(sp, e, b, sem):
            sp.dma_start(wg[b][:], wg_v[e]).then_inc(sem[b], 16)
            sp.dma_start(wu[b][:], wu_v[e]).then_inc(sem[b], 16)
            sp.dma_start(wd[b][:], wd_v[e]).then_inc(sem[b], 16)

        with ExitStack() as routing:
            def rb(name, shape, dt=FP32):
                return routing.enter_context(nc.sbuf_tensor(f"m{L}_{name}", shape, dt))

            wr, br = rb("wr", [P, KT, NG + NE]), rb("br", [P, NG + NE])
            fill = rb("fill", [P, ROUNDS * NE * CAP // P], I32)

            def first_weights(block):
                @block.sync
                def _(sp):
                    sp.dma_start(gain[:], ins["ffn_norm"][L].rearrange("(p k) -> p k", k=KT)).then_inc(g.sig["gain_in"], 16)
                    sp.dma_start(wr[:, :, 0:NG], ins["router_group_w"][L].rearrange("(p k) e -> p k e", k=KT)).then_inc(g.sig["r_in"], 16)
                    sp.dma_start(wr[:, :, NG:], ins["router_expert_w"][L].rearrange("(p k) e -> p k e", k=KT)).then_inc(g.sig["r_in"], 16)
                    sp.dma_start(br[:, 0:NG], ins["router_group_b"][L].partition_broadcast(P)).then_inc(g.sig["r_in"], 16)
                    sp.dma_start(br[:, NG:], ins["router_expert_b"][L].partition_broadcast(P)).then_inc(g.sig["r_in"], 16)
                    sp.wait_ge(g.sig["r_fill"], 1)
                    sp.dma_start(table.rearrange("(p n) a -> p (n a)", p=P), fill[:]).then_inc(g.sig["r_empty"], 16)
                    for b in range(4):
                        load_expert(sp, b, b, g.sig["w_in"])

                @block.gpsimd
                def _(pool):
                    nc.gpsimd.memset(fill[:], 2 * S).then_inc(g.sig["r_fill"], 1)

            xs, x_t = rb("xs", [P, TT, D]), rb("xt", [P, KT, S])
            normalise(nc, g, xs, x_t, gain[:], True, store=(xs_dram[0:S], xs_dram[S:2 * S]), ready=(g.sig["gain_in"], 16),
                      besides=first_weights)
            route(nc, g, L, wr, br, x_t, gate, n_max, table)
        xg = [sb(f"xg{b}", [CAP, D]) for b in range(4)]
        with nc.Block() as block:
            @block.gpsimd
            def _(pool):
                pool.wait_ge(g.sig["xs_out"], 32)
                pool.dma_start(idx_all[:], table[0:NE * CAP].rearrange("(p e) a -> p (e a)", e=NE)).then_inc(g.idx_in, 16)
                pool.wait_ge(g.idx_in, 16)

            @block.vector
            def _(dve):
                dve.wait_ge(g.sig["xs_out"], 32)
                for b in range(4):
                    nc.vector.memset(xg[b][:], 0.0).then_inc(g.sig["zero"], 1)
                dve.wait_ge(g.sig["zero"], 4)

        ids_g = [sb(f"ids_g{b}", [CAP, 1], I32) for b in range(4)]
        ids_s = [sb(f"ids_s{b}", [CAP, 1], I32) for b in range(4)]
        xg_t = [sb(f"xgt{b}", [P, KT, CAP]) for b in range(2)]
        act_g = [sb(f"ag{b}", [P, 2, CAP]) for b in range(2)]
        hid = [sb(f"hid{b}", [P, 2, CAP]) for b in range(2)]
        ysb = [sb(f"ysb{b}", [CAP, D]) for b in range(4)]
        m = dict(wg=wg, wu=wu, wd=wd, gain=gain, xg=xg, ids_g=ids_g, ids_s=ids_s, xg_t=xg_t, act_g=act_g, hid=hid,
                            ysb=ysb, xs_dram=xs_dram, y_dram=y_dram, table=table, load_expert=load_expert, idx_all=idx_all)
        experts(nc, g, L, None, m)
        experts(nc, g, L, n_max, m)
        combine(nc, g, L, gate, y_dram, out)


def route(nc, g, L, wr, br, x_t, gate, n_max, table):
    f = g.view
    with ExitStack() as mem:
        def sb(name, shape, dt=FP32):
            return mem.enter_context(nc.sbuf_tensor(f"r{L}_{name}", shape, dt))

        lg = sb("lg", [P, TT, NG + NE])
        eg = sb("eg", [P, TT, NG])
        cand4 = sb("cand4", [P, TT, NG])
        one_g = sb("one_g", [P, TT, NG])
        ml = sb("ml", [P, TT, NE])
        cand = sb("cand", [P, TT, NE])
        pick = [sb(f"pick{c}", [P, TT, NE]) for c in range(2)]
        both = sb("both", [P, TT, NE])
        st = sb("st", [P, 12, TT])
        rank = sb("rank", [P, TT, NE])
        slot = sb("slot", [P, 2, TT])
        slot_i = sb("slot_i", [P, 2, TT], I32)
        pair_i = sb("pair_i", [P, 2, TT], I32)
        top = sb("top", [P, 1])
        block = mem.enter_context(nc.Block())

        @block.tensor
        def _(pe):
            pe.wait_ge(g.sig["r_in"], 64)
            for t in range(TT):
                for k in range(KT):
                    last = nc.tensor.matmul(g.ps[:, 0, t * 64:t * 64 + NG + NE], x_t[:, k, t * P:(t + 1) * P], wr[:, k, :],
                                            start=(k == 0), stop=(k == KT - 1))
            last.then_inc(g.sig["r_lg"], 1)
            pe.wait_ge(g.sig["r_both"], 1)
            for t in range(TT):
                for u in range(t + 1):
                    last = nc.tensor.matmul(g.ps[:, 1, t * NE:(t + 1) * NE], f("upper") if u == t else f("ones"), both[:, u],
                                            start=(u == 0), stop=(u == t))
            for u in range(TT):
                last = nc.tensor.matmul(g.ps[:, 2, 0:NE], f("ones"), both[:, u], start=(u == 0), stop=(u == TT - 1))
            last.then_inc(g.sig["r_rank"], 1)

        @block.scalar
        def _(act):
            act.wait_ge(g.sig["r_sub"], 1)
            nc.scalar.activation(eg[:], eg[:], ACT.Exp).then_inc(g.sig["r_exp"], 1)
            act.wait_ge(g.sig["r_sub"], 2)
            nc.scalar.activation(st[:, 5], st[:, 4], ACT.Exp).then_inc(g.sig["r_exp"], 1)

        @block.vector
        def _(dve):
            link = Link(dve, g.sig["r_link"])

            def col(t_, n):
                return t_.unsqueeze(2).to_broadcast([P, TT, n])

            def first_max(src, n, iota, far, c_, onehot, m):
                link(nc.vector.tensor_reduce(m, src, AX.X, ALU.max))
                link(nc.vector.tensor_tensor(c_, src, col(m, n), ALU.is_ge))
                link(nc.vector.scalar_tensor_tensor(c_, c_, -far, f(iota).unsqueeze(1).to_broadcast([P, TT, n]), ALU.mult, ALU.add))
                link(nc.vector.tensor_reduce(st[:, 11], c_, AX.X, ALU.min))
                link(nc.vector.tensor_tensor(onehot, c_, col(st[:, 11], n), ALU.is_equal))

            dve.wait_ge(g.sig["r_in"], 64)
            dve.wait_ge(g.sig["r_lg"], 1)
            link(nc.vector.tensor_tensor(lg[:], g.ps[:, 0, 0:256].rearrange("p (t e) -> p t e", e=64)[:, :, 0:NG + NE],
                                         br[:].unsqueeze(1).to_broadcast([P, TT, NG + NE]), ALU.add))
            first_max(lg[:, :, 0:NG], NG, "iota4", 8.0, cand4[:], one_g[:], st[:, 0])
            nc.vector.tensor_tensor(eg[:], lg[:, :, 0:NG], col(st[:, 0], NG), ALU.subtract).then_inc(g.sig["r_sub"], 1)
            og = one_g[:].unsqueeze(3).to_broadcast([P, TT, NG, EPG])
            ml4, lg4 = (v.rearrange("p t (g e) -> p t g e", g=NG) for v in (ml[:], lg[:, :, NG:]))
            c4 = cand[:].rearrange("p t (g e) -> p t g e", g=NG)
            nc.vector.tensor_tensor(ml4, lg4, og, ALU.mult).then_inc(g.sig["r_ml"], 1)
            link(nc.vector.tensor_scalar(c4, og, -1.0, BIG, ALU.add, ALU.mult))
            dve.wait_ge(g.sig["r_ml"], 1)
            link(nc.vector.tensor_tensor(ml[:], ml[:], cand[:], ALU.add))
            first_max(ml[:], NE, "iota32", 64.0, cand[:], pick[0][:], st[:, 2])
            link(nc.vector.scalar_tensor_tensor(ml[:], pick[0][:], -2.0 * BIG, ml[:], ALU.mult, ALU.add))
            first_max(ml[:], NE, "iota32", 64.0, cand[:], pick[1][:], st[:, 3])
            nc.vector.tensor_tensor(both[:], pick[0][:], pick[1][:], ALU.add).then_inc(g.sig["r_both"], 1)
            nc.vector.tensor_tensor(st[:, 4], st[:, 3], st[:, 2], ALU.subtract).then_inc(g.sig["r_sub"], 1)
            dve.wait_ge(g.sig["r_exp"], 2)
            link(nc.vector.tensor_reduce(st[:, 6], eg[:], AX.X, ALU.add))
            link(nc.vector.tensor_scalar(st[:, 7], st[:, 5], 1.0, None, ALU.add))
            link(nc.vector.tensor_tensor(st[:, 8], st[:, 6], st[:, 7], ALU.mult))
            link(nc.vector.reciprocal(gate[:, 0], st[:, 8]))
            link(nc.vector.tensor_tensor(gate[:, 1], gate[:, 0], st[:, 5], ALU.mult))
            dve.wait_ge(g.sig["r_rank"], 1)
            link(nc.vector.tensor_copy(rank[:], g.ps[:, 1, 0:TT * NE].rearrange("p (t e) -> p t e", t=TT)))
            link(nc.vector.tensor_reduce(top[:], g.ps[:, 2, 0:NE], AX.X, ALU.max))
            link(nc.vector.tensor_copy(n_max[:], top[:]))
            link(nc.vector.scalar_tensor_tensor(rank[:], rank[:], float(NE), f("iota32").unsqueeze(1).to_broadcast([P, TT, NE]),
                                                ALU.mult, ALU.add))
            for c in range(2):
                link(nc.vector.tensor_tensor(cand[:], rank[:], pick[c][:], ALU.mult))
                link(nc.vector.tensor_reduce(slot[:, c], cand[:], AX.X, ALU.add))
            link(nc.vector.tensor_copy(pair_i[:], f("pair").rearrange("p (c t) -> p c t", c=2)))
            nc.vector.tensor_copy(slot_i[:], slot[:]).then_inc(g.sig["r_slot"], 1)

        @block.gpsimd
        def _(pool):
            pool.wait_ge(g.sig["r_empty"], 16)
            pool.wait_ge(g.sig["r_slot"], 1)
            for c in range(2):
                for t in range(TT):
                    pool.indirect_dma_start(out=table, out_offset=bass.IndirectOffsetOnAxis(ap=slot_i[:, c, t:t + 1], axis=0),
                                            in_=pair_i[:, c, t:t + 1], in_offset=None).then_inc(g.r_tab, 16)
            pool.wait_ge(g.r_tab, 16 * 8)


def experts(nc, g, L, n_max, m):
    f = g.view
    wg, wu, wd, gain, xg, ids_g, ids_s, xg_t = m["wg"], m["wu"], m["wd"], m["gain"], m["xg"], m["ids_g"], m["ids_s"], m["xg_t"]
    act_g, hid, ysb, xs_dram, y_dram, table, load_expert, idx_all = (
        m["act_g"], m["hid"], m["ysb"], m["xs_dram"], m["y_dram"], m["table"], m["load_expert"], m["idx_all"])
    more = n_max is not None
    s = g.ex[more]
    PASSES = NE // 4

    def passes(eng, run, r):
        with eng.Fori(0, PASSES) as i:
            run(i + (r - 1) * PASSES if more else i, i)

    def rounds(eng, one_round):
        if not more:
            one_round(0)
        else:
            top = eng.value_load(n_max[0:1, 0:1], min_val=0, max_val=S)
            for r in range(1, ROUNDS):
                with eng.If(top > r * CAP):
                    one_round(r)

    with nc.Block() as block:

        @block.sync
        def _(sp):
            def run(i, e4):
                for b in range(4):
                    sp.wait_ge(s["down"][b], i + (0 if not more else 1))
                    load_expert(sp, 4 * e4 + b, b, s["w"])
            if not more:
                with sp.Fori(1, PASSES) as i:
                    run(i, i)
            else:
                for b in range(4):
                    sp.nop().then_inc(s["down"][b], 1)
                rounds(sp, lambda r: passes(sp, run, r))

        @block.gpsimd
        def _(pool):
            held = Held(pool, s["held"])

            def gather(n, e4, b):
                nc.gpsimd.tensor_copy(ids_g[b][:], idx_all[:, bass.ds(4 * e4 + b, 1)]).then_inc(s["ids"][b], 1)
                pool.wait_ge(s["ids"][b], n + 1)
                held()
                pool.indirect_dma_start(out=xg[b][:], out_offset=None, in_=xs_dram,
                                        in_offset=bass.IndirectOffsetOnAxis(ap=ids_g[b][:, 0:1], axis=0),
                                        bounds_check=2 * S - 1, oob_is_err=False).then_inc(s["rows"][b], 16)

            def ready(i, e4, b, first, last):
                if not first:
                    pool.wait_ge(s["scat"][b], 16 * i)
                nc.gpsimd.tensor_copy(ids_s[b][:], idx_all[:, bass.ds(4 * e4 + b, 1)]).then_inc(s["y_free"][b], 1)
                if not last:
                    pool.wait_ge(s["turn"], 8 * i + 2 * b + 2)
                    gather(i + 1, e4 + 1, b)

            def scatter(i, b):
                pool.wait_ge(s["y_free"][b], i + 1)
                pool.wait_ge(s["y"][b], 2 * i + 2)
                held()
                pool.indirect_dma_start(out=y_dram, out_offset=bass.IndirectOffsetOnAxis(ap=ids_s[b][:, 0:1], axis=0),
                                        in_=ysb[b][:], in_offset=None,
                                        bounds_check=2 * S - 1, oob_is_err=False).then_inc(s["scat"][b], 16)

            def one_pass(i, e4, first=False, last=False):
                ready(i, e4, 0, first, last)
                for b in range(1, 4):
                    ready(i, e4, b, first, last)
                    scatter(i, b - 1)
                scatter(i, 3)

            def one_round(r):
                base = (r - 1) * PASSES if more else 0
                if more:
                    if r > 1:
                        for b in range(4):
                            pool.wait_ge(s["scat"][b], 16 * base)
                    pool.dma_start(idx_all[:], table[r * NE * CAP:(r + 1) * NE * CAP].rearrange("(p e) a -> p (e a)", e=NE))\
                        .then_inc(g.idx_in, 16)
                    pool.wait_ge(g.idx_in, 16 * (r + 1))
                for b in range(4):
                    gather(base, 0, b)
                one_pass(base, 0, first=True)
                with pool.Fori(1, PASSES - 1) as e4:
                    one_pass(e4 + base, e4)
                one_pass(base + PASSES - 1, PASSES - 1, last=True)
                for b in range(4):
                    pool.wait_ge(s["scat"][b], 16 * (base + PASSES))

            rounds(pool, one_round)

        @block.tensor
        def _(pe):
            def turn(i, b):
                pe.wait_ge(s["rows"][b], 16 * i + 16)
                if b >= 2:
                    pe.wait_ge(s["up"], 4 * i + b - 1)
                    pe.wait_ge(s["xt"][b % 2], 4 * i + 2)
                for k in range(KT):
                    last = nc.tensor.transpose(g.ps[:, 2 * (b % 2) + k // 4, (k % 4) * CAP:(k % 4 + 1) * CAP],
                                               xg[b][:, k:D:KT], f("ident")[0:CAP, 0:CAP])
                    if k % 4 == 3:
                        last.then_inc(s["turn"], 1)

            def up(i, b):
                pe.wait_ge(s["w"][b], 48 * i + 48)
                pe.wait_ge(s["xt"][b % 2], 4 * i + 2 * (b // 2) + 2)
                if b >= 2:
                    pe.wait_ge(s["hid"], 4 * i + b - 1)
                bank = g.ps[:, 4 + b % 2, :]
                for n, w in enumerate((wg[b], wu[b])):
                    for j in range(2):
                        for k in range(KT):
                            last = nc.tensor.matmul(bank[:, (2 * n + j) * CAP:(2 * n + j + 1) * CAP], w[:, k, j * P:(j + 1) * P],
                                                    xg_t[b % 2][:, k, :], start=(k == 0), stop=(k == KT - 1))
                last.then_inc(s["up"], 1)

            def down(i, b):
                pe.wait_ge(s["hid"], 4 * i + b + 1)
                for c in range(2):
                    if b >= 1:
                        pe.wait_ge(s["y"][b - 1], 2 * i + 1 + c)
                    for j in range(2):
                        last = nc.tensor.matmul(g.ps[0:CAP, 6 + c, :], hid[b % 2][:, j, :], wd[b][:, j, c * S:(c + 1) * S],
                                                start=(j == 0), stop=(j == 1))
                    if c == 0:
                        last.then_inc(s["half"], 1)
                last.then_inc(s["down"][b], 1)

            def run(i, e4):
                turn(i, 0)
                turn(i, 1)
                up(i, 0)
                for b in range(1, 4):
                    if b + 1 < 4:
                        turn(i, b + 1)
                    up(i, b)
                    down(i, b - 1)
                down(i, 3)

            rounds(pe, lambda r: passes(pe, run, r))

        def xt_out(eng, i, b, half):
            eng.wait_ge(s["turn"], 8 * i + 2 * b + half + 1)
            if b >= 2:
                eng.wait_ge(s["up"], 4 * i + b - 1)
            gn = gain[:, 4 * half:4 * half + 4].unsqueeze(2).to_broadcast([P, 4, CAP])
            nc.vector.tensor_tensor(xg_t[b % 2][:, 4 * half:4 * half + 4, :],
                                    g.ps[:, 2 * (b % 2) + half, 0:4 * CAP].rearrange("p (k n) -> p k n", n=CAP), gn,
                                    ALU.mult).then_inc(s["xt"][b % 2], 1)

        @block.scalar
        def _(act):
            def silu(i, b):
                act.wait_ge(s["up"], 4 * i + b + 1)
                if b >= 2:
                    act.wait_ge(s["hid"], 4 * i + b - 1)
                nc.scalar.activation(act_g[b % 2][:], g.ps[:, 4 + b % 2, 0:2 * CAP].rearrange("p (j n) -> p j n", j=2),
                                     ACT.Silu).then_inc(s["silu"], 1)

            def y_out(i, b):
                act.wait_ge(s["y_free"][b], i + 1)
                act.wait_ge(s["half"], 4 * i + b + 1)
                nc.scalar.activation(ysb[b][:, 0:S], g.ps[0:CAP, 6, :], ACT.Copy).then_inc(s["y"][b], 1)
                act.wait_ge(s["down"][b], i + (2 if more else 1))
                nc.scalar.activation(ysb[b][:, S:D], g.ps[0:CAP, 7, :], ACT.Copy).then_inc(s["y"][b], 1)

            def run(i, e4):
                silu(i, 0)
                for b in range(1, 4):
                    silu(i, b)
                    y_out(i, b - 1)
                y_out(i, 3)

            rounds(act, lambda r: passes(act, run, r))

        @block.vector
        def _(dve):
            def mix(i, b):
                dve.wait_ge(s["silu"], 4 * i + b + 1)
                if b >= 2:
                    dve.wait_ge(s["half"], 4 * i + b - 1)
                    dve.wait_ge(s["down"][b - 2], i + (2 if more else 1))
                nc.vector.tensor_tensor(hid[b % 2][:], act_g[b % 2][:],
                                        g.ps[:, 4 + b % 2, 2 * CAP:4 * CAP].rearrange("p (j n) -> p j n", j=2),
                                        ALU.mult).then_inc(s["hid"], 1)

            def run(i, e4):
                for b in range(2):
                    for half in range(2):
                        xt_out(dve, i, b, half)
                mix(i, 0)
                for b in range(1, 4):
                    if b + 1 < 4:
                        for half in range(2):
                            xt_out(dve, i, b + 1, half)
                    mix(i, b)

            rounds(dve, lambda r: passes(dve, run, r))


def combine(nc, g, L, gate, y_dram, out):
    with nc.sbuf_tensor(f"c{L}_y", [P, 2, TT, D], FP32) as y, nc.Block() as block:

        @block.sync
        def _(sp):
            src = y_dram.rearrange("(c t p) d -> p c t d", p=P, c=2)
            for t in range(TT):
                for c in range(2):
                    sp.dma_start(y[:, c, t], src[:, c, t]).then_inc(g.sig["y_in"][t], 16)
            if out is not None:
                dst = out[0].rearrange("(t p) d -> p t d", p=P)
                for t in range(TT):
                    sp.wait_ge(g.sig["y_add"], 2 * t + 2)
                    sp.dma_start(dst[:, t], g.x[:, t]).then_inc(g.sig["out_done"], 16)
                sp.wait_ge(g.sig["out_done"], 16 * TT)

        @block.vector
        def _(dve):
            for t in range(TT):
                dve.wait_ge(g.sig["y_in"][t], 32)
                for c in range(2):
                    nc.vector.scalar_tensor_tensor(g.x[:, t], y[:, c, t], gate[:, c, t:t + 1], g.x[:, t], ALU.mult,
                                                   ALU.add).then_inc(g.sig["y_add"], 1)
                    dve.wait_ge(g.sig["y_add"], 2 * t + c + 1)


def rwkv_layer(nc, g, ins):
    with signals(nc, "rw_", RWKV_SIGNALS, RWKV_GROUPS) as g.sig, ExitStack() as mem:
        def sb(name, shape, dt=FP32):
            return mem.enter_context(nc.sbuf_tensor("rw_" + name, shape, dt))

        g.c_stage = dict(zip("ABKVR", g.sig["c_staged"]))
        a = Shared()
        a.r, a.k, a.v, a.kk, a.b = (sb(n, [P, KT, S]) for n in ("r", "k", "v", "kk", "b"))
        a.cs = g.x[:].rearrange("p t (h s) -> p (t h) s", s=S)
        bon = sb("bon", [P, 2, S])
        with ExitStack() as proj:
            def pb(name, shape):
                return proj.enter_context(nc.sbuf_tensor("rp_" + name, shape, FP32))

            w = Shared()
            w.big = pb("w", [P, 2, KT, 256])
            w.w1 = {1: pb("w1", [P, KT, 64]), 4: pb("a1", [P, KT, 64]), 5: pb("g1", [P, KT, LORA_G])}
            w.w2 = {1: pb("w2", [64, D]), 4: pb("a2", [64, D])}
            w.g2 = [pb("g2a", [P, D]), pb("g2b", [LORA_G - P, D])]

            def first_weights(block):
                @block.sync
                def _(sp):
                    rwkv_load(sp, g, ins, w)

            x_t = pb("xt", [P, KT, S])
            with nc.sbuf_tensor("rw_xs", [P, TT, D], FP32) as xs:
                normalise(nc, g, xs, x_t, g.vec[:, V_MIX1:V_MIX1 + 8], False, besides=first_weights)
            x0 = pb("x0", [P, KT, S])
            rwkv_project(nc, g, ins, a, x_t, x0, w)
            rwkv_keys(nc, g, a, x0, x_t, bon)
        rwkv_chunks(nc, g, a)
        w_o = sb("wo", [P, 2, KT, S])
        rwkv_finish(nc, g, a, ins["rwkv_w_o"][0], w_o)
        project_out(nc, g, w_o, None, a.r, None)


BIG_CHUNKS = [(j, c) for j in (0, 3, 2) for c in range(4)]
BIG_NAMES = {0: "rwkv_w_r", 3: "rwkv_w_v", 2: "rwkv_w_k"}


def load_chunk(sp, g, ins, w, n):
    j, c = BIG_CHUNKS[n]
    src = ins[BIG_NAMES[j]][0].rearrange("(k p) (c n) -> c p k n", p=P, n=256)[c]
    sp.dma_start(w.big[:, n % 2], src).then_inc(g.sig["wt_in"][n % 2], 16)


def rwkv_load(sp, g, ins, w):
    for j, n1, n2 in ((1, "rwkv_decay_w1", "rwkv_decay_w2"), (4, "rwkv_iclr_a1", "rwkv_iclr_a2")):
        sp.dma_start(w.w1[j][:], ins[n1][0].rearrange("(k p) n -> p k n", p=P)).then_inc(g.sig["lo_in"], 16)
        sp.dma_start(w.w2[j][:], ins[n2][0]).then_inc(g.sig["lo_in"], 16)
    sp.dma_start(w.w1[5][:], ins["rwkv_gate_g1"][0].rearrange("(k p) n -> p k n", p=P)).then_inc(g.sig["lo_in"], 16)
    sp.dma_start(w.g2[0][:], ins["rwkv_gate_g2"][0][0:P]).then_inc(g.sig["lo_in"], 16)
    sp.dma_start(w.g2[1][:], ins["rwkv_gate_g2"][0][P:LORA_G]).then_inc(g.sig["lo_in"], 16)
    sp.dma_start(g.x_dram, g.x[:]).then_inc(g.sig["x_saved"], 16)
    for n in range(2):
        load_chunk(sp, g, ins, w, n)


def rwkv_project(nc, g, ins, a, x_t, x0, w):
    ORDER = [1, 4, 5, 0, 3, 2]
    xj = [x0, a.kk]
    f = g.view
    with ExitStack() as mem:
        def sb(name, shape, dt=FP32):
            return mem.enter_context(nc.sbuf_tensor("rp_" + name, shape, dt))

        wt, w1, w2, g2 = w.big, w.w1, w.w2, w.g2
        omm = sb("omm", [P, 48])
        hid = {1: sb("hw", [64, S]), 4: sb("ha", [64, S])}
        hg = [sb("hga", [P, S]), sb("hgb", [LORA_G - P, S])]
        stage = sb("st", [P, 2, S])
        block = mem.enter_context(nc.Block())
        big = {0: a.r, 3: a.v, 2: a.k}
        chunks = BIG_CHUNKS
        outs = [("h", 1, 0), ("h", 4, 0)] + [("z", 1, k) for k in range(KT)] + [("h", 5, 0), ("h", 5, 1)]
        outs += [("z", 4, k) for k in range(KT)] + [("p", 0, k) for k in range(KT)] + [("z", 5, k) for k in range(KT)]
        outs += [("p", 3, k) for k in range(KT)] + [("p", 2, k) for k in range(KT)]
        at = {o: n for n, o in enumerate(outs)}

        @block.sync
        def _(sp):
            for n in range(2, len(chunks)):
                last = at["p", chunks[n - 2][0], 2 * chunks[n - 2][1] + 1]
                sp.wait_ge(g.sig["pj_mm"], last + 1)
                load_chunk(sp, g, ins, w, n)

        @block.tensor
        def _(pe):
            pe.wait_ge(g.sig["lo_in"], 16 * 7)
            for n, (kind, j, k) in enumerate(outs):
                bank = g.ps[:, n % 8, :]
                if n >= 8:
                    pe.wait_ge(g.sig["pj_ev"], n - 7)
                if kind == "h":
                    src = xj[ORDER.index(j) % 2]
                    pe.wait_ge(g.sig["xj_mix"], KT * (ORDER.index(j) + 1))
                    m0, m1 = (k * P, min((k + 1) * P, w1[j].shape[2]))
                    for d in range(KT):
                        last = nc.tensor.matmul(bank[0:m1 - m0], w1[j][:, d, m0:m1], src[:, d, :], start=(d == 0), stop=(d == KT - 1))
                elif kind == "z" and j != 5:
                    pe.wait_ge(g.sig["pj_ev"], at["h", j, 0] + 1)
                    last = nc.tensor.matmul(bank, w2[j][:, k * P:(k + 1) * P], hid[j][:], start=True, stop=True)
                elif kind == "z":
                    pe.wait_ge(g.sig["pj_ev"], at["h", 5, 1] + 1)
                    for part in range(2):
                        last = nc.tensor.matmul(bank, g2[part][:, k * P:(k + 1) * P], hg[part][:], start=(part == 0), stop=(part == 1))
                else:
                    src = xj[ORDER.index(j) % 2]
                    c = chunks.index((j, k // 2))
                    pe.wait_ge(g.sig["xj_mix"], KT * (ORDER.index(j) + 1))
                    pe.wait_ge(g.sig["wt_in"][c % 2], 16 * (c // 2 + 1))
                    for d in range(KT):
                        last = nc.tensor.matmul(bank, wt[:, c % 2, d, (k % 2) * P:(k % 2 + 1) * P], src[:, d, :],
                                                start=(d == 0), stop=(d == KT - 1))
                last.then_inc(g.sig["pj_mm"], 1)

        def used(n):
            j = ORDER[n]
            return at[("h", j, 1 if j == 5 else 0) if n < 3 else ("p", j, KT - 1)] + 1

        @block.scalar
        def _(act):
            def scaled(n):
                act.wait_ge(g.sig["omm"], 1)
                if n >= 2:
                    act.wait_ge(g.sig["pj_mm"], used(n - 2))
                for k in range(KT):
                    c = 8 * ORDER[n] + k
                    nc.scalar.activation(xj[n % 2][:, k], x_t[:, k], ACT.Copy, scale=omm[:, c:c + 1]).then_inc(g.sig["xj_scaled"], 1)

            scaled(0)
            scaled(1)
            nth = 2
            for n, (kind, j, k) in enumerate(outs):
                if nth < 6 and used(nth - 2) <= n:
                    scaled(nth)
                    nth += 1
                act.wait_ge(g.sig["pj_mm"], n + 1)
                bank = g.ps[:, n % 8, :]
                if kind == "h" and j != 5:
                    ins_ = nc.scalar.activation(hid[j][:], bank[0:64], ACT.Tanh if j == 1 else ACT.Copy)
                elif kind == "h":
                    ins_ = nc.scalar.activation(hg[k][:], bank[0:P if k == 0 else LORA_G - P], ACT.Sigmoid)
                elif kind == "z" and j == 1:
                    ins_ = nc.scalar.activation(a.r[:, k], bank, ACT.Sigmoid, bias=g.vec[:, V_W0 + k:V_W0 + k + 1])
                elif kind == "z" and j == 4:
                    ins_ = nc.scalar.activation(a.b[:, k], bank, ACT.Sigmoid, bias=g.vec[:, V_A0 + k:V_A0 + k + 1])
                elif kind == "z":
                    if k >= 2:
                        act.wait_ge(g.sig["gate_out"][k % 2], 16 * (k // 2))
                    ins_ = nc.scalar.activation(stage[:, k % 2], bank, ACT.Copy)
                else:
                    if j == 0:
                        act.wait_ge(g.sig["scanned"], KT)
                    ins_ = nc.scalar.activation(big[j][:, k], bank, ACT.Copy)
                ins_.then_inc(g.sig["pj_ev"], 1)
                if kind == "z" and j == 5:
                    act.wait_ge(g.sig["pj_ev"], n + 1)
                    act.dma_start(g.gate_dram[k], stage[:, k % 2]).then_inc(g.sig["gate_out"][k % 2], 16)
            act.wait_ge(g.sig["gate_out"][0], 16 * 4)
            act.wait_ge(g.sig["gate_out"][1], 16 * 4)

        @block.vector
        def _(dve):
            nc.vector.tensor_scalar(omm[:], g.vec[:, V_MU:V_MU + 48], -1.0, 1.0, ALU.mult, ALU.add).then_inc(g.sig["omm"], 1)

            def mixed(n):
                for k in range(KT):
                    c = V_MU + 8 * ORDER[n] + k
                    dve.wait_ge(g.sig["xj_scaled"], KT * n + k + 1)
                    to = xj[n % 2][:, k, 1:S]
                    nc.vector.scalar_tensor_tensor(to, x_t[:, k, 0:S - 1], g.vec[:, c:c + 1], to, ALU.mult, ALU.add).then_inc(g.sig["xj_mix"], 1)

            for n in range(3):
                mixed(n)
            dve.wait_ge(g.sig["x_saved"], 16)
            for k in range(KT):
                dve.wait_ge(g.sig["pj_ev"], at["z", 1, k] + 1)
                nc.vector.tensor_tensor_scan(a.cs[:, k], f("scan"), a.r[:, k], 0.0, ALU.mult, ALU.add).then_inc(g.sig["scanned"], 1)
            for n in range(3, 6):
                mixed(n)


def rwkv_keys(nc, g, a, tmp, tmp2, bon):
    f = g.view
    with ExitStack() as mem:
        def sb(name, shape, dt=FP32):
            return mem.enter_context(nc.sbuf_tensor("rk_" + name, shape, dt))

        omka = sb("omka", [P, KT])
        norm = sb("norm", [HEADS, 3, S])
        block = mem.enter_context(nc.Block())

        @block.vector
        def _(dve):
            nc.vector.tensor_scalar(omka[:], g.vec[:, V_KA:V_KA + 8], -1.0, 1.0, ALU.mult, ALU.add).then_inc(g.sig["k_om"], 1)
            for k in range(KT):
                nc.vector.tensor_scalar(a.kk[:, k], a.k[:, k], g.vec[:, V_KK + k:V_KK + k + 1], None, ALU.mult).then_inc(g.sig["k_raw"], 1)
            dve.wait_ge(g.sig["k_norm"], 1)
            nc.vector.tensor_scalar(norm[:, 1], norm[:, 0], 1e-12, None, ALU.max).then_inc(g.sig["k_max"], 1)
            dve.wait_ge(g.sig["k_max"], 1)
            nc.vector.reciprocal(norm[:, 2], norm[:, 1]).then_inc(g.sig["k_inv"], 1)
            for k in range(KT):
                dve.wait_ge(g.sig["k_bc"], k + 1)
                nc.vector.tensor_tensor(a.kk[:, k], a.kk[:, k], g.ps[:, 1 + k % 3, :], ALU.mult).then_inc(g.sig["k_kk"], 1)
                dve.wait_ge(g.sig["k_new"], 2 * k + 2)
                dve.wait_ge(g.sig["k_kk"], k + 1)
                nc.vector.scalar_tensor_tensor(a.b[:, k], a.kk[:, k], -1.0, a.b[:, k], ALU.mult, ALU.mult).then_inc(g.sig["k_b"], 1)
                nc.vector.scalar_tensor_tensor(tmp2[:, k], a.r[:, k], g.vec[:, V_RK + k:V_RK + k + 1], a.k[:, k], ALU.mult,
                                               ALU.mult).then_inc(g.sig["k_rk"], 1)
            for k in range(KT):
                dve.wait_ge(g.sig["k_bon"], k + 1)
                if k >= 2:
                    dve.wait_ge(g.sig["bon_out"][k % 2], 16 * (k // 2))
                nc.vector.tensor_tensor(bon[:, k % 2], a.v[:, k], g.ps[:, 4 + k % 4, :], ALU.mult).then_inc(g.sig["k_bv"], 1)

        @block.gpsimd
        def _(pool):
            pool.wait_ge(g.sig["k_om"], 1)
            pool.wait_ge(g.sig["k_raw"], KT)
            for k in range(KT):
                pool.wait_ge(g.sig["k_sqmm"], 1)
                nc.gpsimd.tensor_scalar(tmp[:, k], a.b[:, k], g.vec[:, V_KA + k:V_KA + k + 1], omka[:, k:k + 1],
                                        ALU.mult, ALU.add).then_inc(g.sig["k_new"], 1)
                pool.wait_ge(g.sig["k_new"], 2 * k + 1)
                nc.gpsimd.tensor_tensor(a.k[:, k], a.k[:, k], tmp[:, k], ALU.mult).then_inc(g.sig["k_new"], 1)

        @block.scalar
        def _(act):
            for k in range(KT):
                act.wait_ge(g.sig["k_raw"], k + 1)
                nc.scalar.activation(tmp[:, k], a.kk[:, k], ACT.Square).then_inc(g.sig["k_sq"], 1)
            act.wait_ge(g.sig["k_sqmm"], 1)
            nc.scalar.activation(norm[:, 0], g.ps[0:HEADS, 0, :], ACT.Sqrt).then_inc(g.sig["k_norm"], 1)

        @block.tensor
        def _(pe):
            for k in range(KT):
                pe.wait_ge(g.sig["k_sq"], k + 1)
                last = nc.tensor.matmul(g.ps[0:HEADS, 0, :], f("sel")[:, k * HEADS:(k + 1) * HEADS], tmp[:, k],
                                        start=(k == 0), stop=(k == KT - 1))
            last.then_inc(g.sig["k_sqmm"], 1)
            pe.wait_ge(g.sig["k_inv"], 1)
            for k in range(KT):
                if k >= 3:
                    pe.wait_ge(g.sig["k_kk"], k - 2)
                nc.tensor.matmul(g.ps[:, 1 + k % 3, :], f("selt")[0:HEADS, k * P:(k + 1) * P], norm[:, 2],
                                 start=True, stop=True).then_inc(g.sig["k_bc"], 1)
            for k in range(KT):
                pe.wait_ge(g.sig["k_rk"], k + 1)
                if k >= 4:
                    pe.wait_ge(g.sig["k_bv"], k - 3)
                nc.tensor.matmul(g.ps[:, 4 + k % 4, :], f("blk"), tmp2[:, k], start=True, stop=True).then_inc(g.sig["k_bon"], 1)

        @block.sync
        def _(sp):
            for k in range(KT):
                sp.wait_ge(g.sig["k_bv"], k + 1)
                sp.dma_start(g.bonus_dram[k], bon[:, k % 2]).then_inc(g.sig["bon_out"][k % 2], 16)


LEVELS = (2, 4, 8, 16, 32)
CHUNK_STEPS = [("Bt", "act"), ("Kt", "act"), ("Vt", "act"), ("MT", "act"), ("M", "dve"), ("NT", "dve"),
               ("RBT", "dve"), ("RKT", "dve")]
for _n in LEVELS:
    CHUNK_STEPS += [(f"Y{_n}", "act")] + ([(f"Z{_n}", "dve")] if _n < 32 else []) + [(f"ZT{_n}", "dve")]
CHUNK_STEPS += [("NV", "act")]
STEP_AT = {name: n for n, (name, _) in enumerate(CHUNK_STEPS)}


def steps_of(who, upto):
    return sum(w == who for _, w in CHUNK_STEPS[:STEP_AT[upto] + 1])


def rwkv_chunks(nc, g, a):
    f = g.view
    N_ACT = sum(w == "act" for _, w in CHUNK_STEPS)
    N_DVE = sum(w == "dve" for _, w in CHUNK_STEPS)
    N = len(CHUNK_STEPS)
    with ExitStack() as mem:
        def sb(name, shape, dt=FP32):
            return mem.enter_context(nc.sbuf_tensor("rc_" + name, shape, dt))

        e_s = sb("e", [P, 2 * KT, CH + 1])
        A, B, K, R = (sb(n, [P, KT, P]) for n in "ABKR")
        tB, tK, tV = (sb("t" + n, [P, 2 * KT, CH]) for n in "BKV")
        MT, T, TT_, F, Y, NT, RBT, RKT, W, U = (sb(n, [P, 2, KT, CH]) for n in
                                                ("MT", "T", "TT", "F", "Y", "NT", "RBT", "RKT", "W", "U"))
        state = sb("S", [P, KT, CH])
        e_end = sb("end", [P, 2 * KT])
        ysb = sb("y", [P, KT, CH])
        V, e_i = (m[:].rearrange("p a k c -> p (a k c)").rearrange("p (k s) -> p k s", s=P) for m in (F, Y))
        NV = MT
        block = mem.enter_context(nc.Block())

        def pair(ap, i):
            return ap[:, :, bass.ds(i * P, P)]

        def following(i):
            return (i + 1) % 4

        def rows(c):
            return slice(CH * c, CH * c + CH)

        def all16(ap):
            return ap[:].rearrange("p a k c -> p (a k) c")

        def first_bank(step, half):
            return 4 * (STEP_AT[step] % 2) + 2 * half

        def two_banks(step, half):
            b = first_bank(step, half)
            return g.ps[:, b:b + 2, 0:4 * CH].rearrange("p a (k c) -> p a k c", c=CH)

        def u_banks(half):
            return g.ps[:, 6 * half:6 * half + 2, 0:4 * CH].rearrange("p a (k c) -> p a k c", c=CH)

        def part(m, half):
            return m[:, :, 4 * half:4 * half + 4, :]

        def after(eng, i, step, half=1):
            who = CHUNK_STEPS[STEP_AT[step]][1]
            sem, n = (g.sig["c_act"], N_ACT) if who == "act" else (g.sig["c_dve"], N_DVE)
            eng.wait_ge(sem, 2 * (i * n + steps_of(who, step)) - 1 + half)

        @block.tensor
        def _(pe):
            pe.wait_ge(g.sig["c_state"], 1)
            held = Held(pe, g.sig["c_held"])

            def begin(i, step, half, *read):
                n = STEP_AT[step]
                wanted = [*read] + ([CHUNK_STEPS[n - 2][0]] if n >= 2 else [])
                for who in ("act", "dve"):
                    its = [w for w in wanted if CHUNK_STEPS[STEP_AT[w]][1] == who]
                    if its:
                        after(pe, i, max(its, key=STEP_AT.get), half)
                held()

            def turned(i, step, src, ready):
                pe.wait_ge(g.c_stage[ready], i + 1)
                for half in range(2):
                    begin(i, step, half)
                    for k in range(4):
                        last = nc.tensor.transpose(g.ps[:, first_bank(step, half), k * P:(k + 1) * P], src[:, 4 * half + k, :], f("ident"))
                    last.then_inc(g.sig["c_mm"], 1)

            def from_features(i, step, lhs, rhs):
                for half in range(2):
                    out = two_banks(step, half)
                    begin(i, step, half)
                    for k in range(4 * half, 4 * half + 4):
                        for par in range(2):
                            for c in range(2):
                                q = rows(par)
                                last = nc.tensor.matmul(out[rows(c), par, k % 4], lhs[q, k, rows(c)], rhs[q, k, rows(c)], start=True, stop=True)
                    last.then_inc(g.sig["c_mm"], 1)

            def from_tokens(i, step, lhs, rhs, *read):
                for half in range(2):
                    out = two_banks(step, half)
                    begin(i, step, half, *read)
                    for turn in (((0, 0), (1, 1)), ((1, 0), (0, 1))):
                        for k in range(4 * half, 4 * half + 4):
                            for c, par in turn:
                                last = nc.tensor.matmul(out[rows(c), par, k % 4], lhs(rows(c), par, k), rhs(rows(c), par, k), start=True, stop=True)
                    last.then_inc(g.sig["c_mm"], 1)

            def of(m):
                return lambda q, par, k: m[q, par, k]

            def tok(m):
                return lambda q, par, k: m[q, 2 * k + par]

            with pe.Fori(0, 4) as i:
                turned(i, "Bt", B, "B")
                turned(i, "Kt", K, "K")
                turned(i, "Vt", V, "V")
                pe.wait_ge(g.c_stage["A"], i + 1)
                from_features(i, "MT", B, A)
                from_features(i, "M", A, B)
                from_features(i, "NT", K, A)
                pe.wait_ge(g.c_stage["R"], i + 1)
                from_features(i, "RBT", B, R)
                from_features(i, "RKT", K, R)
                for n in LEVELS:
                    pe.wait_ge(g.sig["c_f"], 5 * i + LEVELS.index(n) + 1)
                    if n == 2:
                        pe.wait_ge(g.sig["c_t0"], i + 1)
                    half = [] if n == 2 else [f"Z{n // 2}"]
                    from_tokens(i, f"Y{n}", of(F), of(T), *half)
                    half = [] if n == 2 else [f"ZT{n // 2}"]
                    if n < 32:
                        from_tokens(i, f"Z{n}", of(TT_), of(Y), f"Y{n}", *half)
                    from_tokens(i, f"ZT{n}", of(Y), of(TT_), f"Y{n}", *half)
                from_tokens(i, "NV", of(NT), tok(tV), "NT", "Vt")
                after(pe, i, "ZT32")
                after(pe, i, "NV")
                for c in range(2):
                    t = 2 * i + c
                    if c == 1:
                        pe.wait_ge(g.sig["c_st2"], t + 0)
                    held()
                    for half in range(2):
                        for k in range(4):
                            for par in range(2):
                                last = nc.tensor.matmul(u_banks(half)[rows(c), par, k], A[rows(par), 4 * half + k, rows(c)],
                                                        state[rows(par), 4 * half + k], start=True, stop=True)
                        last.then_inc(g.sig["c_u"], 1)
                    if c == 1:
                        pe.wait_ge(g.sig["c_ys2"], 2 * t)
                    held()
                    for k in range(KT):
                        for par in range(2):
                            last = nc.tensor.matmul(g.ps[rows(par), 2 + par, k * CH:(k + 1) * CH], state[rows(par), k],
                                                    R[rows(par), k, rows(c)], start=True, stop=True)
                            if k == KT - 1:
                                last.then_inc(g.sig["c_ys"], 1)
                    for half in range(2):
                        pe.wait_ge(g.sig["c_u2"], 2 * t + half + 1)
                        held()
                        for k in range(4):
                            for par in range(2):
                                last = nc.tensor.matmul(u_banks(half)[rows(c), par, k], TT_[rows(c), par, 4 * half + k],
                                                        W[rows(c), par, 4 * half + k], start=True, stop=True)
                        last.then_inc(g.sig["c_tw"], 1)
                    for k in range(KT):
                        if k % 4 == 0:
                            pe.wait_ge(g.sig["c_uc"], 2 * t + k // 4 + 1)
                            held()
                        o = [g.ps[rows(par), 4, k * CH:(k + 1) * CH] for par in range(2)]
                        for par in range(2):
                            nc.tensor.matmul(o[par], tB[rows(c), 2 * k + par], U[rows(c), par, k], start=True, stop=False)
                        for par in range(2):
                            last = nc.tensor.matmul(o[par], tK[rows(c), 2 * k + par], tV[rows(c), 2 * k + par], start=False, stop=True)
                    last.then_inc(g.sig["c_su"], 1)
                    if c == 1:
                        pe.wait_ge(g.sig["c_y"], t)
                    held()
                    for k in range(KT):
                        o = [g.ps[rows(par), 5, k * CH:(k + 1) * CH] for par in range(2)]
                        for par in range(2):
                            nc.tensor.matmul(o[par], U[rows(c), par, k], RBT[rows(c), par, k], start=True, stop=False)
                        for par in range(2):
                            last = nc.tensor.matmul(o[par], tV[rows(c), 2 * k + par], RKT[rows(c), par, k], start=False, stop=True)
                    last.then_inc(g.sig["c_yu"], 1)
                pe.wait_ge(g.sig["c_y"], 2 * i + 2)
                held()

        @block.scalar
        def _(act):
            def copy(i, step, dst):
                turned = step in ("Bt", "Kt", "Vt")
                for half in range(2):
                    act.wait_ge(g.sig["c_mm"], 2 * (i * N + STEP_AT[step]) + half + 1)
                    src = (g.ps[:, first_bank(step, half), :].rearrange("p (k c) -> p k c", c=CH) if turned
                           else two_banks(step, half))
                    nc.scalar.activation(dst(half), src, ACT.Copy).then_inc(g.sig["c_act"], 1)

            def of(m):
                return lambda half: part(m, half)

            def tok(m):
                return lambda half: m[:, 8 * half:8 * half + 8]

            def stage(i):
                cs = pair(a.cs, i)
                nc.scalar.activation(e_s[:, :, 1:].rearrange("p (k c) s -> p k c s", c=2),
                                     cs.rearrange("p k (c s) -> p k c s", c=2), ACT.Exp, scale=-DECAY).then_inc(g.sig["c_exp"], 1)
                nc.scalar.activation(e_i, cs, ACT.Exp, scale=DECAY).then_inc(g.sig["c_exp"], 1)
                nc.scalar.activation(V, pair(a.v, i), ACT.Copy).then_inc(g.c_stage["V"], 1)

            stage(0)
            with act.Fori(0, 4) as i:
                for step, dst in (("Bt", tok(tB)), ("Kt", tok(tK)), ("Vt", tok(tV)), ("MT", of(MT))):
                    copy(i, step, dst)
                for n in LEVELS:
                    copy(i, f"Y{n}", of(Y))
                copy(i, "NV", of(NV))
                for c in range(2):
                    t = 2 * i + c
                    if c == 1:
                        act.wait_ge(g.sig["c_y"], t)
                    for par in range(2):
                        act.wait_ge(g.sig["c_ys"], 2 * t + par + 1)
                        nc.scalar.activation(ysb[rows(par)], g.ps[rows(par), 2 + par, :].rearrange("p (k c) -> p k c", c=CH),
                                             ACT.Copy).then_inc(g.sig["c_ys2"], 1)
                    for half in range(2):
                        act.wait_ge(g.sig["c_tw"], 2 * t + half + 1)
                        nc.scalar.activation(part(U, half)[rows(c)], u_banks(half)[rows(c)], ACT.Copy).then_inc(g.sig["c_uc"], 1)
                stage(following(i))
                act.wait_ge(g.sig["c_y"], 2 * i + 2)

        @block.gpsimd
        def _(pool):
            nc.gpsimd.memset(state[:], 0.0).then_inc(g.sig["c_zero"], 1)
            nc.gpsimd.memset(e_s[:, :, 0:1], 1.0).then_inc(g.sig["c_zero"], 1)
            pool.wait_ge(g.sig["c_zero"], 2)
            pool.nop().then_inc(g.sig["c_state"], 1)

            def stage(n, i):
                pool.wait_ge(g.sig["c_exp"], 2 * n + 1)
                nc.gpsimd.tensor_tensor(R[:].rearrange("p k (c s) -> p k c s", c=2), pair(a.r, i).rearrange("p k (c s) -> p k c s", c=2),
                                        e_s[:, :, 1:].rearrange("p (k c) s -> p k c s", c=2), ALU.mult).then_inc(g.c_stage["R"], 1)

            stage(0, 0)
            with pool.Fori(0, 4) as i:
                for n in LEVELS:
                    after(pool, i, "MT")
                    if n == 2:
                        after(pool, i, "Vt")
                    else:
                        after(pool, i, f"Y{n // 2}")
                    nc.gpsimd.tensor_tensor(all16(F), all16(MT), f(f"lev{n}").unsqueeze(1).to_broadcast([P, 2 * KT, CH]),
                                            ALU.mult).then_inc(g.sig["c_f"], 1)
                pool.wait_ge(g.sig["c_ys"], 4 * i + 4)
                stage(i + 1, following(i))

        @block.vector
        def _(dve):
            def quad(ap):
                return ap.rearrange("p k (c s) -> p k c s", c=2)

            def stage(n, i):
                before = e_s[:, :, 0:CH].rearrange("p (k c) s -> p k c s", c=2)
                dve.wait_ge(g.sig["c_exp"], 2 * n + 1)
                nc.vector.tensor_tensor(quad(A[:]), quad(pair(a.kk, i)), before, ALU.mult).then_inc(g.c_stage["A"], 1)
                dve.wait_ge(g.sig["c_exp"], 2 * n + 2)
                nc.vector.tensor_tensor(B[:], pair(a.b, i), e_i, ALU.mult).then_inc(g.c_stage["B"], 1)
                nc.vector.tensor_tensor(K[:], pair(a.k, i), e_i, ALU.mult).then_inc(g.c_stage["K"], 1)

            def ends():
                nc.vector.tensor_copy(e_end[:], e_s[:, :, CH]).then_inc(g.sig["c_end"], 1)

            dve.wait_ge(g.sig["c_state"], 1)
            stage(0, 0)
            ends()
            with dve.Fori(0, 4) as i:
                after(dve, i, "MT")
                lev1, eye = (f(n).unsqueeze(1).to_broadcast([P, 2 * KT, CH]) for n in ("lev1", "eye64"))
                nc.vector.tensor_tensor(all16(TT_), all16(MT), lev1, ALU.mult).then_inc(g.sig["c_l"], 1)
                dve.wait_ge(g.sig["c_l"], 3 * i + 1)
                nc.vector.tensor_tensor(all16(TT_), all16(TT_), eye, ALU.add).then_inc(g.sig["c_l"], 1)

                def masked(step, dst, mask):
                    for half in range(2):
                        dve.wait_ge(g.sig["c_mm"], 2 * (i * N + STEP_AT[step]) + half + 1)
                        nc.vector.tensor_tensor(part(dst, half), two_banks(step, half),
                                                f(mask).unsqueeze(1).unsqueeze(1).to_broadcast([P, 2, 4, CH]), ALU.mult).then_inc(g.sig["c_dve"], 1)

                masked("M", T, "lev1t")
                dve.wait_ge(g.sig["c_l"], 3 * i + 2)
                after(dve, i, "M")
                nc.vector.tensor_tensor(all16(T), all16(T), eye, ALU.add).then_inc(g.sig["c_l"], 1)
                dve.wait_ge(g.sig["c_l"], 3 * i + 3)
                nc.vector.nop().then_inc(g.sig["c_t0"], 1)
                masked("NT", NT, "strict")
                masked("RBT", RBT, "incl")
                masked("RKT", RKT, "incl")
                for n in LEVELS:
                    for step, dst in ((f"Z{n}", T), (f"ZT{n}", TT_)):
                        if step not in STEP_AT:
                            continue
                        for half in range(2):
                            dve.wait_ge(g.sig["c_mm"], 2 * (i * N + STEP_AT[step]) + half + 1)
                            nc.vector.tensor_tensor(part(dst, half), two_banks(step, half), part(dst, half),
                                                    ALU.add).then_inc(g.sig["c_dve"], 1)
                after(dve, i, "NV")
                for c in range(2):
                    t = 2 * i + c
                    for half in range(2):
                        dve.wait_ge(g.sig["c_u"], 2 * t + half + 1)
                        nc.vector.tensor_tensor(part(W, half)[rows(c)], u_banks(half)[rows(c)], part(NV, half)[rows(c)],
                                                ALU.add).then_inc(g.sig["c_u2"], 1)
                    if c == 1:
                        stage(i + 1, following(i))
                    dve.wait_ge(g.sig["c_su"], t + 1)
                    nc.vector.tensor_tensor(state[:], g.ps[:, 4, :].rearrange("p (k c) -> p k c", c=CH), state[:], ALU.add).then_inc(g.sig["c_st1"], 1)
                    dve.wait_ge(g.sig["c_st1"], t + 1)
                    dve.wait_ge(g.sig["c_end"], i + 1)
                    end = e_end[:, c:2 * KT:2].unsqueeze(2).to_broadcast([P, KT, CH])
                    nc.vector.tensor_tensor(state[:], state[:], end, ALU.mult).then_inc(g.sig["c_st2"], 1)
                    if c == 1:
                        dve.wait_ge(g.sig["c_st2"], t + 1)
                        ends()
                    dve.wait_ge(g.sig["c_yu"], t + 1)
                    dve.wait_ge(g.sig["c_ys2"], 2 * t + 2)
                    nc.vector.tensor_tensor(a.r[:, :, bass.ds(i * P + c * CH, CH)], g.ps[:, 5, :].rearrange("p (k c) -> p k c", c=CH),
                                            ysb[:], ALU.add).then_inc(g.sig["c_y"], 1)


def rwkv_finish(nc, g, a, w, w_o):
    f = g.view
    with ExitStack() as mem:
        def sb(name, shape, dt=FP32):
            return mem.enter_context(nc.sbuf_tensor("rf_" + name, shape, dt))

        sq = sb("sq", [P, 2, S])
        norm = sb("norm", [HEADS, 3, S])
        block = mem.enter_context(nc.Block())
        y, gate, bonus = a.r, a.k, a.v

        @block.sync
        def _(sp):
            sp.dma_start(gate[:], g.gate_dram.rearrange("k p s -> p k s")).then_inc(g.sig["f_gate"], 16)
            for b in range(2):
                sp.wait_ge(g.sig["bon_out"][b], 64)
            sp.dma_start(bonus[:], g.bonus_dram.rearrange("k p s -> p k s")).then_inc(g.sig["f_bonus"], 16)
            sp.dma_start(g.x[:], g.x_dram).then_inc(g.sig["x_back"], 16)
            load_out(sp, g, w, w_o)
            sp.wait_ge(g.sig["x_back"], 16)

        @block.tensor
        def _(pe):
            for k in range(KT):
                if k >= 3:
                    pe.wait_ge(g.sig["f_c"], k - 2)
                nc.tensor.matmul(g.ps[:, 1 + k % 3, :], f("blkmean"), y[:, k], start=True, stop=True).then_inc(g.sig["f_mean"], 1)
            for k in range(KT):
                pe.wait_ge(g.sig["f_sq"], k + 1)
                last = nc.tensor.matmul(g.ps[0:HEADS, 0, :], f("sel")[:, k * HEADS:(k + 1) * HEADS], sq[:, k % 2],
                                        start=(k == 0), stop=(k == KT - 1))
                last.then_inc(g.sig["f_var"], 1)
            pe.wait_ge(g.sig["f_inv"], 1)
            for k in range(KT):
                if k >= 4:
                    pe.wait_ge(g.sig["f_n"], k - 3)
                nc.tensor.matmul(g.ps[:, 4 + k % 4, :], f("selt")[0:HEADS, k * P:(k + 1) * P], norm[:, 2],
                                 start=True, stop=True).then_inc(g.sig["f_bc"], 1)

        @block.scalar
        def _(act):
            for k in range(KT):
                act.wait_ge(g.sig["f_c"], k + 1)
                if k >= 2:
                    act.wait_ge(g.sig["f_var"], k - 1)
                nc.scalar.activation(sq[:, k % 2], y[:, k], ACT.Square).then_inc(g.sig["f_sq"], 1)
            act.wait_ge(g.sig["f_ms"], 1)
            nc.scalar.activation(norm[:, 1], norm[:, 0], ACT.Sqrt).then_inc(g.sig["f_std"], 1)
            for k in range(KT):
                act.wait_ge(g.sig["f_n"], k + 1)
                nc.scalar.activation(y[:, k], y[:, k], ACT.Identity, bias=g.vec[:, V_LNB + k:V_LNB + k + 1],
                                     scale=g.vec[:, V_LNW + k:V_LNW + k + 1]).then_inc(g.sig["f_ln"], 1)

        @block.vector
        def _(dve):
            for k in range(KT):
                dve.wait_ge(g.sig["f_mean"], k + 1)
                nc.vector.tensor_tensor(y[:, k], y[:, k], g.ps[:, 1 + k % 3, :], ALU.subtract).then_inc(g.sig["f_c"], 1)
            dve.wait_ge(g.sig["f_var"], KT)
            nc.vector.tensor_scalar(norm[:, 0], g.ps[0:HEADS, 0, :], 1.0 / CH, 64e-5, ALU.mult, ALU.add).then_inc(g.sig["f_ms"], 1)
            dve.wait_ge(g.sig["f_std"], 1)
            nc.vector.reciprocal(norm[:, 2], norm[:, 1]).then_inc(g.sig["f_inv"], 1)
            for k in range(KT):
                dve.wait_ge(g.sig["f_bc"], k + 1)
                nc.vector.tensor_tensor(y[:, k], y[:, k], g.ps[:, 4 + k % 4, :], ALU.mult).then_inc(g.sig["f_n"], 1)
            dve.wait_ge(g.sig["f_gate"], 16)
            for k in range(KT):
                dve.wait_ge(g.sig["f_b"], k + 1)
                nc.vector.tensor_tensor(y[:, k], y[:, k], gate[:, k], ALU.mult).then_inc(g.sig["f_y"], 1)

        @block.gpsimd
        def _(pool):
            pool.wait_ge(g.sig["f_bonus"], 16)
            for k in range(KT):
                pool.wait_ge(g.sig["f_ln"], k + 1)
                nc.gpsimd.tensor_tensor(y[:, k], y[:, k], bonus[:, k], ALU.add).then_inc(g.sig["f_b"], 1)


@contextmanager
def signals(nc, tag, names, groups=()):
    made = []

    def new(name):
        made.append(nc.alloc_semaphore(name=tag + name))
        return made[-1]

    yield {**{name: new(name) for name in names}, **{name: [new(f"{name}{b}") for b in range(n)] for name, n in groups}}
    with nc.Block() as block:
        @block.gpsimd
        def _(pool):
            for s in made:
                pool.sem_clear(s)
    for s in made:
        nc.release_semaphore(s)


ATTENTION_SIGNALS = (
    "const_in", "vec_in", "vec_t", "vec_ready", "const_b",
    "hn_small", "hn_pe", "hn_w", "hn_sum", "hn_sq", "hn_ms", "hn_rms", "hn_gz", "hn_exp",
    "hn_kt", "hn_kev", "hn_hid", "hn_hs", "hn_gu", "hn_th", "hn_cmp", "hn_kc", "hn_kms", "hn_krm",
    "hn_kct", "hn_kct2", "hn_link", "hn_kst", "hn_pet", "hn_raw", "hn_blk", "hn_gel", "hn_kn",
    "att_link", "sn_sq", "sn_ms", "sn_rms", "sn_link", "po_tr", "po_mm", "po_done")
MOE_SIGNALS = ("gain_in", "r_in", "r_both", "r_sub", "r_exp", "r_lg", "r_rank", "r_fill", "r_empty", "r_ml", "zero", "r_slot",
               "r_link", "xs_out", "y_add", "out_done")
RWKV_SIGNALS = (
    "po_tr", "po_mm", "po_done", "x_saved", "lo_in", "pj_mm", "pj_ev", "xj_mix", "xj_scaled", "omm", "scanned",
    "k_om", "k_raw", "k_norm", "k_max", "k_inv", "k_bc", "k_kk", "k_new", "k_b", "k_rk", "k_bon", "k_bv", "k_sqmm", "k_sq",
    "c_mm", "c_act", "c_dve", "c_state", "c_zero", "c_exp", "c_f", "c_t0", "c_l", "c_u", "c_u2", "c_tw", "c_uc", "c_end", "c_ys", "c_ys2", "c_su",
    "c_yu", "c_y", "c_st1", "c_st2", "c_held", "f_gate", "f_bonus", "x_back", "f_c", "f_mean", "f_sq", "f_var", "f_inv", "f_n",
    "f_bc", "f_ms", "f_std", "f_ln", "f_b", "f_y")
RWKV_GROUPS = (("po_in", 2), ("po_ev", 2), ("wt_in", 2), ("gate_out", 2), ("bon_out", 2), ("c_staged", 5))
EXPERT_SIGNALS = ("held", "up", "hid", "silu", "half", "turn")
EXPERT_GROUPS = (("down", 4), ("ids", 4), ("y", 4), ("y_free", 4), ("xt", 2))


def build(nc, ins, out):
    _, where = const_table()
    g = Shared()
    g.norms = 0
    with ExitStack() as mem:
        def sb(name, shape, dt=FP32):
            return mem.enter_context(nc.sbuf_tensor(name, shape, dt))

        g.const = sb("const", [P, max(b for _, b in where.values())])
        g.view = lambda name: g.const[:, where[name][0]:where[name][1]]
        g.identb, g.negb, g.cnegb = sb("identb", [P, P], BF16), sb("negb", [P, P], BF16), sb("cnegb", [P, TT * NCMP], BF16)
        g.x = sb("x", [P, TT, D])
        g.vec = sb("vec", [P, V_ROWS])
        g.subg = sb("subg", [P, 2])
        g.ps = mem.enter_context(nc.psum_tensor("ps", [P, 8, S], FP32))
        g.xs_dram = [nc.dram_tensor(f"xs_dram{L}", (2 * S, D), FP32, kind="Internal").ap() for L in range(2)]
        g.y_dram = [nc.dram_tensor(f"y_dram{L}", (2 * S, D), FP32, kind="Internal").ap() for L in range(2)]
        g.table = [nc.dram_tensor(f"table{L}", (ROUNDS * NE * CAP, 1), I32, kind="Internal").ap() for L in range(2)]
        g.x_dram = nc.dram_tensor("x_dram", (P, TT, D), FP32, kind="Internal").ap()
        g.gate_dram = nc.dram_tensor("gate_dram", (KT, P, S), FP32, kind="Internal").ap()
        g.bonus_dram = nc.dram_tensor("bonus_dram", (KT, P, S), FP32, kind="Internal").ap()
        g.x_in, g.n_ms, g.n_rms, g.n_rs, g.n_xs, g.n_tr, g.n_ev = (
            mem.enter_context(nc.semaphore(name)) for name in ("x_in", "n_ms", "n_rms", "n_rs", "n_xs", "n_tr", "n_ev"))
        g.n_sum = [mem.enter_context(nc.semaphore(f"n_sum{b}")) for b in range(2)]
        g.table_sems = [[mem.enter_context(nc.semaphore(f"{name}{L}")) for name in ("idx_in", "r_tab")] for L in range(2)]
        g.row_sems, g.scat_sems = (
            [[[mem.enter_context(nc.semaphore(f"{name}{L}{more}{b}")) for b in range(4)] for more in range(2)] for L in range(2)]
            for name in ("rows", "scat"))
        attention_layer(nc, g, ins)
        moe_layer(nc, g, 0, ins)
        rwkv_layer(nc, g, ins)
        moe_layer(nc, g, 1, ins, out)


def attention_layer(nc, g, ins):
    groups = [("win_in", 2), ("win_done", 2), ("win_free", 2), ("po_in", 2), ("po_ev", 2), ("da", 12), ("na", 12)]
    with signals(nc, "att_", ATTENTION_SIGNALS, groups) as g.sig, ExitStack() as layer:
        g.da, g.na = ((*s[:4], (s[4], s[5]), *s[6:]) for s in (g.sig["da"], g.sig["na"]))
        g.att_base = [0]
        def lb(name, shape, dt=FP32):
            return layer.enter_context(nc.sbuf_tensor(name, shape, dt))

        ocat = lb("ocat", [P, TT, D])
        w_out = lb("w_out", [P, 2, KT, S])
        with ExitStack() as att:
            def ab(name, shape, dt=FP32):
                return att.enter_context(nc.sbuf_tensor(name, shape, dt))

            h = ab("h", [P, TT, IN_COLS])
            with nc.sbuf_tensor("w_in", [P, 2, KT, IN_CHUNK], FP32) as wt, nc.sbuf_tensor("xs0", [P, TT, D], FP32) as xs, \
                    nc.sbuf_tensor("xt0", [P, KT, S], FP32) as x_t:
                setup(nc, g, ins)

                def first_columns(block):
                    @block.sync
                    def _(sp):
                        for b in range(2):
                            load_in(sp, g, ins["attn_w_in"][0], wt, b, b)

                normalise(nc, g, xs, x_t, g.vec[:, V_MIX0:V_MIX0 + 8], False, besides=first_columns)
                project_in(nc, g, ins["attn_w_in"][0], wt, x_t, h)
            kt_sel, kt_win, kc_t = ab("kt_sel", [P, S]), ab("kt_win", [P, S]), ab("kc_t", [P, NCMP])
            vc = ab("vc", [NCMP, 2, 64])
            rs, gates, lamv, qg = ab("rs", [P, TT, 52]), ab("gates", [P, TT, 24]), ab("lamv", [P, 4]), ab("qg", [P, 2])
            head_norms(nc, g, h, ins, kt_sel, kt_win, kc_t, vc, rs, gates, lamv, qg, w_out)
            diff_attention(nc, g, h, ocat, rs, qg, lamv)
            nsa_attention(nc, g, h, ocat, rs, qg, gates, kt_sel, kt_win, kc_t, vc)
        norm = sub_norm(nc, g, ocat, lb("sn_sq", [P, TT, 512]), lb("sn_st", [P, 2, TT, 8]), lb("sn_rms", [P, TT, 8]))
        o_t = lb("o_t", [P, KT, S])
        scales = [g.subg[:, 0:1]] * 4 + [g.subg[:, 1:2]] * 4
        project_out(nc, g, w_out, ocat, o_t, scales, norm)


def moe_layer(nc, g, L, ins, out=None):
    g.idx_in, g.r_tab = g.table_sems[L]
    with signals(nc, f"moe{L}_", MOE_SIGNALS, [("w_in", 4), ("y_in", TT)]) as g.sig:
        g.ex = []
        with ExitStack() as experts_signals:
            for more in range(2):
                s = experts_signals.enter_context(signals(nc, f"moe{L}_{more}_", EXPERT_SIGNALS, EXPERT_GROUPS + (() if not more else (("w", 4),))))
                s["rows"], s["scat"] = g.row_sems[L][more], g.scat_sems[L][more]
                if not more:
                    s["w"] = g.sig["w_in"]
                g.ex.append(s)
            moe(nc, g, L, ins, out)


INPUTS = ["x", "mix_norm", "attn_w_in", "attn_gate_bias", "diff_q_norm", "diff_k_norm", "diff_lambda", "diff_subln",
          "nsa_q_norm", "nsa_k_norm", "nsa_cmp_pe", "nsa_cmp_w1", "nsa_cmp_w2", "attn_w_out", "rwkv_mix", "rwkv_w_r",
          "rwkv_w_k", "rwkv_w_v", "rwkv_decay_w0", "rwkv_decay_w1", "rwkv_decay_w2", "rwkv_iclr_a0", "rwkv_iclr_a1",
          "rwkv_iclr_a2", "rwkv_gate_g1", "rwkv_gate_g2", "rwkv_k_k", "rwkv_k_a", "rwkv_r_k", "rwkv_ln_w", "rwkv_ln_b",
          "rwkv_w_o", "ffn_norm", "router_group_w", "router_group_b", "router_expert_w", "router_expert_b",
          "expert_w_gate", "expert_w_up", "expert_w_down"]


def kernel(**inputs):
    import concourse.bacc as bacc
    from concourse.bass_utils import run_bass_kernel_spmd

    nc = bacc.Bacc("TRN2", target_bir_lowering=False, num_devices=1)
    arrays, ins = {}, {}
    for name in INPUTS:
        a = np.ascontiguousarray(inputs[name])
        arrays[f"in_{name}"] = a
        ins[name] = nc.dram_tensor(f"in_{name}", a.shape, FP32, kind="ExternalInput").ap()
    arrays["in_const"] = const_table()[0]
    ins["const"] = nc.dram_tensor("in_const", arrays["in_const"].shape, FP32, kind="ExternalInput").ap()
    out = nc.dram_tensor("out", (1, S, D), FP32, kind="ExternalOutput").ap()
    build(nc, ins, out)
    result = run_bass_kernel_spmd(nc, [arrays], core_ids=[0])
    return result.results[0]["out"]
```
